# Optimizing a Trainium2 kernel written in Bass

```python
import jax
import jax.numpy as jnp
from jax import lax
import numpy as np
import jax, jax.numpy as jnp

D_MODEL = 1024
BATCH = 1
SEQ = 1024
DEPTH = 2

N_MIXERS = 2
N_LRU_LAYERS = (DEPTH + N_MIXERS - 1) // N_MIXERS
N_RWKV_LAYERS = DEPTH // N_MIXERS
D_RNN = 1280
LRU_BLOCKS = 10
LRU_BLOCK = D_RNN // LRU_BLOCKS
CONV_WIDTH = 4
LRU_C = 8.0
LRU_MIN_RAD = 0.9
LRU_MAX_RAD = 0.999
RW_HEAD = 64
RW_HEADS = D_MODEL // RW_HEAD
LORA_DECAY = 64
LORA_AAA = 64
LORA_MV = 32
LORA_GATE = 160
N_SHIFT_MIX = 6
RW_GN_EPS = 64e-5
D_FF = ((8 * D_MODEL // 3 + 255) // 256) * 256
D_PLE = 256
RMS_EPS = 1e-6


def rms_norm(x, g):
    xf = x.astype(jnp.float32)
    y = xf * lax.rsqrt(jnp.mean(xf * xf, axis=-1, keepdims=True) + RMS_EPS)
    return (y * g.astype(jnp.float32)).astype(x.dtype)

def causal_depthwise_conv(x, w, b):
    K = w.shape[0]
    T = x.shape[1]
    xp = jnp.pad(x, ((0, 0), (K - 1, 0), (0, 0)))
    y = b
    for k in range(K):
        y = y + xp[:, k:k + T] * w[k]
    return y

def block_diag_linear(x, w, b):
    B, T, _ = x.shape
    xb = x.reshape(B, T, LRU_BLOCKS, LRU_BLOCK)
    y = jnp.einsum('btnc,ncd->btnd', xb, w.astype(x.dtype))
    return y.reshape(B, T, D_RNN) + b.astype(x.dtype)

def rg_lru(x, wa, ba, wx, bx, lam):
    xf = x.astype(jnp.float32)
    r = jax.nn.sigmoid(block_diag_linear(xf, wa, ba))
    i = jax.nn.sigmoid(block_diag_linear(xf, wx, bx))
    log_a = -LRU_C * r * jax.nn.softplus(-lam.astype(jnp.float32))
    a = jnp.exp(log_a)
    b = jnp.sqrt(-jnp.expm1(2.0 * log_a)) * (i * xf)

    def combine(c1, c2):
        a1, b1 = c1
        a2, b2 = c2
        return a1 * a2, a2 * b1 + b2

    _, h = lax.associative_scan(combine, (a, b), axis=1)
    return h.astype(x.dtype)

def hawk_block(x, w_in, b_in, conv_w, conv_b, wa, ba, wx, bx, lam, w_out, b_out):
    gx = x @ w_in + b_in
    gate_branch, rec_branch = jnp.split(gx, 2, axis=-1)
    gate_branch = jax.nn.gelu(gate_branch)
    rec = causal_depthwise_conv(rec_branch, conv_w, conv_b)
    rec = rg_lru(rec, wa, ba, wx, bx, lam)
    return (rec * gate_branch) @ w_out + b_out

def token_shift(x):
    return jnp.pad(x[:, :-1], ((0, 0), (1, 0), (0, 0)))

def rwkv7_scan(r, w, k, v, a_vec, b_vec):
    B, T, H, N = r.shape
    xs = tuple(jnp.moveaxis(t, 1, 0) for t in (r, w, k, v, a_vec, b_vec))

    def step(S, inp):
        r_t, w_t, k_t, v_t, a_t, b_t = inp
        sa = jnp.einsum('bhvk,bhk->bhv', S, a_t)
        S = S * w_t[:, :, None, :] + sa[..., None] * b_t[:, :, None, :] + v_t[..., None] * k_t[:, :, None, :]
        y = jnp.einsum('bhvk,bhk->bhv', S, r_t)
        return S, y

    S0 = jnp.zeros((B, H, N, N), jnp.float32)
    _, y = lax.scan(step, S0, xs)
    return jnp.moveaxis(y, 0, 1)

def rwkv7_time_mix(x, v_first, mu, w_rkv, w_o, w0, w1, w2, a0, a1, a2, g1, g2,
                   k_k, k_a, r_k, ln_w, ln_b, vres):
    B, T, D = x.shape
    f32 = jnp.float32
    xx = token_shift(x) - x
    xs = x[None] + xx[None] * mu[:, None, None, :]
    xr, xw, xk, xv, xa, xg = xs
    r, k, v = jnp.einsum('nbtd,nde->nbte', jnp.stack([xr, xk, xv]), w_rkv)
    w = -jax.nn.softplus(-(w0 + jnp.tanh(xw @ w1) @ w2)) - 0.5
    a = jax.nn.sigmoid(a0 + (xa @ a1) @ a2)
    g = jax.nn.sigmoid(xg @ g1) @ g2

    def heads(t):
        return t.reshape(B, T, RW_HEADS, RW_HEAD).astype(f32)

    kk = heads(k * k_k)
    kk = kk / jnp.maximum(jnp.sqrt(jnp.sum(kk * kk, axis=-1, keepdims=True)), 1e-12)
    k = k * (1.0 + (a - 1.0) * k_a)
    if vres is None:
        v_first = v
    else:
        v0, v1, v2 = vres
        v = v + (v_first - v) * jax.nn.sigmoid(v0 + (xv @ v1) @ v2)
    decay = jnp.exp(-jnp.exp(w.astype(f32)))
    rh, kh, vh, ah = heads(r), heads(k), heads(v), heads(a)
    y = rwkv7_scan(rh, heads(decay), kh, vh, -kk, kk * ah)
    mean = jnp.mean(y, axis=-1, keepdims=True)
    var = jnp.mean(jnp.square(y - mean), axis=-1, keepdims=True)
    yn = ((y - mean) * lax.rsqrt(var + RW_GN_EPS)).reshape(B, T, D)
    yn = yn * ln_w.astype(f32) + ln_b.astype(f32)
    bonus = jnp.sum(rh * kh * r_k.astype(f32), axis=-1, keepdims=True) * vh
    out = (yn + bonus.reshape(B, T, D)).astype(x.dtype) * g
    return out @ w_o, v_first

def swiglu(x, w_in, w_out):
    gu = x @ w_in
    gate, up = jnp.split(gu, 2, axis=-1)
    return (jax.nn.silu(gate) * up) @ w_out

def first_inputs(seed: int = 0) -> dict:
    key = jax.random.key(seed)
    ks = iter(jax.random.split(key, 64))
    f32 = jnp.float32

    def nrm(shape, scale):
        return scale * jax.random.normal(next(ks), shape, f32)

    def gain(shape):
        return 1.0 + nrm(shape, 0.02)

    D, DR, NL, NR, L = D_MODEL, D_RNN, N_LRU_LAYERS, N_RWKV_LAYERS, DEPTH
    x = nrm((BATCH, SEQ, D), 1.0)
    p = nrm((L, BATCH, SEQ, D_PLE), 1.0)
    u = jax.random.uniform(next(ks), (NL, DR), f32, LRU_MIN_RAD, LRU_MAX_RAD)
    lru_lambda = jnp.log(u) - jnp.log1p(-u)
    rw_w0 = jax.random.uniform(next(ks), (NR, D), f32, -6.0, 1.0)
    rw_mu = jax.random.uniform(next(ks), (NR, N_SHIFT_MIX, D), f32)
    return {
        "x": x,
        "p": p,
        "norm_mix": gain((L, D)),
        "norm_ffn": gain((L, D)),
        "norm_ple": gain((L, D)),
        "norm_final": gain((D,)),
        "lru_w_in": nrm((NL, D, 2 * DR), D ** -0.5),
        "lru_b_in": nrm((NL, 2 * DR), 0.01),
        "lru_conv_w": nrm((NL, CONV_WIDTH, DR), CONV_WIDTH ** -0.5),
        "lru_conv_b": nrm((NL, DR), 0.01),
        "lru_w_gate_a": nrm((NL, LRU_BLOCKS, LRU_BLOCK, LRU_BLOCK), LRU_BLOCK ** -0.5),
        "lru_b_gate_a": nrm((NL, DR), 0.01),
        "lru_w_gate_x": nrm((NL, LRU_BLOCKS, LRU_BLOCK, LRU_BLOCK), LRU_BLOCK ** -0.5),
        "lru_b_gate_x": nrm((NL, DR), 0.01),
        "lru_lambda": lru_lambda,
        "lru_w_out": nrm((NL, DR, D), DR ** -0.5),
        "lru_b_out": nrm((NL, D), 0.01),
        "rw_mu": rw_mu,
        "rw_w_rkv": nrm((NR, 3, D, D), D ** -0.5),
        "rw_w_o": nrm((NR, D, D), D ** -0.5),
        "rw_w0": rw_w0,
        "rw_w1": nrm((NR, D, LORA_DECAY), D ** -0.5),
        "rw_w2": nrm((NR, LORA_DECAY, D), 0.1 * LORA_DECAY ** -0.5),
        "rw_a0": nrm((NR, D), 0.5),
        "rw_a1": nrm((NR, D, LORA_AAA), D ** -0.5),
        "rw_a2": nrm((NR, LORA_AAA, D), 0.1 * LORA_AAA ** -0.5),
        "rw_v0": 1.0 + nrm((NR - 1, D), 0.1),
        "rw_v1": nrm((NR - 1, D, LORA_MV), D ** -0.5),
        "rw_v2": nrm((NR - 1, LORA_MV, D), 0.1 * LORA_MV ** -0.5),
        "rw_g1": nrm((NR, D, LORA_GATE), D ** -0.5),
        "rw_g2": nrm((NR, LORA_GATE, D), LORA_GATE ** -0.5),
        "rw_k_k": 0.85 + nrm((NR, D), 0.05),
        "rw_k_a": 1.0 + nrm((NR, D), 0.05),
        "rw_r_k": nrm((NR, RW_HEADS, RW_HEAD), 0.1),
        "rw_ln_w": gain((NR, D)),
        "rw_ln_b": nrm((NR, D), 0.01),
        "ffn_w_in": nrm((L, D, 2 * D_FF), D ** -0.5),
        "ffn_w_out": nrm((L, D_FF, D), D_FF ** -0.5),
        "ple_w_proj": nrm((L, D_PLE, D), D_PLE ** -0.5),
        "ple_w_gate": nrm((L, D, D), D ** -0.5),
    }

def first_block(x, p, norm_mix, norm_ffn, norm_ple, norm_final,
              lru_w_in, lru_b_in, lru_conv_w, lru_conv_b, lru_w_gate_a, lru_b_gate_a,
              lru_w_gate_x, lru_b_gate_x, lru_lambda, lru_w_out, lru_b_out,
              rw_mu, rw_w_rkv, rw_w_o, rw_w0, rw_w1, rw_w2, rw_a0, rw_a1, rw_a2,
              rw_v0, rw_v1, rw_v2, rw_g1, rw_g2, rw_k_k, rw_k_a, rw_r_k, rw_ln_w, rw_ln_b,
              ffn_w_in, ffn_w_out, ple_w_proj, ple_w_gate):
    h = x
    v_first = None
    for i in range(DEPTH):
        j = i // N_MIXERS
        xn = rms_norm(h, norm_mix[i])
        if i % N_MIXERS == 0:
            mix = hawk_block(xn, lru_w_in[j], lru_b_in[j], lru_conv_w[j], lru_conv_b[j],
                             lru_w_gate_a[j], lru_b_gate_a[j], lru_w_gate_x[j], lru_b_gate_x[j],
                             lru_lambda[j], lru_w_out[j], lru_b_out[j])
        else:
            vres = None if j == 0 else (rw_v0[j - 1], rw_v1[j - 1], rw_v2[j - 1])
            mix, v_first = rwkv7_time_mix(xn, v_first, rw_mu[j], rw_w_rkv[j], rw_w_o[j],
                                          rw_w0[j], rw_w1[j], rw_w2[j], rw_a0[j], rw_a1[j], rw_a2[j],
                                          rw_g1[j], rw_g2[j], rw_k_k[j], rw_k_a[j], rw_r_k[j],
                                          rw_ln_w[j], rw_ln_b[j], vres)
        h = h + mix
        h = h + swiglu(rms_norm(h, norm_ffn[i]), ffn_w_in[i], ffn_w_out[i])
        ple = (p[i] @ ple_w_proj[i]) * jax.nn.sigmoid(rms_norm(h, norm_ple[i]) @ ple_w_gate[i])
        h = h + ple
    return rms_norm(h, norm_final)


_first_inputs = first_inputs


def first_inputs(seed=0):
    import zlib

    import numpy as np

    out = dict(_first_inputs(seed))
    spreads = {}
    factors = {'norm_mix': 2.875,
     'norm_ffn': 2.962,
     'norm_ple': 8.0,
     'norm_final': 2.989,
     'lru_b_in': 2.977,
     'lru_conv_b': 3.116,
     'lru_b_gate_a': 8.0,
     'lru_b_gate_x': 8.0,
     'lru_b_out': 4.655,
     'rw_w1': 8.0,
     'rw_w2': 8.0,
     'rw_a1': 3.66,
     'rw_a2': 3.683,
     'rw_k_k': 3.207,
     'rw_ln_w': 7.211,
     'rw_ln_b': 8.0}
    for name, (base, spread) in spreads.items():
        noise = np.random.default_rng([zlib.crc32(name.encode()), seed]).standard_normal(out[name].shape)
        drawn = base * np.exp(spread * noise) if base else spread * noise
        out[name] = jnp.asarray(drawn.astype(out[name].dtype))
    for name, factor in factors.items():
        out[name] = (out[name] * factor).astype(out[name].dtype)
    return out


_narrow_inputs = first_inputs


def first_inputs(seed=0):

    out = dict(_narrow_inputs(seed))
    wider = {'norm_ple': 12.0, 'norm_final': 3.36, 'rw_ln_w': 5.87, 'rw_ln_b': 10.94}
    for name, times in wider.items():
        mean = out[name].mean()
        out[name] = (mean + times * (out[name] - mean)).astype(out[name].dtype)
    return out


DEPTH_2 = 1

CONV_WIDTH_2 = D_MODEL
CONV_SIZE = 31
SSM_WIDTH = D_MODEL // 2
SSM_GROUP = 16
SSM_GROUPS = SSM_WIDTH // SSM_GROUP
SSM_STATE = 64
DT_MIN = 0.001
DT_MAX = 0.1
LN_EPS = 1e-5
IN_SPLITS = (2 * CONV_WIDTH_2, CONV_WIDTH_2, SSM_WIDTH, SSM_WIDTH, D_MODEL, D_MODEL)
IN_WIDTH = sum(IN_SPLITS)
IN_OFFSETS = [int(v) for v in np.cumsum(IN_SPLITS)[:-1]]


def rms_norm_2(x, g):
    xf = x.astype(jnp.float32)
    y = xf * lax.rsqrt(jnp.mean(xf * xf, axis=-1, keepdims=True) + RMS_EPS)
    return (y * g.astype(jnp.float32)).astype(x.dtype)

def layer_norm(x, g, b):
    xf = x.astype(jnp.float32)
    mu = jnp.mean(xf, axis=-1, keepdims=True)
    xc = xf - mu
    var = jnp.mean(xc * xc, axis=-1, keepdims=True)
    y = xc * lax.rsqrt(var + LN_EPS) * g.astype(jnp.float32) + b.astype(jnp.float32)
    return y.astype(x.dtype)

def causal_depthwise_conv_2(u, w, b):
    c = u.shape[-1]
    y = lax.conv_general_dilated(
        u, w[:, None, :].astype(u.dtype), window_strides=(1,),
        padding=[(CONV_SIZE - 1, 0)],
        dimension_numbers=("NWC", "WIO", "NWC"),
        feature_group_count=c)
    return y + b

def s5_mimo(u, lam_re, lam_im, log_dt, b_re, b_im, c_re, c_im, d):
    bsz, length, _ = u.shape
    f32 = jnp.float32
    uf = u.astype(f32).reshape(bsz, length, SSM_GROUPS, SSM_GROUP)
    dt = jnp.exp(log_dt.astype(f32))[:, None]
    lr = lam_re.astype(f32)
    li = lam_im.astype(f32)
    mag = jnp.exp(lr * dt)
    ar = mag * jnp.cos(li * dt)
    ai = mag * jnp.sin(li * dt)
    den = lr * lr + li * li
    zr = ((ar - 1.0) * lr + ai * li) / den
    zi = (ai * lr - (ar - 1.0) * li) / den
    br = b_re.astype(f32)
    bi = b_im.astype(f32)
    bbar_re = zr[..., None] * br - zi[..., None] * bi
    bbar_im = zr[..., None] * bi + zi[..., None] * br
    bu_re = jnp.einsum("blgh,gph->blgp", uf, bbar_re)
    bu_im = jnp.einsum("blgh,gph->blgp", uf, bbar_im)
    a_re = jnp.broadcast_to(ar, bu_re.shape)
    a_im = jnp.broadcast_to(ai, bu_re.shape)

    def combine(e1, e2):
        a1r, a1i, b1r, b1i = e1
        a2r, a2i, b2r, b2i = e2
        return (a2r * a1r - a2i * a1i,
                a2r * a1i + a2i * a1r,
                a2r * b1r - a2i * b1i + b2r,
                a2r * b1i + a2i * b1r + b2i)

    _, _, s_re, s_im = lax.associative_scan(combine, (a_re, a_im, bu_re, bu_im), axis=1)
    y = (jnp.einsum("blgp,ghp->blgh", s_re, c_re.astype(f32))
         - jnp.einsum("blgp,ghp->blgh", s_im, c_im.astype(f32))
         + d.astype(f32) * uf)
    return y.reshape(bsz, length, SSM_WIDTH).astype(u.dtype)

def hybrid_layer(x, pre_g, w_in, conv_w, conv_b, conv_ln_g, conv_ln_b, w_conv_out,
                 lam_re, lam_im, log_dt, b_re, b_im, c_re, c_im, d,
                 w_glu, b_glu, w_ssm_out, w_out, post_g):
    h = rms_norm_2(x, pre_g)
    proj = jnp.einsum("bld,de->ble", h, w_in)
    conv_in, z_c, u_s, z_s, g_c, g_s = jnp.split(proj, IN_OFFSETS, axis=-1)
    ca, cb = jnp.split(conv_in, 2, axis=-1)
    cu = ca * jax.nn.sigmoid(cb)
    cu = causal_depthwise_conv_2(cu, conv_w, conv_b)
    cu = jax.nn.silu(layer_norm(cu, conv_ln_g, conv_ln_b))
    conv_out = jnp.einsum("blc,cd->bld", cu * jax.nn.silu(z_c), w_conv_out)
    y = jax.nn.gelu(s5_mimo(u_s, lam_re, lam_im, log_dt, b_re, b_im, c_re, c_im, d))
    y = y * jax.nn.sigmoid(jnp.einsum("blc,ce->ble", y, w_glu) + b_glu)
    ssm_out = jnp.einsum("blc,cd->bld", y * jax.nn.silu(z_s), w_ssm_out)
    merged = jax.nn.sigmoid(g_c) * conv_out + jax.nn.sigmoid(g_s) * ssm_out
    out = jnp.einsum("bld,de->ble", merged, w_out)
    return x + rms_norm_2(out, post_g)

def second_inputs(seed: int = 0) -> dict:
    key = jax.random.key(seed)
    ks = jax.random.split(key, 24)
    f32 = jnp.float32
    nrm = lambda k, shape, scale: jax.random.normal(k, shape, f32) * scale
    L, G, P, H = DEPTH_2, SSM_GROUPS, SSM_STATE, SSM_GROUP
    n = jnp.arange(P, dtype=f32)
    log_dt = (jnp.log(DT_MIN) + jax.random.uniform(ks[11], (L, G), f32)
              * (jnp.log(DT_MAX) - jnp.log(DT_MIN)))
    return {
        "x": jax.random.normal(ks[0], (BATCH, SEQ, D_MODEL), f32),
        "pre_norm_gain": 1.0 + nrm(ks[1], (L, D_MODEL), 0.05),
        "w_in": nrm(ks[2], (L, D_MODEL, IN_WIDTH), D_MODEL ** -0.5),
        "conv_w": nrm(ks[3], (L, CONV_SIZE, CONV_WIDTH_2), CONV_SIZE ** -0.5),
        "conv_b": nrm(ks[4], (L, CONV_WIDTH_2), 0.02),
        "conv_ln_gain": 1.0 + nrm(ks[5], (L, CONV_WIDTH_2), 0.05),
        "conv_ln_bias": nrm(ks[6], (L, CONV_WIDTH_2), 0.02),
        "w_conv_out": nrm(ks[7], (L, CONV_WIDTH_2, D_MODEL), CONV_WIDTH_2 ** -0.5),
        "ssm_lambda_re": -0.5 + nrm(ks[8], (L, G, P), 0.01),
        "ssm_lambda_im": jnp.pi * n + nrm(ks[9], (L, G, P), 0.01),
        "ssm_log_dt": log_dt,
        "ssm_b_re": nrm(ks[12], (L, G, P, H), (2.0 * H) ** -0.5),
        "ssm_b_im": nrm(ks[13], (L, G, P, H), (2.0 * H) ** -0.5),
        "ssm_c_re": nrm(ks[14], (L, G, H, P), (2.0 * P) ** -0.5),
        "ssm_c_im": nrm(ks[15], (L, G, H, P), (2.0 * P) ** -0.5),
        "ssm_d": nrm(ks[16], (L, G, H), 1.0),
        "w_ssm_glu": nrm(ks[17], (L, SSM_WIDTH, SSM_WIDTH), SSM_WIDTH ** -0.5),
        "b_ssm_glu": nrm(ks[18], (L, SSM_WIDTH), 0.02),
        "w_ssm_out": nrm(ks[19], (L, SSM_WIDTH, D_MODEL), SSM_WIDTH ** -0.5),
        "w_out": nrm(ks[20], (L, D_MODEL, D_MODEL), D_MODEL ** -0.5),
        "post_norm_gain": 1.0 + nrm(ks[21], (L, D_MODEL), 0.05),
    }

def second_block(x, pre_norm_gain, w_in, conv_w, conv_b, conv_ln_gain, conv_ln_bias, w_conv_out,
              ssm_lambda_re, ssm_lambda_im, ssm_log_dt, ssm_b_re, ssm_b_im, ssm_c_re, ssm_c_im,
              ssm_d, w_ssm_glu, b_ssm_glu, w_ssm_out, w_out, post_norm_gain):
    for l in range(DEPTH_2):
        x = hybrid_layer(x, pre_norm_gain[l], w_in[l], conv_w[l], conv_b[l], conv_ln_gain[l],
                         conv_ln_bias[l], w_conv_out[l], ssm_lambda_re[l], ssm_lambda_im[l],
                         ssm_log_dt[l], ssm_b_re[l], ssm_b_im[l], ssm_c_re[l], ssm_c_im[l],
                         ssm_d[l], w_ssm_glu[l], b_ssm_glu[l], w_ssm_out[l], w_out[l],
                         post_norm_gain[l])
    return x


def setup_inputs(seed=0):
    out = dict(first_inputs(seed))
    for name, value in second_inputs(seed + 1).items():
        if name != "x":
            out[name + "_2"] = value
    return out


def reference(
    x, p, norm_mix, norm_ffn, norm_ple, norm_final, lru_w_in, lru_b_in, lru_conv_w, lru_conv_b,
    lru_w_gate_a, lru_b_gate_a, lru_w_gate_x, lru_b_gate_x, lru_lambda, lru_w_out, lru_b_out,
    rw_mu, rw_w_rkv, rw_w_o, rw_w0, rw_w1, rw_w2, rw_a0, rw_a1, rw_a2, rw_v0, rw_v1, rw_v2,
    rw_g1, rw_g2, rw_k_k, rw_k_a, rw_r_k, rw_ln_w, rw_ln_b, ffn_w_in, ffn_w_out, ple_w_proj,
    ple_w_gate, pre_norm_gain_2, w_in_2, conv_w_2, conv_b_2, conv_ln_gain_2, conv_ln_bias_2,
    w_conv_out_2, ssm_lambda_re_2, ssm_lambda_im_2, ssm_log_dt_2, ssm_b_re_2, ssm_b_im_2,
    ssm_c_re_2, ssm_c_im_2, ssm_d_2, w_ssm_glu_2, b_ssm_glu_2, w_ssm_out_2, w_out_2,
    post_norm_gain_2,
):
    x = first_block(
        x, p, norm_mix, norm_ffn, norm_ple, norm_final, lru_w_in, lru_b_in, lru_conv_w,
        lru_conv_b, lru_w_gate_a, lru_b_gate_a, lru_w_gate_x, lru_b_gate_x, lru_lambda,
        lru_w_out, lru_b_out, rw_mu, rw_w_rkv, rw_w_o, rw_w0, rw_w1, rw_w2, rw_a0, rw_a1, rw_a2,
        rw_v0, rw_v1, rw_v2, rw_g1, rw_g2, rw_k_k, rw_k_a, rw_r_k, rw_ln_w, rw_ln_b, ffn_w_in,
        ffn_w_out, ple_w_proj, ple_w_gate,
    )
    return second_block(
        x, pre_norm_gain_2, w_in_2, conv_w_2, conv_b_2, conv_ln_gain_2, conv_ln_bias_2,
        w_conv_out_2, ssm_lambda_re_2, ssm_lambda_im_2, ssm_log_dt_2, ssm_b_re_2, ssm_b_im_2,
        ssm_c_re_2, ssm_c_im_2, ssm_d_2, w_ssm_glu_2, b_ssm_glu_2, w_ssm_out_2, w_out_2,
        post_norm_gain_2,
    )


_drawn_inputs = setup_inputs


def setup_inputs(seed=0):
    import zlib

    import numpy as np

    out = dict(_drawn_inputs(seed))
    spreads = {}
    factors = {'conv_b_2': 5.302,
     'conv_ln_gain_2': 3.648,
     'conv_ln_bias_2': 8.0,
     'ssm_lambda_re_2': 64.0,
     'ssm_lambda_im_2': 40.872,
     'ssm_log_dt_2': 44.208,
     'ssm_b_re_2': 57.296,
     'ssm_b_im_2': 58.672,
     'ssm_c_re_2': 58.928,
     'ssm_c_im_2': 56.64,
     'b_ssm_glu_2': 61.1,
     'post_norm_gain_2': 3.592}
    for name, (base, spread) in spreads.items():
        noise = np.random.default_rng([zlib.crc32(name.encode()), seed]).standard_normal(out[name].shape)
        drawn = base * np.exp(spread * noise) if base else spread * noise
        out[name] = jnp.asarray(drawn.astype(out[name].dtype))
    for name, factor in factors.items():
        out[name] = (out[name] * factor).astype(out[name].dtype)
    return out
```

```python
import numpy as np
import concourse.bass as bass
from concourse import mybir
from contextlib import ExitStack

P = 128
T = 1024
HALF = 512
D = 1024
DT = D // P
RNN = 1280
RT = RNN // P
FF = 2816
FT = FF // P
FF_GROUPS = (8, 8, 6)
PLE_T = 2
SEMAPHORES = 120
KMAX = 8
RMS_EPS = 1e-6
GN_EPS = 64e-5
LN_EPS = 1e-5
CHUNK = 64
HEAD = 64
TAPS = 31
SSM_G, SSM_P, SSM_H = 32, 64, 16
SC = 8
SN = T // SC

PARAMS = [
    ("norm_mix0", 8), ("norm_mix1", 8), ("norm_ffn0", 8), ("norm_ffn1", 8), ("norm_ple0", 8),
    ("norm_ple1", 8), ("norm_final", 8), ("lru_b_in", 20), ("conv_w", 40), ("conv_b", 10),
    ("b_gate_a", 10), ("b_gate_x", 10), ("lru_lambda", 10), ("lru_b_out", 8),
    ("rw_mu", 48), ("rw_w0", 8), ("rw_a0", 8), ("rw_k_k", 8), ("rw_k_a", 8), ("rw_r_k", 8),
    ("rw_ln_w", 8), ("rw_ln_b", 8),
    ("pre_norm2", 8), ("conv_w2", TAPS * 8), ("conv_b2", 8), ("ln_g2", 8), ("ln_b2", 8),
    ("b_glu2", 4), ("post_norm2", 8), ("ssm_d2", 4),
]
COL, _at = {}, 0
for _name, _n in PARAMS:
    COL[_name] = _at
    _at += _n
NPARAM = _at

CONSTS = ["ident", "mean", "heads", "mask_a", "mask_r"] + [f"level{s}" for s in (1, 2, 4, 8, 16, 32)]
CIX = {n: i for i, n in enumerate(CONSTS)}

class Signal:

    def __init__(self, name, sem, base):
        self.name, self.sem, self.base = name, sem, base

    def at(self, n):
        return self.base + n

    def passed(self, n):
        self.base += n

class Chain:

    def __init__(self, eng, done, start=0):
        self.eng, self.done, self.start, self.n = eng, done, start, 0

    def __call__(self, inst):
        self.n += 1
        inst.then_inc(self.done.sem, 1)
        self.eng.wait_ge(self.done.sem, self.done.at(self.start + self.n))

def build(nc, A, out, stop=None, start=None):
    fp32, r32 = mybir.dt.float32, mybir.dt.float32r
    ALU, ACT = mybir.AluOpType, mybir.ActivationFunctionType
    ds = bass.ds
    ctx = ExitStack()
    with ctx:
        def sb(name, shape, dt=fp32, c=ctx):
            return c.enter_context(nc.sbuf_tensor(name, shape, dt))

        semaphores = [(ctx.enter_context(nc.semaphore(f"signal{n}")), 1) for n in range(SEMAPHORES)]
        signals, made_in = {}, [[]]

        def sig(name):
            if name not in signals:
                signals[name] = Signal(name, *semaphores.pop(0))
                made_in[-1].append(name)
            return signals[name]

        def stage(f):
            def run(*args, **kwargs):
                made_in.append([])
                f(*args, **kwargs)
                for name in made_in.pop():
                    s = signals.pop(name)
                    semaphores.append((s.sem, s.base))
            return run

        with nc.Block() as block:
            @block.sync
            def _(sp):
                for s, _ in semaphores[0::4]:
                    sp.sem_inc(s, 1)

            @block.scalar
            def _(act):
                for s, _ in semaphores[1::4]:
                    act.sem_inc(s, 1)

            @block.gpsimd
            def _(pl):
                for s, _ in semaphores[2::4]:
                    pl.sem_inc(s, 1)

            @block.vector
            def _(dve):
                for s, _ in semaphores[3::4]:
                    dve.sem_inc(s, 1)

        H = sb("H", [P, DT, T])
        par = sb("par", [P, NPARAM])
        const = sb("const", [P, 3, P])
        eps = sb("eps", [P, 4])
        wraw = [sb(f"wraw{s}", [P, KMAX * P]) for s in "AB"]
        whi = [sb(f"whi{s}", [P, KMAX, P], r32) for s in "AB"]
        wlo = [sb(f"wlo{s}", [P, KMAX, P], r32) for s in "AB"]
        ps = [ctx.enter_context(nc.psum_tensor(f"ps{s}", [P, 2, HALF], fp32)) for s in "ABCD"]
        flat = [p[:, :, :].rearrange("p a b -> p (a b)") for p in ps]
        ident, mean = const[:, 0, :], const[:, 1, :]

        raw_in = [sig("raw_in_A"), sig("raw_in_B")]
        hi_done = [sig("hi_done_A"), sig("hi_done_B")]
        lo_done = [sig("lo_done_A"), sig("lo_done_B")]
        mm_done = [sig("mm_done_A"), sig("mm_done_B")]
        ps_free = [sig("ps_free_A"), sig("ps_free_B")]

        def pcol(name, i):
            return par[:, ds(COL[name] + i, 1)]

        def project(count, strips, scalar=None, vector=None, pool=None, own=(), vector_alone=None,
                    scalar_first=None):
            ns = len(strips)

            def split_hi(act, s, i):
                kt = strips[s][2]
                act.wait_ge(raw_in[s].sem, raw_in[s].at(16 * (i + 1)))
                act.wait_ge(mm_done[s].sem, mm_done[s].at(i))
                act.activation(whi[s][:, 0:kt, :], wraw[s][:, 0:kt * P].rearrange("p (k n) -> p k n", n=P),
                               ACT.Copy).then_inc(hi_done[s].sem, 1)

            def split_lo(pl, s, i):
                kt = strips[s][2]
                pl.wait_ge(hi_done[s].sem, hi_done[s].at(i + 1))
                pl.tensor_tensor(wlo[s][:, 0:kt, :], wraw[s][:, 0:kt * P].rearrange("p (k n) -> p k n", n=P),
                                 whi[s][:, 0:kt, :].bitcast(fp32), ALU.subtract).then_inc(lo_done[s].sem, 1)

            def loop(eng, step):
                if count > 2:
                    with eng.Fori(0, count - 1) as i:
                        step(i, False)
                else:
                    for i in range(count - 1):
                        step(i, False)
                step(count - 1, True)

            with nc.Block() as block:
                @block.sync
                def _(sp):
                    def step(i, last):
                        for s in range(ns):
                            w, at, kt = strips[s][:3]
                            sp.wait_ge(lo_done[s].sem, lo_done[s].at(i))
                            sp.dma_start(wraw[s][:, 0:kt * P], w[ds(at(i), 1), :, :].rearrange("a p n -> p (a n)"))\
                              .then_inc(raw_in[s].sem, 16)
                    loop(sp, step)

                @block.scalar
                def _(act):
                    if scalar_first is not None:
                        scalar_first(act)
                    for s in range(ns):
                        split_hi(act, s, 0)

                    def step(i, last):
                        for s in range(ns):
                            if scalar is not None:
                                act.wait_ge(mm_done[s].sem, mm_done[s].at(i + 1))
                                scalar(act, s, i, last)
                            if not last:
                                split_hi(act, s, i + 1)
                    loop(act, step)

                @block.gpsimd
                def _(pl):
                    for s in range(ns):
                        split_lo(pl, s, 0)

                    def step(i, last):
                        for s in range(ns):
                            if not last:
                                split_lo(pl, s, i + 1)
                            if pool is not None:
                                pool(pl, s, i, last)
                    loop(pl, step)

                @block.tensor
                def _(pe):
                    def step(i, last):
                        for s in range(ns):
                            kt, xh, xl = strips[s][2:5]
                            pe.wait_ge(lo_done[s].sem, lo_done[s].at(i + 1))
                            pe.wait_ge(ps_free[s].sem, ps_free[s].at(i))
                            for k in range(kt):
                                for wp, xp in ((whi, xh), (whi, xl), (wlo, xh)):
                                    for h in range(2):
                                        mm = pe.matmul(ps[s][:, h, :], wp[s][:, k, :],
                                                       xp[:, k, h * HALF:(h + 1) * HALF],
                                                       start=(k == 0 and wp is whi and xp is xh),
                                                       stop=(k == kt - 1 and wp is wlo))
                            mm.then_inc(mm_done[s].sem, 1)
                    loop(pe, step)

                if vector is not None:
                    @block.vector
                    def _(dve):
                        def step(i, last):
                            for s in range(ns):
                                dve.wait_ge(mm_done[s].sem, mm_done[s].at(i + 1))
                                vector(dve, s, i, last)
                        loop(dve, step)
                elif vector_alone is not None:
                    block.vector(vector_alone)
            for s in range(ns):
                raw_in[s].passed(16 * count)
                for group in (hi_done, lo_done, mm_done, ps_free):
                    group[s].passed(count)
            for name, n in own:
                sig(name).passed(n)

        loaded = sig("loaded")
        made = sig("made")
        with nc.Block() as block:
            @block.sync
            def _(sp):
                sp.dma_start(H[:, :, :], A["xT"]).then_inc(loaded.sem, 16)
                sp.dma_start(par[:, :], A["params"]).then_inc(loaded.sem, 16)
                sp.dma_start(const[:, :, :], A["consts"][:, 0:3, :]).then_inc(loaded.sem, 16)

            @block.vector
            def _(dve):
                for n, v in enumerate((RMS_EPS, GN_EPS, LN_EPS, 0.0)):
                    dve.memset(eps[:, n:n + 1], v).then_inc(made.sem, 1)
                dve.wait_ge(made.sem, made.at(4))
                dve.wait_ge(loaded.sem, loaded.at(48))
        loaded.passed(48)
        made.passed(4)

        @stage
        def norm(src, gain, xh, xl, c, keep=None, n=DT, tag="", room=None):
            if room is None:
                room = sb("room" + tag, [P, 5, T], fp32, c)
            sq, rs, xn = room[:, 0:2, :], room[:, 2, :], room[:, 3:5, :]
            sq_done, sum_part, root, inv = sig("sq_done"), sig("sum_part"), sig("root"), sig("inv")
            xn_done, xh_done, xl_done = sig("xn_done"), sig("xh_done"), sig("xl_done")
            with nc.Block() as block:
                @block.scalar
                def _(act):
                    for k in range(n):
                        if k >= 2:
                            act.wait_ge(sum_part.sem, sum_part.at(k - 1))
                        act.activation(sq[:, k % 2, :], src[:, k, :], ACT.Square).then_inc(sq_done.sem, 1)
                    act.wait_ge(sum_part.sem, sum_part.at(n))
                    act.activation(rs, flat[2], ACT.Sqrt, bias=eps[:, 0:1]).then_inc(root.sem, 1)
                    if xh is not None:
                        for k in range(n):
                            act.wait_ge(xn_done.sem, xn_done.at(k + 1))
                            act.activation(xh[:, k, :], xn[:, k % 2, :], ACT.Copy).then_inc(xh_done.sem, 1)

                @block.tensor
                def _(pe):
                    for k in range(n):
                        pe.wait_ge(sq_done.sem, sq_done.at(k + 1))
                        for h in range(2):
                            mm = pe.matmul(ps[2][:, h, :], mean, sq[:, k % 2, h * HALF:(h + 1) * HALF],
                                           start=(k == 0), stop=(k == n - 1))
                        mm.then_inc(sum_part.sem, 1)

                @block.vector
                def _(dve):
                    dve.wait_ge(root.sem, root.at(1))
                    dve.reciprocal(rs, rs).then_inc(inv.sem, 1)
                    dve.wait_ge(inv.sem, inv.at(1))
                    for k in range(n):
                        if xh is not None and k >= 2:
                            dve.wait_ge(xl_done.sem, xl_done.at(k - 1))
                        if xh is not None:
                            dst = xn[:, k % 2, :]
                        else:
                            dst = keep[:, k, :]
                        dve.scalar_tensor_tensor(out=dst, in0=src[:, k, :], scalar=pcol(gain, k), in1=rs,
                                                 op0=ALU.mult, op1=ALU.mult).then_inc(xn_done.sem, 1)
                    if xh is None:
                        dve.wait_ge(xn_done.sem, xn_done.at(n))

                if xh is not None:
                    @block.gpsimd
                    def _(pl):
                        for k in range(n):
                            pl.wait_ge(xh_done.sem, xh_done.at(k + 1))
                            pl.tensor_tensor(xl[:, k, :], xn[:, k % 2, :], xh[:, k, :].bitcast(fp32),
                                             ALU.subtract).then_inc(xl_done.sem, 1)
            for s in (sq_done, sum_part):
                s.passed(n)
            root.passed(1)
            inv.passed(1)
            xn_done.passed(n)
            if xh is not None:
                xh_done.passed(n)
                xl_done.passed(n)

        def add_to_residual(kt, w, col, xh, xl, bias=None):
            def vector(dve, s, i, last):
                if bias is None:
                    dve.tensor_tensor(H[:, ds(2 * i + s, 1), :], ps_tile(s), H[:, ds(2 * i + s, 1), :],
                                      ALU.add).then_inc(ps_free[s].sem, 1)
                else:
                    dve.scalar_tensor_tensor(out=H[:, ds(2 * i + s, 1), :], in0=ps_tile(s),
                                             scalar=pcol(bias, 2 * i + s), in1=H[:, ds(2 * i + s, 1), :],
                                             op0=ALU.add, op1=ALU.add).then_inc(ps_free[s].sem, 1)
            wv = w[:, :, col * P:(col + kt) * P]
            project(DT // 2, [(wv, lambda i, s=s: 2 * i + s, kt, xh, xl) for s in range(2)], vector=vector)

        def ps_tile(s):
            return flat[s].rearrange("p (a t) -> p a t", a=1)

        def one(t):
            return t.rearrange("p (a t) -> p a t", a=1)

        @stage
        def ffn(l):
            with ExitStack() as c:
                xh = sb(f"ffn_xh{l}", [P, DT, T], r32, c)
                xl = sb(f"ffn_xl{l}", [P, DT, T], r32, c)
                with ExitStack() as c2:
                    norm(H, f"norm_ffn{l}", xh, xl, c2, tag=f"f{l}")
                hh = sb(f"ffn_hh{l}", [P, FF_GROUPS[0], T], r32, c)
                hl = sb(f"ffn_hl{l}", [P, FF_GROUPS[0], T], r32, c)
                gate = sb(f"ffn_gate{l}", [P, T], fp32, c)
                first = 0
                for g in FF_GROUPS:
                    hid_hi, hid_lo = sig("hid_hi"), sig("hid_lo")

                    def scalar(act, s, i, last):
                        if s == 0:
                            act.wait_ge(ps_free[1].sem, ps_free[1].at(i))
                            act.wait_ge(hid_lo.sem, hid_lo.at(i))
                            act.activation(gate[:, :], flat[0], ACT.Silu).then_inc(ps_free[0].sem, 1)
                        else:
                            act.wait_ge(ps_free[1].sem, ps_free[1].at(i + 1))
                            act.activation(hh[:, ds(i, 1), :], one(gate[:, :]), ACT.Copy).then_inc(hid_hi.sem, 1)

                    def vector(dve, s, i, last):
                        if s == 1:
                            dve.wait_ge(ps_free[0].sem, ps_free[0].at(i + 1))
                            dve.tensor_tensor(gate[:, :], flat[1], gate[:, :], ALU.mult)\
                               .then_inc(ps_free[1].sem, 1)

                    def pool(pl, s, i, last):
                        if s == 1:
                            pl.wait_ge(hid_hi.sem, hid_hi.at(i + 1))
                            pl.tensor_tensor(hl[:, ds(i, 1), :], one(gate[:, :]), hh[:, ds(i, 1), :].bitcast(fp32),
                                             ALU.subtract).then_inc(hid_lo.sem, 1)

                    w = A[f"ffn_in{l}"]
                    project(g, [(w, lambda i, o=first: o + i, DT, xh, xl), (w, lambda i, o=first: FT + o + i, DT, xh, xl)],
                            scalar, vector, pool, own=(("hid_hi", g), ("hid_lo", g)))
                    add_to_residual(g, A[f"ffn_out{l}"], first, hh, hl)
                    first += g

        @stage
        def ple(l):
            with ExitStack() as c:
                xh = sb(f"ple_xh{l}", [P, DT, T], r32, c)
                xl = sb(f"ple_xl{l}", [P, DT, T], r32, c)
                with ExitStack() as c2:
                    norm(H, f"norm_ple{l}", xh, xl, c2, tag=f"p{l}")
                p = sb(f"ple_p{l}", [P, PLE_T, T], fp32, c)
                ph = sb(f"ple_ph{l}", [P, PLE_T, T], r32, c)
                pl_ = sb(f"ple_pl{l}", [P, PLE_T, T], r32, c)
                gate = sb(f"ple_gate{l}", [P, T], fp32, c)
                split_operand(A["pT"][l], p, ph, pl_)
                used = sig("ple_used")

                def scalar(act, s, i, last):
                    if s == 0:
                        act.wait_ge(used.sem, used.at(i))
                        act.activation(gate[:, :], flat[0], ACT.Sigmoid).then_inc(ps_free[0].sem, 1)

                def vector(dve, s, i, last):
                    if s == 1:
                        dve.wait_ge(ps_free[0].sem, ps_free[0].at(i + 1))
                        dve.tensor_tensor(gate[:, :], flat[1], gate[:, :], ALU.mult).then_inc(ps_free[1].sem, 1)
                        dve.wait_ge(ps_free[1].sem, ps_free[1].at(i + 1))
                        dve.tensor_tensor(H[:, ds(i, 1), :], one(gate[:, :]), H[:, ds(i, 1), :],
                                          ALU.add).then_inc(used.sem, 1)
                project(DT, [(A[f"ple_gate{l}"], lambda i: i, DT, xh, xl), (A[f"ple_proj{l}"], lambda i: i, PLE_T, ph, pl_)],
                        scalar, vector, own=(("ple_used", DT),))

        @stage
        def split_operand(src, p, ph, pl_):
            p_in, p_hi, p_lo = sig("p_in"), sig("p_hi"), sig("p_lo")
            with nc.Block() as block:
                if src is not None:
                    @block.sync
                    def _(sp):
                        sp.dma_start(p[:, :, :], src).then_inc(p_in.sem, 16)

                @block.scalar
                def _(act):
                    if src is not None:
                        act.wait_ge(p_in.sem, p_in.at(16))
                    act.activation(ph[:, :, :], p[:, :, :], ACT.Copy).then_inc(p_hi.sem, 1)

                @block.gpsimd
                def _(pl):
                    pl.wait_ge(p_hi.sem, p_hi.at(1))
                    pl.tensor_tensor(pl_[:, :, :], p[:, :, :], ph[:, :, :].bitcast(fp32), ALU.subtract)\
                      .then_inc(p_lo.sem, 1)
            if src is not None:
                p_in.passed(16)
            p_hi.passed(1)
            p_lo.passed(1)

        @stage
        def hawk():
            with ExitStack() as c:
                gate = sb("hawk_gate", [P, RT, T], fp32, c)
                c_rec = ExitStack()
                rec = sb("hawk_rec", [P, RT, 3 + T], fp32, c_rec)
                with ExitStack() as c1:
                    xh = sb("hawk_xh", [P, DT, T], r32, c1)
                    xl = sb("hawk_xl", [P, DT, T], r32, c1)
                    norm(H, "norm_mix0", xh, xl, None, room=gate[:, 0:5, :])

                    def gelu(act, s, i, last):
                        act.activation(gate[:, ds(2 * i + s, 1), :], ps_tile(s), ACT.Gelu_apprx_tanh,
                                       bias=pcol("lru_b_in", 2 * i + s)).then_inc(ps_free[s].sem, 1)
                    project(RT // 2, [(A["hawk_in"], lambda i, s=s: 2 * i + s, DT, xh, xl) for s in range(2)], gelu)

                    def keep(act, s, i, last):
                        act.activation(rec[:, ds(2 * i + s, 1), 3:3 + T], ps_tile(s), ACT.Identity,
                                       bias=pcol("lru_b_in", RT + 2 * i + s)).then_inc(ps_free[s].sem, 1)
                    project(RT // 2, [(A["hawk_in"], lambda i, s=s: RT + 2 * i + s, DT, xh, xl) for s in range(2)], keep)
                lru(rec, gate)
                c_rec.close()
                xh = sb("lru_xh", [P, RT, T], r32, c)
                xl = sb("lru_xl", [P, RT, T], r32, c)
                split_operand(None, gate, xh, xl)
                add_to_residual(RT // 2, A["hawk_out"], 0, xh, xl, bias="lru_b_out")
                add_to_residual(RT // 2, A["hawk_out"], RT // 2, xh[:, RT // 2:RT, :], xl[:, RT // 2:RT, :])

        @stage
        def lru(rec, gate):
            with ExitStack() as c:
                gw = sb("lru_gw", [P, 2, P], fp32, c)
                sp8 = sb("lru_sp", [P, 8, RT], fp32, c)
                xf = sb("lru_xf", [P, T], fp32, c)
                ta = sb("lru_ta", [P, T], fp32, c)
                ti = sb("lru_ti", [P, T], fp32, c)
                av = sb("lru_a", [P, T], fp32, c)
                tz = sb("lru_tz", [P, T], fp32, c)
                e = sb("lru_e", [P, T], fp32, c)
                prep, gw_in, xf_done, gates = sig("lru_prep"), sig("lru_gw_in"), sig("lru_xf_done"), sig("lru_gates")
                t_done, e_done, s_done, b_done = sig("lru_t"), sig("lru_e"), sig("lru_s"), sig("lru_b")
                dchain, achain = sig("dve_chain"), sig("act_chain")
                lam = par[:, COL["lru_lambda"]:COL["lru_lambda"] + RT]
                with nc.Block() as block:
                    @block.vector
                    def _(dve):
                        ch = Chain(dve, dchain)
                        ch(dve.memset(rec[:, :, 0:3], 0.0))
                        ch(dve.tensor_scalar(sp8[:, 0, :], lam, -1.0, 0.0, ALU.mult, ALU.max))
                        ch(dve.scalar_tensor_tensor(out=sp8[:, 1, :], in0=sp8[:, 0, :], scalar=2.0, in1=lam,
                                                    op0=ALU.mult, op1=ALU.add))
                        dve.tensor_scalar(sp8[:, 6, :], par[:, COL["b_gate_a"]:COL["b_gate_a"] + RT], 0.5, None,
                                          ALU.mult).then_inc(prep.sem, 1)
                        dve.tensor_scalar(sp8[:, 7, :], par[:, COL["b_gate_x"]:COL["b_gate_x"] + RT], 0.5, None,
                                          ALU.mult).then_inc(prep.sem, 1)
                        dve.wait_ge(prep.sem, prep.at(3))
                        ch(dve.tensor_scalar(sp8[:, 3, :], sp8[:, 2, :], 1.0, None, ALU.add))
                        ch(dve.tensor_scalar(sp8[:, 4, :], sp8[:, 3, :], -1.0, None, ALU.add))
                        dve.tensor_scalar(sp8[:, 5, :], sp8[:, 4, :], 0.0, None, ALU.is_equal).then_inc(prep.sem, 1)
                        dve.wait_ge(prep.sem, prep.at(5))
                        ch(dve.tensor_tensor(sp8[:, 4, :], sp8[:, 4, :], sp8[:, 5, :], ALU.add))
                        ch(dve.tensor_tensor(sp8[:, 1, :], sp8[:, 1, :], sp8[:, 5, :], ALU.add))
                        ch(dve.reciprocal(sp8[:, 4, :], sp8[:, 4, :]))
                        ch(dve.tensor_tensor(sp8[:, 1, :], sp8[:, 1, :], sp8[:, 4, :], ALU.mult))
                        ch(dve.tensor_tensor(sp8[:, 1, :], sp8[:, 1, :], sp8[:, 2, :], ALU.mult))
                        ch(dve.tensor_tensor(sp8[:, 1, :], sp8[:, 1, :], sp8[:, 0, :], ALU.add))
                        ch(dve.tensor_scalar(sp8[:, 4, :], sp8[:, 1, :], 4.0, None, ALU.mult))
                        ch(dve.tensor_scalar(sp8[:, 5, :], sp8[:, 1, :], -4.0, None, ALU.mult))
                        chain_n.append(ch.n)

                    @block.scalar
                    def _(act):
                        act.wait_ge(prep.sem, prep.at(2))
                        act.wait_ge(dchain.sem, dchain.at(3))
                        act.activation(sp8[:, 2, :], sp8[:, 1, :], ACT.Exp, scale=-1.0).then_inc(prep.sem, 1)
                        act.wait_ge(prep.sem, prep.at(4))
                        act.wait_ge(dchain.sem, dchain.at(5))
                        act.activation(sp8[:, 1, :], sp8[:, 3, :], ACT.Ln).then_inc(prep.sem, 1)
                prep.passed(5)
                dchain.passed(chain_n.pop())

                def col(j, n):
                    return sp8[:, j, ds(n, 1)]
                with nc.Block() as block:
                    @block.sync
                    def _(sp):
                        with sp.Fori(0, RT) as n:
                            sp.wait_ge(gates.sem, gates.at(n))
                            sp.dma_start(gw[:, 0, :], A["gate_a"][ds(n, 1), :, :].rearrange("a p n -> p (a n)"))\
                              .then_inc(gw_in.sem, 16)
                            sp.dma_start(gw[:, 1, :], A["gate_x"][ds(n, 1), :, :].rearrange("a p n -> p (a n)"))\
                              .then_inc(gw_in.sem, 16)

                    @block.tensor
                    def _(pe):
                        with pe.Fori(0, RT) as n:
                            pe.wait_ge(gw_in.sem, gw_in.at(32 * n + 32))
                            pe.wait_ge(xf_done.sem, xf_done.at(n + 1))
                            pe.wait_ge(t_done.sem, t_done.at(n))
                            for j in range(2):
                                for h in range(2):
                                    mm = pe.matmul(ps[j][:, h, :], gw[:, j, :], xf[:, h * HALF:(h + 1) * HALF],
                                                   start=True, stop=True)
                            mm.then_inc(gates.sem, 1)

                    @block.scalar
                    def _(act):
                        per = 3
                        with act.Fori(0, RT) as n:
                            ch = Chain(act, achain, per * n)
                            act.wait_ge(gates.sem, gates.at(n + 1))
                            act.wait_ge(b_done.sem, b_done.at(n))
                            ch(act.activation(ta[:, :], flat[0], ACT.Tanh, scale=0.5, bias=col(6, n)))
                            act.activation(ti[:, :], flat[1], ACT.Tanh, scale=0.5, bias=col(7, n)).then_inc(t_done.sem, 1)
                            ch(act.activation(av[:, :], ta[:, :], ACT.Exp, scale=col(5, n), bias=col(5, n)))
                            ch(act.activation(tz[:, :], ta[:, :], ACT.Tanh, scale=col(4, n), bias=col(4, n)))
                            act.wait_ge(e_done.sem, e_done.at(n + 1))
                            act.activation(e[:, :], e[:, :], ACT.Sqrt).then_inc(s_done.sem, 1)
                            assert ch.n == per

                    @block.vector
                    def _(dve):
                        per = 7
                        with dve.Fori(0, RT) as n:
                            ch = Chain(dve, dchain, per * n)
                            dve.wait_ge(gates.sem, gates.at(n))
                            ch(dve.tensor_scalar(one(xf[:, :]), rec[:, ds(n, 1), 0:T], pcol("conv_w", n),
                                                 pcol("conv_b", n), ALU.mult, ALU.add))
                            for j in range(1, 4):
                                i = dve.scalar_tensor_tensor(out=one(xf[:, :]), in0=rec[:, ds(n, 1), j:j + T],
                                                             scalar=pcol("conv_w", j * RT + n), in1=one(xf[:, :]),
                                                             op0=ALU.mult, op1=ALU.add)
                                if j < 3:
                                    ch(i)
                            i.then_inc(xf_done.sem, 1)
                            dve.wait_ge(achain.sem, achain.at(3 * n + 3))
                            ch(dve.tensor_scalar(e[:, :], tz[:, :], 1.0, None, ALU.add))
                            ch(dve.reciprocal(e[:, :], e[:, :]))
                            dve.scalar_tensor_tensor(out=e[:, :], in0=tz[:, :], scalar=2.0, in1=e[:, :],
                                                     op0=ALU.mult, op1=ALU.mult).then_inc(e_done.sem, 1)
                            dve.wait_ge(t_done.sem, t_done.at(n + 1))
                            ch(dve.scalar_tensor_tensor(out=ti[:, :], in0=ti[:, :], scalar=1.0, in1=xf[:, :],
                                                        op0=ALU.add, op1=ALU.mult))
                            dve.wait_ge(s_done.sem, s_done.at(n + 1))
                            ch(dve.scalar_tensor_tensor(out=ti[:, :], in0=ti[:, :], scalar=0.5, in1=e[:, :],
                                                        op0=ALU.mult, op1=ALU.mult))
                            i = dve.tensor_tensor_scan(out=ta[:, :], data0=av[:, :], data1=ti[:, :], initial=0.0,
                                                       op0=ALU.mult, op1=ALU.add)
                            i.then_inc(sig("lru_scan").sem, 1)
                            dve.wait_ge(sig("lru_scan").sem, sig("lru_scan").at(n + 1))
                            dve.tensor_tensor(gate[:, ds(n, 1), :], one(ta[:, :]), gate[:, ds(n, 1), :], ALU.mult)\
                               .then_inc(b_done.sem, 1)
                            assert ch.n == per, ch.n
                dchain.passed(7 * RT)
                achain.passed(3 * RT)
                gw_in.passed(32 * RT)
                for s in (xf_done, gates, t_done, e_done, s_done, b_done, sig("lru_scan")):
                    s.passed(RT)

        def after(name, n):
            s = sig(name)
            return s.sem, s.at(n)

        def tick(name, by=1):
            return sig(name).sem, by

        def passed(counts):
            for name, n in counts.items():
                sig(name).passed(n)

        def dram(name, shape):
            return nc.dram_tensor(name, shape, fp32, kind="Internal").ap()

        def store_strips(dst, stage, func, bias=None):
            def scalar(act, s, i, last):
                m = 2 * i + s
                act.wait_ge(*after(f"strip_out_{'AB'[s]}", 16 * i))
                if bias is None:
                    act.activation(stage[:, s, :], flat[s], func).then_inc(ps_free[s].sem, 1)
                else:
                    act.activation(stage[:, s, :], flat[s], func, bias=pcol(bias, m)).then_inc(ps_free[s].sem, 1)
                act.wait_ge(ps_free[s].sem, ps_free[s].at(i + 1))
                act.dma_start(dst(m), stage[:, s, :]).then_inc(*tick(f"strip_out_{'AB'[s]}", 16))
                if last:
                    act.wait_ge(*after(f"strip_out_{'AB'[s]}", 16 * (i + 1)))
            return scalar

        @stage
        def rwkv():
            rows = lambda t: (lambda m: t[ds(m, 1), :, :].rearrange("a p t -> p (a t)"))
            R_, K_, V_ = (dram(f"rwd_{n}", [DT, P, T]) for n in "rkv")
            S_, A_, G_ = (dram(f"rwd_{n}", [DT, P, T]) for n in ("decay", "a", "g"))
            VG = dram("rw_vg", [4 * DT, P, 2 * P])
            QD = dram("rw_arbk", [4 * DT, P, 2, 4, P])
            PC = dram("rw_pc", [4 * DT, P, 4])
            BN = dram("rw_bonus", [DT, P, T])
            Y_ = dram("rw_y", [4 * DT, P, 2 * P])
            with ExitStack() as c:
                xn = sb("rw_xn", [P, DT, T], fp32, c)
                xh = sb("rw_xh", [P, DT, T], r32, c)
                xl = sb("rw_xl", [P, DT, T], r32, c)
                hh = sb("rw_hh", [P, 2, T], r32, c)
                hl = sb("rw_hl", [P, 2, T], r32, c)
                stage = sb("rw_stage", [P, 2, T], fp32, c)
                with ExitStack() as c2:
                    norm(H, "norm_mix1", None, None, c2, keep=xn, tag="r")

                def mixed(j):
                    with nc.Block() as block:
                        @block.gpsimd
                        def _(pl):
                            for k in range(DT):
                                if k >= 2:
                                    pl.wait_ge(*after("mix_hi", k - 1))
                                pl.tensor_tensor(stage[:, k % 2, 1:T], xn[:, k, 0:T - 1], xn[:, k, 1:T], ALU.subtract)\
                                  .then_inc(*tick("mix_diff"))
                                pl.tensor_scalar(stage[:, k % 2, 0:1], xn[:, k, 0:1], -1.0, None, ALU.mult)\
                                  .then_inc(*tick("mix_diff"))
                                if k >= 1:
                                    pl.wait_ge(*after("mix_hi", k))
                                    pl.tensor_tensor(xl[:, k - 1, :], stage[:, (k - 1) % 2, :],
                                                     xh[:, k - 1, :].bitcast(fp32), ALU.subtract).then_inc(*tick("mix_lo"))
                                    pl.wait_ge(*after("mix_lo", k))
                            k = DT
                            pl.wait_ge(*after("mix_hi", k))
                            pl.tensor_tensor(xl[:, k - 1, :], stage[:, (k - 1) % 2, :],
                                             xh[:, k - 1, :].bitcast(fp32), ALU.subtract).then_inc(*tick("mix_lo"))

                        @block.vector
                        def _(dve):
                            for k in range(DT):
                                dve.wait_ge(*after("mix_diff", 2 * k + 2))
                                dve.scalar_tensor_tensor(out=stage[:, k % 2, :], in0=stage[:, k % 2, :],
                                                         scalar=pcol("rw_mu", j * DT + k), in1=xn[:, k, :],
                                                         op0=ALU.mult, op1=ALU.add).then_inc(*tick("mix_x"))

                        @block.scalar
                        def _(act):
                            for k in range(DT):
                                act.wait_ge(*after("mix_x", k + 1))
                                act.activation(xh[:, k, :], stage[:, k % 2, :], ACT.Copy).then_inc(*tick("mix_hi"))
                    passed({"mix_diff": 2 * DT, "mix_x": DT, "mix_hi": DT, "mix_lo": DT})

                def wide(w, dst, m0=0, func=ACT.Copy, bias=None, kt=DT, x=(xh, xl)):
                    project(DT // 2, [(w, lambda i, s=s: m0 + 2 * i + s, kt, *x) for s in range(2)],
                            store_strips(dst, stage, func, bias),
                            own=(("strip_out_A", 16 * DT // 2), ("strip_out_B", 16 * DT // 2)))

                def narrow(w, nt, func):
                    def scalar(act, s, i, last):
                        act.activation(stage[:, s, :], flat[s], func).then_inc(ps_free[s].sem, 1)
                        act.wait_ge(ps_free[s].sem, ps_free[s].at(1))
                        act.activation(hh[:, s, :], stage[:, s, :], ACT.Copy).then_inc(*tick("lora_hi"))

                    def pool(pl, s, i, last):
                        pl.wait_ge(*after("lora_hi", s + 1))
                        pl.tensor_tensor(hl[:, s, :], stage[:, s, :], hh[:, s, :].bitcast(fp32), ALU.subtract)\
                          .then_inc(*tick("lora_lo"))
                    project(1, [(w, lambda i, s=s: i + s, DT, xh, xl) for s in range(nt)], scalar, pool=pool,
                            own=(("lora_hi", nt), ("lora_lo", nt)))

                mixed(0)
                wide(A["rkv"], rows(R_))
                mixed(2)
                wide(A["rkv"], rows(K_), DT)
                mixed(3)
                wide(A["rkv"], rows(V_), 2 * DT)
                mixed(1)
                narrow(A["rw_w1"], 1, ACT.Tanh)
                wide(A["rw_w2"], rows(S_), 0, ACT.Sigmoid, "rw_w0", 1, (hh, hl))
                mixed(4)
                narrow(A["rw_a1"], 1, ACT.Copy)
                wide(A["rw_a2"], rows(A_), 0, ACT.Sigmoid, "rw_a0", 1, (hh, hl))
                mixed(5)
                narrow(A["rw_g1"], 2, ACT.Sigmoid)
                wide(A["rw_g2"], rows(G_), 0, ACT.Copy, None, 2, (hh, hl))

            rwkv_operands(R_, K_, V_, S_, A_, QD, PC, BN, VG)
            rwkv_scan(QD, PC, VG, Y_)
            with ExitStack() as c:
                o = sb("rw_o", [P, DT, T], fp32, c)
                xh = sb("rwo_xh", [P, DT, T], r32, c)
                xl = sb("rwo_xl", [P, DT, T], r32, c)
                rwkv_output(Y_, BN, G_, o)
                split_operand(None, o, xh, xl)
                add_to_residual(DT, A["rw_o"], 0, xh, xl)

        DECAY = float(np.exp(-0.5))

        @stage
        def rwkv_operands(R_, K_, V_, S_, A_, QD, PC, BN, VG):
            with ExitStack() as c:
                heads = const[:, 2, :]
                reset = sb("op_reset", [P, T], fp32, c)
                x = {n: sb(f"op_{n}", [P, T], fp32, c) for n in
                     ("r", "k", "v", "w", "a", "s", "sm", "p", "pi", "pp", "kk", "t", "inv", "b", "k2", "rk", "bn")}
                q = sb("op_q", [P, 4, 2, 4, P], fp32, c)
                pc = sb("op_pc", [P, 16], fp32, c)
                src = {"r": R_, "k": K_, "v": V_, "w": S_, "a": A_}

                def part(j):
                    return q[:, :, :, j, :].rearrange("p g q t -> p (g q) t")

                def by8(t):
                    return t[:, :].rearrange("p (g t) -> p g t", g=8)
                with nc.Block() as block:
                    @block.vector
                    def _(dve):
                        dve.memset(reset[:, :], 1.0).then_inc(*tick("op_reset"))
                        dve.wait_ge(*after("op_reset", 1))
                        dve.memset(reset[:, 0:T:CHUNK], 0.0).then_inc(*tick("op_reset"))
                        dve.wait_ge(*after("op_reset", 2))
                passed({"op_reset": 2})
                with nc.Block() as block:
                    @block.sync
                    def _(sp):
                        with sp.Fori(0, DT) as m:
                            for n in src:
                                sp.wait_ge(*after("op_out", 16 * 7 * m))
                                sp.dma_start(x[n][:, :], src[n][ds(m, 1), :, :].rearrange("a p t -> p (a t)"))\
                                  .then_inc(*tick("op_in", 16))
                            sp.wait_ge(*after("op_q", 4 * m + 4))
                            for g in range(4):
                                sp.dma_start(QD[ds(4 * m + g, 1), :, :, :, :].rearrange("a p q j t -> p (a q j t)"),
                                             q[:, g, :, :, :].rearrange("p q j t -> p (q j t)")).then_inc(*tick("op_out", 16))
                            sp.wait_ge(*after("op_pc", m + 1))
                            sp.dma_start(PC[ds(4 * m, 4), :, :].rearrange("g p c -> p g c"),
                                         pc[:, :].rearrange("p (g c) -> p g c", g=4)).then_inc(*tick("op_out", 16))
                            sp.dma_start(VG[ds(4 * m, 4), :, :].rearrange("g p t -> p g t"),
                                         x["v"][:, :].rearrange("p (g t) -> p g t", g=4)).then_inc(*tick("op_out", 16))
                            sp.wait_ge(*after("op_bonus", m + 1))
                            sp.dma_start(BN[ds(m, 1), :, :].rearrange("a p t -> p (a t)"), x["bn"][:, :])\
                              .then_inc(*tick("op_out", 16))
                        sp.wait_ge(*after("op_out", 16 * 7 * DT))

                    @block.gpsimd
                    def _(pl):
                        with pl.Fori(0, DT) as m:
                            pl.wait_ge(*after("op_s", m + 1))
                            pl.tensor_tensor(x["sm"][:, :], x["s"][:, :], x["w"][:, :], ALU.subtract)\
                              .then_inc(*tick("op_sm"))
                            pl.wait_ge(*after("op_p", m + 1))
                            pl.tensor_tensor(part(1), by8(x["r"]), by8(x["p"]), ALU.mult).then_inc(*tick("op_q"))
                            pl.tensor_copy(pc[:, :], x["p"][:, CHUNK - 1:T:CHUNK]).then_inc(*tick("op_pc"))
                            pl.wait_ge(*after("op_k2", m + 1))
                            pl.wait_ge(*after("op_pi", m + 1))
                            pl.tensor_tensor(part(3), by8(x["k2"]), by8(x["pi"]), ALU.mult).then_inc(*tick("op_q"))

                    @block.scalar
                    def _(act):
                        with act.Fori(0, DT) as m:
                            act.wait_ge(*after("op_in", 80 * m + 80))
                            act.wait_ge(*after("op_s", m + 1))
                            act.activation(x["p"][:, :], x["s"][:, :], ACT.Exp, scale=-DECAY).then_inc(*tick("op_p"))
                            act.activation(x["pi"][:, :], x["s"][:, :], ACT.Exp, scale=DECAY).then_inc(*tick("op_pi"))
                            act.wait_ge(*after("op_sm", m + 1))
                            act.activation(x["pp"][:, :], x["sm"][:, :], ACT.Exp, scale=-DECAY).then_inc(*tick("op_pp"))
                            act.wait_ge(*after("op_kk", m + 1))
                            act.activation(x["t"][:, :], x["kk"][:, :], ACT.Square).then_inc(*tick("op_sq"))
                            act.wait_ge(*after("op_norm", m + 1))
                            act.activation(x["inv"][:, :], flat[0], ACT.Sqrt).then_inc(*tick("op_root"))

                    @block.tensor
                    def _(pe):
                        with pe.Fori(0, DT) as m:
                            pe.wait_ge(*after("op_sq", m + 1))
                            for h in range(2):
                                mm = pe.matmul(ps[0][:, h, :], heads, x["t"][:, h * HALF:(h + 1) * HALF],
                                               start=True, stop=True)
                            mm.then_inc(*tick("op_norm"))
                            pe.wait_ge(*after("op_rk", m + 1))
                            pe.wait_ge(*after("op_bonus", m))
                            for h in range(2):
                                mm = pe.matmul(ps[1][:, h, :], heads, x["rk"][:, h * HALF:(h + 1) * HALF],
                                               start=True, stop=True)
                            mm.then_inc(*tick("op_rksum"))

                    @block.vector
                    def _(dve):
                        with dve.Fori(0, DT) as m:
                            dve.wait_ge(*after("op_in", 80 * m + 80))
                            dve.wait_ge(*after("op_out", 16 * 7 * m))
                            dve.tensor_tensor_scan(out=x["s"][:, :], data0=reset[:, :], data1=x["w"][:, :],
                                                   initial=0.0, op0=ALU.mult, op1=ALU.add).then_inc(*tick("op_s"))
                            dve.tensor_scalar(x["kk"][:, :], x["k"][:, :], pcol("rw_k_k", m), None, ALU.mult)\
                               .then_inc(*tick("op_kk"))
                            dve.tensor_scalar(x["b"][:, :], x["a"][:, :], -1.0, pcol("rw_k_a", m), ALU.add, ALU.mult)\
                               .then_inc(*tick("op_v"))
                            dve.wait_ge(*after("op_v", 6 * m + 1))
                            dve.scalar_tensor_tensor(out=x["k2"][:, :], in0=x["b"][:, :], scalar=1.0, in1=x["k"][:, :],
                                                     op0=ALU.add, op1=ALU.mult).then_inc(*tick("op_k2"))
                            dve.wait_ge(*after("op_k2", m + 1))
                            dve.scalar_tensor_tensor(out=x["rk"][:, :], in0=x["r"][:, :], scalar=pcol("rw_r_k", m),
                                                     in1=x["k2"][:, :], op0=ALU.mult, op1=ALU.mult).then_inc(*tick("op_rk"))
                            dve.wait_ge(*after("op_root", m + 1))
                            dve.tensor_scalar(x["inv"][:, :], x["inv"][:, :], 1e-12, None, ALU.max).then_inc(*tick("op_v"))
                            dve.wait_ge(*after("op_v", 6 * m + 2))
                            dve.reciprocal(x["inv"][:, :], x["inv"][:, :]).then_inc(*tick("op_v"))
                            dve.wait_ge(*after("op_v", 6 * m + 3))
                            dve.tensor_tensor(x["kk"][:, :], x["kk"][:, :], x["inv"][:, :], ALU.mult).then_inc(*tick("op_v"))
                            dve.wait_ge(*after("op_v", 6 * m + 4))
                            dve.wait_ge(*after("op_pp", m + 1))
                            dve.scalar_tensor_tensor(out=part(0), in0=by8(x["kk"]), scalar=-1.0, in1=by8(x["pp"]),
                                                     op0=ALU.mult, op1=ALU.mult).then_inc(*tick("op_q"))
                            dve.tensor_tensor(x["b"][:, :], x["kk"][:, :], x["a"][:, :], ALU.mult).then_inc(*tick("op_v"))
                            dve.wait_ge(*after("op_v", 6 * m + 5))
                            dve.wait_ge(*after("op_pi", m + 1))
                            dve.tensor_tensor(part(2), by8(x["b"]), by8(x["pi"]), ALU.mult).then_inc(*tick("op_q"))
                            dve.wait_ge(*after("op_rksum", m + 1))
                            dve.tensor_tensor(x["bn"][:, :], flat[1], x["v"][:, :], ALU.mult).then_inc(*tick("op_bonus"))
                            dve.wait_ge(*after("op_bonus", m + 1))
                            dve.memset(x["inv"][:, 0:1], 0.0).then_inc(*tick("op_v"))
                            dve.wait_ge(*after("op_v", 6 * m + 6))
                passed({"op_in": 80 * DT, "op_out": 112 * DT, "op_q": 4 * DT, "op_v": 6 * DT})
                passed({n: DT for n in ("op_s", "op_sm", "op_p", "op_pi", "op_pp", "op_pc", "op_kk", "op_k2", "op_sq",
                                        "op_norm", "op_root", "op_rk", "op_rksum", "op_bonus")})

        @stage
        def rwkv_scan(QD, PC, VG, Y_):
            NG = 4 * DT
            LEVELS = (2, 4, 8, 16, 32)
            with ExitStack() as c:
                masks = sb("sc_masks", [P, 4, P], fp32, c)
                levels = sb("sc_levels", [P, 6, P], fp32, c)
                ident2 = sb("sc_ident2", [P, HEAD], fp32, c)
                flags = sb("sc_flags", [P, NG], fp32, c)
                ops = sb("sc_ops", [P, 2, 2, 4, P], fp32, c)
                vv = sb("sc_v", [P, 2, 2, P], fp32, c)
                pcs = sb("sc_pc", [P, 2, 4], fp32, c)
                tm = sb("sc_tm", [P, 2, 3, P], fp32, c)
                arhs = sb("sc_arhs", [P, 2, 2, 2, HEAD], fp32, c)
                G = sb("sc_G", [P, 4, 4, P], fp32, c)
                NT = sb("sc_NT", [P, 6, 4, P], fp32, c)
                X = sb("sc_X", [P, 4, P], fp32, c)
                XT = sb("sc_XT", [P, 4, P], fp32, c)
                Wt = sb("sc_Wt", [P, 4, P], fp32, c)
                WZ = sb("sc_WZ", [P, 4, 2, HEAD], fp32, c)
                MT = sb("sc_MT", [P, 2, 4, HEAD], fp32, c)
                Q = sb("sc_Q", [P, 2, 4, HEAD], fp32, c)
                F = sb("sc_F", [P, 2, 2 * P], fp32, c)
                Yi = sb("sc_Yi", [P, 2, 2 * P], fp32, c)
                y = sb("sc_y", [P, 2, 2 * P], fp32, c)
                S = sb("sc_S", [P, 5, HEAD], fp32, c)
                bank = [ps[b // 2][:, b % 2, :] for b in range(8)]
                four = [b.rearrange("p (u t) -> p u t", u=4) for b in bank]

                with nc.Block() as block:
                    @block.sync
                    def _(sp):
                        for n, name in enumerate(("mask_a", "mask_r", "mask_a", "mask_r")):
                            sp.dma_start(masks[:, n, :], A["consts"][:, CIX[name], :]).then_inc(*tick("sc_const", 16))
                        sp.dma_start(levels[:, :, :], A["consts"][:, CIX["level1"]:CIX["level1"] + 6, :])\
                          .then_inc(*tick("sc_const", 16))
                        sp.dma_start(ident2[:, :], A["scan_ident"]).then_inc(*tick("sc_const", 16))
                        sp.dma_start(flags[:, :], A["scan_flags"]).then_inc(*tick("sc_const", 16))
                        sp.wait_ge(*after("sc_const", 112))

                    @block.vector
                    def _(dve):
                        dve.memset(S[:, :, :], 0.0).then_inc(*tick("sc_const0"))
                        dve.wait_ge(*after("sc_const0", 1))
                passed({"sc_const": 112, "sc_const0": 1})

                def half(e):
                    return slice(e * HEAD, (e + 1) * HEAD)

                def loop(eng, body, tail=None):
                    body(0, None, 0, 0, None, True)
                    with eng.Fori(0, (NG - 2) // 2) as i:
                        body(2 * i + 1, 2 * i, 1, i, i, False)
                        body(2 * i + 2, 2 * i + 1, 0, i + 1, i, False)
                    body(NG - 1, NG - 2, 1, NG // 2 - 1, NG // 2 - 1, False)
                    if tail is not None:
                        tail()

                with nc.Block() as block:
                    @block.sync
                    def _(sp):
                        def body(n, b, j, r, rb, first):
                            if not first:
                                sp.wait_ge(*after("sc_slot_free", b))
                            sp.dma_start(ops[:, j, :, :, :].rearrange("p q j t -> p (q j t)"),
                                         QD[ds(n, 1), :, :, :, :].rearrange("a p q j t -> p (a q j t)")).then_inc(*tick(f"sc_in_{j}", 16))
                            sp.dma_start(vv[:, j, :, :].rearrange("p q t -> p (q t)"),
                                         VG[ds(n, 1), :, :].rearrange("a p t -> p (a t)")).then_inc(*tick(f"sc_in_{j}", 16))
                            sp.dma_start(pcs[:, j, :], PC[ds(n, 1), :, :].rearrange("a p c -> p (a c)"))\
                              .then_inc(*tick(f"sc_in_{j}", 16))
                            if not first:
                                out_y(b, 1 - j)

                        def out_y(n, j):
                            sp.wait_ge(*after("sc_y", n + 1))
                            sp.dma_start(Y_[ds(n, 1), :, :].rearrange("a p t -> p (a t)"), y[:, j, :])\
                              .then_inc(*tick(f"sc_y_out_{j}", 16))

                        def tail():
                            out_y(NG - 1, 1)
                            for j in range(2):
                                sp.wait_ge(*after(f"sc_y_out_{j}", 8 * NG))
                        loop(sp, body, tail)

                    @block.tensor
                    def _(pe):
                        def chain_ready(n, c):
                            pe.wait_ge(*after("sc_S", 5 * n + c + 1))
                            if c == 0:
                                pe.wait_ge(*after("sc_F", n + 1))
                                pe.wait_ge(*after("sc_y", n))

                        def chain(n, j, c):
                            for e in range(2):
                                mm = pe.matmul(bank[5][half(e), c * HEAD:(c + 1) * HEAD],
                                               MT[half(e), j, c, :], S[half(e), c, :], start=True, stop=True,
                                               tile_position=(e * HEAD, e * HEAD))
                            mm.then_inc(*tick("pe_state"))
                            for e in range(2):
                                mm = pe.matmul(bank[4][half(e), c * HEAD:(c + 1) * HEAD], S[half(e), c, :],
                                               F[half(e), j, c * CHUNK:(c + 1) * CHUNK], start=True, stop=True,
                                               tile_position=(e * HEAD, e * HEAD))
                            mm.then_inc(*tick("pe_y"))

                        def body(n, b, j, r, rb, first):
                            pe.wait_ge(*after(f"sc_in_{j}", 48 * r + 48))
                            pe.wait_ge(*after("sc_Yi", n))
                            pe.wait_ge(*after("sc_XTL", n))
                            for q in range(2):
                                for t, src in enumerate((ops[:, j, q, 0, :], ops[:, j, q, 2, :], ops[:, j, q, 3, :],
                                                         vv[:, j, q, :])):
                                    mm = pe.transpose(bank[q][:, t * P:(t + 1) * P], src, ident)
                            mm.then_inc(*tick("pe_tm"))
                            pe.wait_ge(*after("sc_F", n))
                            pe.wait_ge(*after("sc_Q", n))
                            if not first:
                                pe.wait_ge(*after("sc_y", b))
                            for q in range(2):
                                for e in range(2):
                                    for z in range(2):
                                        mm = pe.matmul(bank[2 + 2 * q + e][:, z * 256:(z + 1) * 256],
                                                       ops[half(e), j, q, 2 + z, :],
                                                       ops[half(e), j, q, 0:2, :].rearrange("p j t -> p (j t)"),
                                                       start=True, stop=True, tile_position=(e * HEAD, 0))
                                    mm.then_inc(*tick("pe_score"))
                            pe.wait_ge(*after("sc_X1", n + 1))
                            pe.wait_ge(*after("sc_tm", 2 * n + 2))
                            for u in range(4):
                                mm = pe.transpose(four[0][:, u, :], XT[:, u, :], ident)
                            mm.then_inc(*tick("pe_X"))
                            for li, s in enumerate(LEVELS):
                                pe.wait_ge(*after("sc_X", 5 * n + li + 1))
                                pe.wait_ge(*after("sc_NT", 5 * n + li + 1))
                                if li >= 1 and not first:
                                    chain_ready(b, li - 1)
                                for u in range(4):
                                    mm = pe.matmul(four[6][:, u, :], NT[:, li + 1, u, :], X[:, u, :], start=True, stop=True)
                                mm.then_inc(*tick("pe_W"))
                                if li == 0:
                                    pe.wait_ge(*after("sc_tm", 2 * n + 2))
                                    pe.wait_ge(*after("sc_G", 4 * n + 4))
                                    for q in range(2):
                                        for e in range(2):
                                            mm = pe.matmul(bank[1][:, (2 * q + e) * HEAD:(2 * q + e + 1) * HEAD],
                                                           G[:, 2 * q + e, 2, :], tm[:, q, 2, half(e)], start=True, stop=True)
                                    mm.then_inc(*tick("pe_akv"))
                                elif not first:
                                    chain(b, 1 - j, li - 1)
                                pe.wait_ge(*after("sc_W", 5 * n + li + 1))
                                pe.wait_ge(*after("sc_XT", 4 * n + li))
                                if li < 4:
                                    for u in range(4):
                                        mm = pe.matmul(four[7][:, u, :], XT[:, u, :], Wt[:, u, :], start=True, stop=True)
                                    mm.then_inc(*tick("pe_Y"))

                                for u in range(4):
                                    mm = pe.matmul(four[0][:, u, :], Wt[:, u, :], XT[:, u, :], start=True, stop=True)
                                mm.then_inc(*tick("pe_YT"))
                            pe.wait_ge(*after("sc_XTL", n + 1))
                            pe.wait_ge(*after("sc_akv", n + 1))
                            for q in range(2):
                                for e in range(2):
                                    mm = pe.matmul(four[2][:, 2 * q + e, :], XT[:, 2 * q + e, :],
                                                   arhs[:, q, e, :, :].rearrange("p z f -> p (z f)"), start=True, stop=True)
                            mm.then_inc(*tick("pe_WZ"))
                            pe.wait_ge(*after("sc_WZ", n + 1))
                            pe.wait_ge(*after("sc_y", n))
                            for q in range(2):
                                for e in range(2):
                                    mm = pe.matmul(bank[4][half(e), q * P:(q + 1) * P], WZ[:, 2 * q + e, 0, :],
                                                   G[:, 2 * q + e, 1, :], start=True, stop=True,
                                                   tile_position=(0, e * HEAD))
                            mm.then_inc(*tick("pe_F"))
                            for h in range(2):
                                for q in range(2):
                                    for e in range(2):
                                        mm = pe.matmul(bank[3 - h][half(e), q * HEAD:(q + 1) * HEAD],
                                                       WZ[half(h), 2 * q + e, 0, :], tm[half(h), q, 0, half(e)],
                                                       start=True, stop=True, tile_position=(h * HEAD, e * HEAD))
                            mm.then_inc(*tick("pe_MT"))
                            for h in range(2):
                                for q in range(2):
                                    for e in range(2):
                                        dst = bank[3 - h][half(e), P + q * HEAD:P + (q + 1) * HEAD]
                                        pe.matmul(dst, tm[half(h), q, 0, half(e)], WZ[half(h), 2 * q + e, 1, :],
                                                  start=True, stop=False, tile_position=(h * HEAD, e * HEAD))
                                        mm = pe.matmul(dst, tm[half(h), q, 1, half(e)], tm[half(h), q, 2, half(e)],
                                                       start=False, stop=True, tile_position=(h * HEAD, e * HEAD))
                            mm.then_inc(*tick("pe_Q"))
                            for q in range(2):
                                for e in range(2):
                                    dst = bank[1][half(e), q * P:(q + 1) * P]
                                    pe.matmul(dst, WZ[:, 2 * q + e, 1, :], G[:, 2 * q + e, 1, :], start=True, stop=False,
                                              tile_position=(0, e * HEAD))
                                    mm = pe.matmul(dst, tm[:, q, 2, half(e)], G[:, 2 * q + e, 3, :], start=False, stop=True,
                                                   tile_position=(0, e * HEAD))
                            mm.then_inc(*tick("pe_Yi"))

                        def tail():
                            for c in range(4):
                                chain_ready(NG - 1, c)
                                chain(NG - 1, 1, c)
                        loop(pe, body, tail)

                    @block.scalar
                    def _(act):
                        def body(n, b, j, r, rb, first):
                            act.wait_ge(*after("pe_tm", n + 1))
                            act.wait_ge(*after("pe_Yi", n))
                            for q in range(2):
                                act.activation(arhs[:, q, :, 0, :],
                                               bank[q][:, 0:P].rearrange("p (e f) -> p e f", e=2), ACT.Copy)\
                                   .then_inc(*tick("sc_arhs"))
                                act.activation(tm[:, q, :, :], bank[q][:, P:4 * P].rearrange("p (z f) -> p z f", z=3),
                                               ACT.Copy).then_inc(*tick("sc_tm"))
                            act.wait_ge(*after("pe_X", n + 1))
                            act.activation(X[:, :, :], four[0], ACT.Copy).then_inc(*tick("sc_X"))
                            for li in range(5):
                                act.wait_ge(*after("pe_W", 5 * n + li + 1))
                                act.wait_ge(*after("pe_YT", 5 * n + li))
                                act.activation(Wt[:, :, :], four[6], ACT.Copy).then_inc(*tick("sc_W"))
                                if li == 0:
                                    act.wait_ge(*after("pe_akv", n + 1))
                                    act.activation(arhs[:, :, :, 1, :],
                                                   bank[1][:, 0:256].rearrange("p (q e f) -> p q e f", q=2, e=2), ACT.Copy)\
                                       .then_inc(*tick("sc_akv"))
                            act.wait_ge(*after("pe_WZ", n + 1))
                            act.activation(WZ[:, :, :, :].rearrange("p u z f -> p (u z f)"), bank[2], ACT.Copy)\
                               .then_inc(*tick("sc_WZ"))
                            act.wait_ge(*after("pe_Yi", n + 1))
                            if not first:
                                act.wait_ge(*after("sc_y", b))
                            act.activation(Yi[:, j, :], bank[1][:, 0:256], ACT.Copy).then_inc(*tick("sc_Yi"))
                        loop(act, body)

                    @block.gpsimd
                    def _(pl):
                        def body(n, b, j, r, rb, first):
                            pl.wait_ge(*after("sc_G", 4 * n + 4))
                            for li in range(5):
                                pl.wait_ge(*after("pe_W", 5 * b + li + 1) if not first else after("sc_G", 4))
                                for u in range(4):
                                    op = pl.tensor_tensor(NT[:, li + 1, u, :], G[:, u, 0, :], levels[:, li + 1, :], ALU.mult)
                                op.then_inc(*tick("sc_NT"))
                        loop(pl, body)

                    @block.vector
                    def _(dve):
                        def chain(n, j, r, c):
                            if c == 0:
                                dve.wait_ge(*after("sc_S", 5 * n))
                                dve.tensor_scalar(S[:, 0, :], S[:, 4, :], flags[:, ds(n, 1)], None, ALU.mult)\
                                   .then_inc(*tick("sc_S"))
                            dve.wait_ge(*after("pe_state", 4 * n + c + 1))
                            if c == 0:
                                dve.wait_ge(*after("pe_y", 4 * n))
                                dve.wait_ge(*after("sc_Q", n + 1))
                            dve.scalar_tensor_tensor(out=S[:, c + 1, :], in0=bank[5][:, c * HEAD:(c + 1) * HEAD],
                                                     scalar=pcs[:, j, c:c + 1], in1=Q[:, j, c, :],
                                                     op0=ALU.mult, op1=ALU.add).then_inc(*tick("sc_S"))
                            if c == 3:
                                dve.wait_ge(*after("pe_y", 4 * n + 4))
                                dve.wait_ge(*after("sc_Yi", n + 1))
                                dve.wait_ge(*after("sc_S", 5 * n + 5))
                                dve.wait_ge(*after(f"sc_y_out_{j}", 16 * r))
                                dve.tensor_tensor(y[:, j, :], bank[4][:, 0:256], Yi[:, j, :], ALU.add)\
                                   .then_inc(*tick("sc_y"))

                        def body(n, b, j, r, rb, first):
                            for u in range(4):
                                dve.wait_ge(*after("pe_score", 4 * n + u + 1))
                                if u == 0:
                                    dve.wait_ge(*after("pe_Yi", n))
                                    dve.wait_ge(*after("sc_NT", 5 * n))
                                dve.tensor_tensor(G[:, u, :, :].rearrange("p z t -> p (z t)"), bank[2 + u],
                                                  masks[:, :, :].rearrange("p z t -> p (z t)"), ALU.mult)\
                                   .then_inc(*tick("sc_G"))
                            dve.wait_ge(*after("sc_G", 4 * n + 4))
                            for u in range(4):
                                i = dve.tensor_tensor(XT[:, u, :], G[:, u, 0, :], levels[:, 0, :], ALU.mult)
                                i.then_inc(*tick("sc_v"))
                            dve.wait_ge(*after("sc_v", 4 * n + 4))
                            for u in range(4):
                                i = dve.tensor_tensor(XT[:, u, :], XT[:, u, :], ident, ALU.add)
                            i.then_inc(*tick("sc_X1"))
                            for li in range(5):
                                if 1 <= li and not first:
                                    chain(b, 1 - j, rb, li - 1)
                                if li < 4:
                                    dve.wait_ge(*after("pe_Y", 4 * n + li + 1))
                                    dve.wait_ge(*after("sc_X", 5 * n + li + 1))
                                    dve.tensor_tensor(X[:, :, :], four[7], X[:, :, :], ALU.add).then_inc(*tick("sc_X"))
                                dve.wait_ge(*after("pe_YT", 5 * n + li + 1))
                                if li == 0:
                                    dve.wait_ge(*after("sc_X1", n + 1))
                                else:
                                    dve.wait_ge(*after("sc_XT", 4 * n + li))
                                dve.tensor_tensor(XT[:, :, :], four[0], XT[:, :, :], ALU.add)\
                                   .then_inc(*tick("sc_XT" if li < 4 else "sc_XTL"))

                            dve.wait_ge(*after("pe_Q", n + 1))
                            for h in range(2):
                                op = dve.tensor_tensor(MT[:, j, h:4:2, :], bank[3 - h][:, 0:P].rearrange("p (c f) -> p c f", c=2),
                                                       ident2[:, :].unsqueeze(1).to_broadcast([P, 2, HEAD]), ALU.add)
                            op.then_inc(*tick("sc_MT"))
                            for h in range(2):
                                op = dve.tensor_tensor(Q[:, j, h:4:2, :], bank[3 - h][:, P:2 * P].rearrange("p (c f) -> p c f", c=2),
                                                       pcs[:, j, h:4:2].unsqueeze(2).to_broadcast([P, 2, HEAD]), ALU.mult)
                            op.then_inc(*tick("sc_Q"))
                            dve.wait_ge(*after("pe_F", n + 1))
                            dve.tensor_tensor(F[:, j, :].rearrange("p (q t) -> p q t", q=2),
                                              bank[4][:, 0:256].rearrange("p (q t) -> p q t", q=2), ops[:, j, :, 1, :],
                                              ALU.add).then_inc(*tick("sc_F"))
                            dve.wait_ge(*after("sc_F", n + 1))
                            if not first:
                                dve.memset(S[:, 1, 0:1], 0.0).then_inc(*tick("sc_slot_free"))

                        def tail():
                            for c in range(4):
                                chain(NG - 1, 1, NG // 2 - 1, c)
                        loop(dve, body, tail)
                passed({"sc_in_0": 24 * NG, "sc_in_1": 24 * NG, "sc_y_out_0": 8 * NG, "sc_y_out_1": 8 * NG, "pe_score": 4 * NG, "sc_G": 4 * NG, "sc_v": 4 * NG, "pe_W": 5 * NG,
                        "pe_YT": 5 * NG, "sc_W": 5 * NG, "sc_NT": 5 * NG, "sc_X": 5 * NG, "sc_XT": 4 * NG, "pe_Y": 4 * NG,
                        "sc_S": 5 * NG, "pe_state": 4 * NG, "pe_y": 4 * NG, "sc_tm": 2 * NG, "sc_arhs": 2 * NG,
                        "sc_slot_free": NG - 1})
                passed({n: NG for n in ("pe_tm", "pe_X", "sc_X1", "pe_akv", "sc_akv", "sc_XTL", "pe_WZ", "sc_WZ", "pe_MT", "pe_Q",
                                        "pe_F", "pe_Yi", "sc_Yi", "sc_MT", "sc_Q", "sc_F", "sc_y")})

        @stage
        def rwkv_output(Y_, BN, G_, o):
            with ExitStack() as c:
                heads = const[:, 2, :]
                y, bn, g, sq, rs = (sb(f"ro_{n}", [P, T], fp32, c) for n in ("y", "bn", "g", "sq", "rs"))
                with nc.Block() as block:
                    @block.sync
                    def _(sp):
                        with sp.Fori(0, DT) as m:
                            sp.wait_ge(*after("ro_o", m))
                            sp.dma_start(y[:, :].rearrange("p (g t) -> p g t", g=4),
                                         Y_[ds(4 * m, 4), :, :].rearrange("g p t -> p g t")).then_inc(*tick("ro_in", 16))
                            sp.dma_start(bn[:, :], BN[ds(m, 1), :, :].rearrange("a p t -> p (a t)")).then_inc(*tick("ro_in", 16))
                            sp.dma_start(g[:, :], G_[ds(m, 1), :, :].rearrange("a p t -> p (a t)")).then_inc(*tick("ro_in", 16))

                    @block.tensor
                    def _(pe):
                        with pe.Fori(0, DT) as m:
                            pe.wait_ge(*after("ro_in", 48 * m + 48))
                            for h in range(2):
                                mm = pe.matmul(ps[0][:, h, :], heads, y[:, h * HALF:(h + 1) * HALF], start=True, stop=True)
                            mm.then_inc(*tick("ro_sum"))
                            pe.wait_ge(*after("ro_sq", m + 1))
                            for h in range(2):
                                mm = pe.matmul(ps[1][:, h, :], heads, sq[:, h * HALF:(h + 1) * HALF], start=True, stop=True)
                            mm.then_inc(*tick("ro_var"))

                    @block.scalar
                    def _(act):
                        with act.Fori(0, DT) as m:
                            act.wait_ge(*after("ro_yc", m + 1))
                            act.activation(sq[:, :], y[:, :], ACT.Square).then_inc(*tick("ro_sq"))
                            act.wait_ge(*after("ro_var", m + 1))
                            act.wait_ge(*after("ro_o", m))
                            act.activation(rs[:, :], flat[1], ACT.Sqrt, scale=1.0 / HEAD, bias=eps[:, 1:2]).then_inc(*tick("ro_root"))

                    @block.vector
                    def _(dve):
                        with dve.Fori(0, DT) as m:
                            dve.wait_ge(*after("ro_sum", m + 1))
                            dve.scalar_tensor_tensor(out=y[:, :], in0=flat[0], scalar=-1.0 / HEAD, in1=y[:, :],
                                                     op0=ALU.mult, op1=ALU.add).then_inc(*tick("ro_yc"))
                            dve.wait_ge(*after("ro_root", m + 1))
                            dve.reciprocal(rs[:, :], rs[:, :]).then_inc(*tick("ro_v"))
                            dve.wait_ge(*after("ro_v", 4 * m + 1))
                            dve.tensor_tensor(y[:, :], y[:, :], rs[:, :], ALU.mult).then_inc(*tick("ro_v"))
                            dve.wait_ge(*after("ro_v", 4 * m + 2))
                            dve.tensor_scalar(y[:, :], y[:, :], pcol("rw_ln_w", m), pcol("rw_ln_b", m), ALU.mult, ALU.add)\
                               .then_inc(*tick("ro_v"))
                            dve.wait_ge(*after("ro_v", 4 * m + 3))
                            dve.tensor_tensor(y[:, :], y[:, :], bn[:, :], ALU.add).then_inc(*tick("ro_v"))
                            dve.wait_ge(*after("ro_v", 4 * m + 4))
                            dve.tensor_tensor(o[:, ds(m, 1), :], one(y[:, :]), one(g[:, :]), ALU.mult).then_inc(*tick("ro_o"))
                passed({"ro_in": 48 * DT, "ro_v": 4 * DT})
                passed({n: DT for n in ("ro_sum", "ro_yc", "ro_sq", "ro_var", "ro_root", "ro_o")})

        def final_norm():
            with ExitStack() as c:
                norm(H, "norm_final", None, None, c, keep=H, tag="fin")

        SQ = SSM_G // 2
        SU = SSM_G * SSM_H // P

        @stage
        def hybrid():
            rows = lambda t: (lambda m: t[ds(m, 1), :, :].rearrange("a p t -> p (a t)"))
            ZC, GC, GS, CC = (dram(f"hyd_{n}", [DT, P, T]) for n in ("zc", "gc", "gs", "cc"))
            U_, ZS = (dram(f"hyd_{n}", [SU, P, T]) for n in ("u", "zs"))
            w = A["hybrid_in"]
            with ExitStack() as c:
                xh = sb("hy_xh", [P, DT, T], r32, c)
                xl = sb("hy_xl", [P, DT, T], r32, c)
                stage = sb("hy_stage", [P, 2, T], fp32, c)
                with ExitStack() as c2:
                    norm(H, "pre_norm2", xh, xl, c2, tag="y")
                LEAD = TAPS - 1
                cu = sb("hy_cu", [P, DT, LEAD + T], fp32, c)
                cc = sb("hy_cc", [P, DT, T], fp32, c)

                def scalar(act, s, i, last):
                    if s == 0:
                        act.wait_ge(ps_free[1].sem, ps_free[1].at(i))
                        act.activation(stage[:, 0, :], flat[0], ACT.Sigmoid).then_inc(ps_free[0].sem, 1)

                def vector(dve, s, i, last):
                    if s == 1:
                        dve.wait_ge(ps_free[0].sem, ps_free[0].at(i + 1))
                        dve.tensor_tensor(cu[:, ds(i, 1), LEAD:LEAD + T], ps_tile(1), stage[:, 0:1, :], ALU.mult)\
                           .then_inc(ps_free[1].sem, 1)
                        if last:
                            dve.memset(cu[:, :, 0:LEAD], 0.0).then_inc(*tick("cu_lead"))
                            dve.wait_ge(*after("cu_lead", 1))
                project(DT, [(w, lambda i: DT + i, DT, xh, xl), (w, lambda i: i, DT, xh, xl)], scalar, vector,
                        own=(("cu_lead", 1),))

                def conv(first):
                    def program(dve):
                        for j in range(TAPS):
                            for z in range(2):
                                k = first + z
                                n = 2 * j + z
                                if j == 0:
                                    op = dve.tensor_scalar(cc[:, k, :], cu[:, k, 0:T], pcol("conv_w2", k),
                                                           pcol("conv_b2", k), ALU.mult, ALU.add)
                                else:
                                    dve.wait_ge(*after("taps", n - 1))
                                    op = dve.scalar_tensor_tensor(out=cc[:, k, :], in0=cu[:, k, j:j + T],
                                                                  scalar=pcol("conv_w2", j * DT + k), in1=cc[:, k, :],
                                                                  op0=ALU.mult, op1=ALU.add)
                                op.then_inc(*tick("taps"))
                    return program

                def out_strips(dsts, funcs):
                    def scalar(act, s, i, last):
                        name = f"strip_out_{'AB'[s]}"
                        act.wait_ge(*after(name, 16 * i))
                        act.activation(stage[:, s, :], flat[s], funcs[s]).then_inc(ps_free[s].sem, 1)
                        act.wait_ge(ps_free[s].sem, ps_free[s].at(i + 1))
                        act.dma_start(dsts[s](i), stage[:, s, :]).then_inc(*tick(name, 16))
                        if last:
                            act.wait_ge(*after(name, 16 * (i + 1)))
                    return scalar
                own = (("strip_out_A", 64), ("strip_out_B", 64), ("taps", 2 * TAPS))

                def wide(t, at, func, first):
                    project(4, [(w, lambda i, s=s: at + 2 * i + s, DT, xh, xl) for s in range(2)],
                            out_strips([lambda i, s=s: rows(t)(2 * i + s) for s in range(2)], (func, func)),
                            own=own, vector_alone=conv(first))
                wide(ZC, 16, ACT.Silu, 0)
                project(4, [(w, lambda i: 24 + i, DT, xh, xl), (w, lambda i: 28 + i, DT, xh, xl)],
                        out_strips((rows(U_), rows(ZS)), (ACT.Copy, ACT.Silu)), own=own, vector_alone=conv(2))
                wide(GC, 32, ACT.Sigmoid, 4)
                wide(GS, 40, ACT.Sigmoid, 6)
                with nc.Block() as block:
                    @block.sync
                    def _(sp):
                        sp.dma_start(CC.rearrange("k p t -> p k t"), cc[:, :, :]).then_inc(*tick("cc_out", 16))
                        sp.wait_ge(*after("cc_out", 16))
                passed({"cc_out": 16})

            with ExitStack() as c:
                y = sb("ssm_y", [P, SU, T], fp32, c)
                ssm(U_, y)
                merged = sb("merged", [P, DT, T], fp32, c)
                ssm_out(y, ZS, GS, merged)
                conv_out(CC, ZC, GC, merged)
                c2 = ExitStack()
                xh = sb("wo_xh", [P, DT, T], r32, c2)
                xl = sb("wo_xl", [P, DT, T], r32, c2)
                split_operand(None, merged, xh, xl)

                def keep(act, s, i, last):
                    act.activation(merged[:, ds(2 * i + s, 1), :], ps_tile(s), ACT.Copy).then_inc(ps_free[s].sem, 1)
                project(DT // 2, [(A["w_out2"], lambda i, s=s: 2 * i + s, DT, xh, xl) for s in range(2)], keep)
                c2.close()
                norm(merged, "post_norm2", None, None, c, keep=merged, tag="post")
                with nc.Block() as block:
                    @block.vector
                    def _(dve):
                        for k in range(DT):
                            dve.tensor_tensor(H[:, k, :], H[:, k, :], merged[:, k, :], ALU.add).then_inc(*tick("last_add"))
                        dve.wait_ge(*after("last_add", DT))
                passed({"last_add": DT})

        @stage
        def gated_product(w, kt, xh, xl, G_, merged, add, room):
            g, t = room[:, 0:2, :], room[:, 2:4, :]

            def scalar(act, s, i, last):
                if not last:
                    act.wait_ge(ps_free[s].sem, ps_free[s].at(i + 1))
                    act.dma_start(g[:, s, :], G_[ds(2 * i + 2 + s, 1), :, :].rearrange("a p t -> p (a t)"))\
                       .then_inc(*tick(f"gp_in_{'AB'[s]}", 16))

            def vector(dve, s, i, last):
                dve.wait_ge(*after(f"gp_in_{'AB'[s]}", 16 * (i + 1)))
                m = ds(2 * i + s, 1)
                if add:
                    dve.tensor_tensor(t[:, s, :], flat[s], g[:, s, :], ALU.mult).then_inc(ps_free[s].sem, 1)
                    dve.wait_ge(ps_free[s].sem, ps_free[s].at(i + 1))
                    dve.tensor_tensor(merged[:, m, :], t[:, s:s + 1, :], merged[:, m, :], ALU.add)\
                       .then_inc(*tick("gp_added"))
                else:
                    dve.tensor_tensor(merged[:, m, :], ps_tile(s), g[:, s:s + 1, :], ALU.mult)\
                       .then_inc(ps_free[s].sem, 1)

            def first_gates(act):
                for s in range(2):
                    act.dma_start(g[:, s, :], G_[s, :, :]).then_inc(*tick(f"gp_in_{'AB'[s]}", 16))
            project(DT // 2, [(w, lambda i, s=s: 2 * i + s, kt, xh, xl) for s in range(2)], scalar, vector,
                    scalar_first=first_gates,
                    own=(("gp_added", 8 if add else 0), ("gp_in_A", 64), ("gp_in_B", 64)))

        @stage
        def ssm_out(y, ZS, GS, merged):
            with ExitStack() as c:
                xh = sb("glu_xh", [P, SU, T], r32, c)
                xl = sb("glu_xl", [P, SU, T], r32, c)
                zs = sb("glu_zs", [P, SU, T], fp32, c)
                gate = sb("glu_gate", [P, SU, T], fp32, c)
                split_operand(None, y, xh, xl)

                def scalar(act, s, i, last):
                    m = 2 * i + s
                    act.activation(gate[:, ds(m, 1), :], ps_tile(s), ACT.Sigmoid, bias=pcol("b_glu2", m))\
                       .then_inc(ps_free[s].sem, 1)
                project(SU // 2, [(A["w_glu2"], lambda i, s=s: 2 * i + s, SU, xh, xl) for s in range(2)], scalar)
                with nc.Block() as block:
                    @block.sync
                    def _(sp):
                        sp.dma_start(zs[:, :, :], ZS.rearrange("k p t -> p k t")).then_inc(*tick("zs_in", 16))

                    @block.vector
                    def _(dve):
                        for k in range(SU):
                            dve.tensor_tensor(y[:, k, :], y[:, k, :], gate[:, k, :], ALU.mult).then_inc(*tick("glu_y"))
                        dve.wait_ge(*after("zs_in", 16))
                        for k in range(SU):
                            dve.wait_ge(*after("glu_y", k + 1))
                            dve.tensor_tensor(y[:, k, :], y[:, k, :], zs[:, k, :], ALU.mult).then_inc(*tick("glu_z"))
                        dve.wait_ge(*after("glu_z", SU))
                passed({"zs_in": 16, "glu_y": SU, "glu_z": SU})
                split_operand(None, y, xh, xl)
                gated_product(A["w_ssm_out2"], SU, xh, xl, GS, merged, False, gate)

        @stage
        def conv_out(CC, ZC, GC, merged):
            with ExitStack() as c:
                cc = sb("ln_cc", [P, DT, T], fp32, c)
                with ExitStack() as c2:
                    sq = sb("ln_sq", [P, 2, T], fp32, c2)
                    rs = sb("ln_rs", [P, T], fp32, c2)
                    zc = sb("ln_zc", [P, DT, T], fp32, c2)
                    with nc.Block() as block:
                        @block.sync
                        def _(sp):
                            sp.dma_start(cc[:, :, :], CC.rearrange("k p t -> p k t")).then_inc(*tick("ln_in", 16))
                            sp.dma_start(zc[:, :, :], ZC.rearrange("k p t -> p k t")).then_inc(*tick("ln_z_in", 16))

                        @block.tensor
                        def _(pe):
                            pe.wait_ge(*after("ln_in", 16))
                            for k in range(DT):
                                for h in range(2):
                                    mm = pe.matmul(ps[2][:, h, :], mean, cc[:, k, h * HALF:(h + 1) * HALF],
                                                   start=(k == 0), stop=(k == DT - 1))
                            mm.then_inc(*tick("ln_mean"))
                            for k in range(DT):
                                pe.wait_ge(*after("ln_sq", k + 1))
                                for h in range(2):
                                    mm = pe.matmul(ps[3][:, h, :], mean, sq[:, k % 2, h * HALF:(h + 1) * HALF],
                                                   start=(k == 0), stop=(k == DT - 1))
                                mm.then_inc(*tick("ln_var"))

                        @block.vector
                        def _(dve):
                            dve.wait_ge(*after("ln_in", 16))
                            dve.wait_ge(*after("ln_mean", 1))
                            for k in range(DT):
                                dve.tensor_tensor(cc[:, k, :], cc[:, k, :], flat[2], ALU.subtract).then_inc(*tick("ln_c"))
                            dve.wait_ge(*after("ln_root", 1))
                            dve.reciprocal(rs[:, :], rs[:, :]).then_inc(*tick("ln_inv"))
                            dve.wait_ge(*after("ln_inv", 1))
                            for k in range(DT):
                                dve.wait_ge(*after("ln_c", k + 1))
                                dve.scalar_tensor_tensor(out=cc[:, k, :], in0=cc[:, k, :], scalar=pcol("ln_g2", k),
                                                         in1=rs[:, :], op0=ALU.mult, op1=ALU.mult).then_inc(*tick("ln_n"))
                            dve.wait_ge(*after("ln_z_in", 16))
                            for k in range(DT):
                                dve.wait_ge(*after("ln_act", k + 1))
                                dve.tensor_tensor(cc[:, k, :], cc[:, k, :], zc[:, k, :], ALU.mult).then_inc(*tick("ln_y"))
                            dve.wait_ge(*after("ln_y", DT))

                        @block.scalar
                        def _(act):
                            for k in range(DT):
                                act.wait_ge(*after("ln_c", k + 1))
                                if k >= 2:
                                    act.wait_ge(*after("ln_var", k - 1))
                                act.activation(sq[:, k % 2, :], cc[:, k, :], ACT.Square).then_inc(*tick("ln_sq"))
                            act.wait_ge(*after("ln_var", DT))
                            act.activation(rs[:, :], flat[3], ACT.Sqrt, bias=eps[:, 2:3]).then_inc(*tick("ln_root"))
                            for k in range(DT):
                                act.wait_ge(*after("ln_n", k + 1))
                                act.activation(cc[:, k, :], cc[:, k, :], ACT.Silu, bias=pcol("ln_b2", k)).then_inc(*tick("ln_act"))
                    passed({n: DT for n in ("ln_c", "ln_n", "ln_y", "ln_sq", "ln_var", "ln_act")})
                    passed({"ln_in": 16, "ln_z_in": 16, "ln_mean": 1, "ln_root": 1, "ln_inv": 1})
                xh = sb("co_xh", [P, DT, T], r32, c)
                xl = sb("co_xl", [P, DT, T], r32, c)
                split_operand(None, cc, xh, xl)
                gated_product(A["w_conv_out2"], DT, xh, xl, GC, merged, True, cc)

        @stage
        def ssm(U_, y):
            HS = SC * SSM_H
            with ExitStack() as c:
                toep = sb("ssm_toep", [P, SSM_G, HS], fp32, c)
                bt = sb("ssm_bt", [P, 2, SQ, P], fp32, c)
                cz = sb("ssm_cz", [P, 2, SSM_G, (SC + 1) * SSM_H], fp32, c)
                rot = sb("ssm_rot", [P, 2, SQ, SN], fp32, c)
                decay8 = sb("ssm_decay8", [P, SQ], fp32, c)
                ssm_prepare(toep, bt, cz, rot, decay8, y)
                ut = sb("ssm_ut", [P, SSM_G, SN], fp32, c)
                with ExitStack() as c2:
                    u = sb("ssm_u", [P, SU, T], fp32, c2)
                    uc = sb("ssm_uc", [P, SSM_G, SC, SSM_H], fp32, c2)
                    with nc.Block() as block:
                        @block.sync
                        def _(sp):
                            sp.dma_start(u[:, :, :], U_.rearrange("k p t -> p k t")).then_inc(*tick("su_in", 16))

                        @block.tensor
                        def _(pe):
                            pe.wait_ge(*after("su_in", 16))
                            n = 0
                            for tt in range(SU):
                                for jh in range(2):
                                    if n >= 4:
                                        pe.wait_ge(*after("su_c", n - 3))
                                    for j in range(4):
                                        mm = pe.transpose(ps[n % 4][:, 0, j * P:(j + 1) * P], u[:, tt, 4 * jh + j:T:SC], ident)
                                    mm.then_inc(*tick("pe_uc"))
                                    n += 1
                            for g4 in range(SSM_G // 4):
                                pe.wait_ge(*after("su_c", 8))
                                if g4 >= 4:
                                    pe.wait_ge(*after("su_t", g4 - 3))
                                for g in range(4):
                                    mm = pe.transpose(ps[g4 % 4][:, 1, g * P:(g + 1) * P],
                                                      uc[:, 4 * g4 + g, :, :].rearrange("p j h -> p (j h)"), ident)
                                mm.then_inc(*tick("pe_ut"))

                        @block.vector
                        def _(dve):
                            n = 0
                            for tt in range(SU):
                                for jh in range(2):
                                    dve.wait_ge(*after("pe_uc", n + 1))
                                    dve.tensor_copy(uc[:, 8 * tt:8 * tt + 8, 4 * jh:4 * jh + 4, :].rearrange("p g j h -> p j g h"),
                                                    ps[n % 4][:, 0, :].rearrange("p (j g h) -> p j g h", j=4, g=8))\
                                       .then_inc(*tick("su_c"))
                                    n += 1
                            for g4 in range(SSM_G // 4):
                                dve.wait_ge(*after("pe_ut", g4 + 1))
                                dve.tensor_copy(ut[:, 4 * g4:4 * g4 + 4, :].rearrange("p g c -> p (g c)"), ps[g4 % 4][:, 1, :])\
                                   .then_inc(*tick("su_t"))
                            dve.wait_ge(*after("su_t", 8))
                    passed({"su_in": 16, "pe_uc": 8, "su_c": 8, "pe_ut": 8, "su_t": 8})

                with ExitStack() as c2:
                    b = sb("ssm_b", [P, 2, SQ, SN], fp32, c2)
                    d0, t1 = (y[:, 2 * z:2 * z + 2, :].rearrange("p k t -> p (k t)").rearrange("p (q c) -> p q c", q=SQ)
                              for z in range(2))
                    ee = sb("ssm_e", [P, 2, SQ * SN + 1], fp32, c2)
                    after_c, before_c = ([ee[:, z, o:o + SQ * SN].rearrange("p (q c) -> p q c", q=SQ) for z in range(2)]
                                         for o in (1, 0))
                    cos, sin = rot[:, 0, :, :], rot[:, 1, :, :]
                    with nc.Block() as block:
                        @block.tensor
                        def _(pe):
                            n = 0
                            for z in range(2):
                                for q4 in range(SQ // 4):
                                    if n >= 4:
                                        pe.wait_ge(*after("sb_b", n - 3))
                                    for q in range(4 * q4, 4 * q4 + 4):
                                        for g in range(2):
                                            mm = pe.matmul(ps[n % 4][g * 64:(g + 1) * 64, 0, (q % 4) * SN:(q % 4 + 1) * SN],
                                                           bt[:, z, q, g * 64:(g + 1) * 64], ut[:, 2 * q + g, :],
                                                           start=True, stop=True, tile_position=(0, g * 64))
                                    mm.then_inc(*tick("pe_b"))
                                    n += 1

                        @block.scalar
                        def _(act):
                            n = 0
                            for z in range(2):
                                for q4 in range(SQ // 4):
                                    act.wait_ge(*after("pe_b", n + 1))
                                    act.activation(b[:, z, 4 * q4:4 * q4 + 4, :].rearrange("p q c -> p (q c)"), ps[n % 4][:, 0, :],
                                                   ACT.Copy).then_inc(*tick("sb_b"))
                                    n += 1

                        @block.vector
                        def _(dve):
                            ch = Chain(dve, sig("dve_chain"))
                            ch(dve.tensor_copy(d0[:, :, :], decay8[:, :].unsqueeze(2).to_broadcast([P, SQ, SN])))
                            ch(dve.memset(d0[:, :, 0:1], 0.0))

                            dve.wait_ge(*after("sb_b", 8))
                            br, bi = b[:, 0, :, :], b[:, 1, :, :]
                            er, ei = after_c
                            flat3 = lambda t: t.rearrange("p q c -> p (q c)")
                            ch(dve.tensor_tensor(t1[:, :, :], bi, sin, ALU.mult))
                            ch(dve.tensor_tensor(er, br, cos, ALU.mult))
                            ch(dve.tensor_tensor(er, er, t1[:, :, :], ALU.add))
                            ch(dve.tensor_tensor(t1[:, :, :], br, sin, ALU.mult))
                            ch(dve.tensor_tensor(ei, bi, cos, ALU.mult))
                            ch(dve.tensor_tensor(bi, ei, t1[:, :, :], ALU.subtract))
                            ch(dve.tensor_copy(br, er))
                            ch(dve.tensor_tensor_scan(out=flat3(t1[:, :, :]), data0=flat3(d0[:, :, :]), data1=flat3(br),
                                                      initial=0.0, op0=ALU.mult, op1=ALU.add))
                            ch(dve.tensor_copy(br, t1[:, :, :]))
                            ch(dve.tensor_tensor_scan(out=flat3(t1[:, :, :]), data0=flat3(d0[:, :, :]), data1=flat3(bi),
                                                      initial=0.0, op0=ALU.mult, op1=ALU.add))
                            ch(dve.tensor_tensor(er, br, cos, ALU.mult))
                            ch(dve.tensor_tensor(bi, t1[:, :, :], sin, ALU.mult))
                            ch(dve.tensor_tensor(er, er, bi, ALU.subtract))
                            ch(dve.tensor_tensor(ei, br, sin, ALU.mult))
                            ch(dve.tensor_tensor(bi, t1[:, :, :], cos, ALU.mult))
                            ch(dve.tensor_tensor(ei, ei, bi, ALU.add))
                            for z in range(2):
                                ch(dve.memset(before_c[z][:, :, 0:1], 0.0))
                            chain_n.append(ch.n)
                    passed({"pe_b": 8, "sb_b": 8, "dve_chain": chain_n.pop()})

                    yc = b[:, :, :, :].rearrange("p z q c -> p (z q c)")\
                        .rearrange("p (i g h) -> p i g h", i=SC, g=SSM_G)
                    with nc.Block() as block:
                        @block.tensor
                        def _(pe):
                            for g4 in range(SSM_G // 4):
                                if g4 >= 4:
                                    pe.wait_ge(*after("sy_c", g4 - 3))
                                for g in range(4 * g4, 4 * g4 + 4):
                                    dst = ps[g4 % 4][:, 0, (g % 4) * P:(g % 4 + 1) * P]
                                    pe.matmul(dst, ut[:, g, :], toep[:, g, :], start=True, stop=False)
                                    pe.matmul(dst, before_c[0][:, g // 2, :], cz[:, 0, g, SSM_H:], start=False, stop=False)
                                    mm = pe.matmul(dst, before_c[1][:, g // 2, :], cz[:, 1, g, SSM_H:], start=False, stop=True)
                                mm.then_inc(*tick("pe_yc"))
                            for i in range(SC):
                                pe.wait_ge(*after("sy_c", 8))
                                if i >= 4:
                                    pe.wait_ge(*after("sy_t", i - 3))
                                for tt in range(SU):
                                    mm = pe.transpose(ps[i % 4][:, 1, tt * P:(tt + 1) * P],
                                                      yc[:, i, 8 * tt:8 * tt + 8, :].rearrange("p g h -> p (g h)"), ident)
                                mm.then_inc(*tick("pe_yt"))

                        @block.vector
                        def _(dve):
                            for g4 in range(SSM_G // 4):
                                dve.wait_ge(*after("pe_yc", g4 + 1))
                                dve.tensor_copy(yc[:, :, 4 * g4:4 * g4 + 4, :].rearrange("p i g h -> p g i h"),
                                                ps[g4 % 4][:, 0, :].rearrange("p (g i h) -> p g i h", g=4, i=SC))\
                                   .then_inc(*tick("sy_c"))

                        @block.scalar
                        def _(act):
                            for i in range(SC):
                                act.wait_ge(*after("pe_yt", i + 1))
                                act.activation(y[:, :, i:T:SC], ps[i % 4][:, 1, :].rearrange("p (k c) -> p k c", k=SU),
                                               ACT.Gelu_apprx_tanh).then_inc(*tick("sy_t"))
                    passed({"pe_yc": 8, "sy_c": 8, "pe_yt": 8, "sy_t": 8})

        @stage
        def ssm_prepare(toep, bt, cz, rot, decay8, room):
            with ExitStack() as c:
                lam = sb("sp_lam", [P, 3, SQ], fp32, c)
                bc = sb("sp_bc", [P, 4, SQ, SSM_H], fp32, c)
                dd = sb("sp_d", [SSM_H, SSM_G], fp32, c)
                v = {n: sb(f"sp_{n}", [P, SQ], fp32, c) for n in
                     ("dt", "mag", "th", "n", "s", "s2", "cs", "sn", "zr", "zi", "den", "t", "t2", "pr", "pi")}
                pw = sb("sp_pw", [P, 2, SC + 1, SQ], fp32, c)
                bb = sb("sp_bb", [P, 2, SQ, SSM_H], fp32, c)
                w1 = sb("sp_w1", [P, SQ, SSM_H], fp32, c)
                w2 = sb("sp_w2", [P, SQ, SSM_H], fp32, c)
                p1 = sb("sp_p1", [P, SQ, SSM_H], fp32, c)
                p2 = sb("sp_p2", [P, SQ, SSM_H], fp32, c)
                va = sb("sp_va", [P, 2, SQ, SC, SSM_H], fp32, c)
                gd = room[0:SSM_H, :, :].rearrange("p k t -> p (k t)").rearrange("p (g n) -> p g n", g=SSM_G)
                dg = sb("sp_dg", [SSM_H, SSM_G, SSM_H], fp32, c)
                r1 = sb("sp_r1", [P, SQ, SN // 2], fp32, c)
                ch_n = {}
                INV2PI = float(np.float32(1 / (2 * np.pi)))
                C1 = 6.28125
                C2 = float(np.float32(2 * np.pi - C1) - np.float32(2 * np.pi - C1) % np.float32(2.0 ** -20))
                C3 = float(2 * np.pi - C1 - C2)
                ROUND = float(3 << 22)
                PI = 3.1415925

                def wideh(t):
                    return t.unsqueeze(2).to_broadcast([P, SQ, SSM_H])
                with nc.Block() as block:
                    @block.sync
                    def _(sp):
                        sp.dma_start(lam[:, :, :], A["ssm_lam"]).then_inc(*tick("sp_in", 16))
                        sp.dma_start(bc[:, :, :, :], A["ssm_bc"]).then_inc(*tick("sp_in", 16))
                        sp.dma_start(dd[:, :], A["ssm_d"]).then_inc(*tick("sp_in", 16))
                        sp.wait_ge(*after("sp_gd", 10))
                        sp.wait_ge(*after("sp_zero", 1))
                        for j in range(SC):
                            sp.dma_start(toep[j * SSM_H:(j + 1) * SSM_H, :, j * SSM_H:P],
                                         gd[:, :, 0:P - j * SSM_H]).then_inc(*tick("sp_toep", 16))
                        sp.wait_ge(*after("sp_toep", 16 * SC))

                    @block.scalar
                    def _(act):
                        act.wait_ge(*after("sp_in", 48))
                        act.activation(v["dt"][:, :], lam[:, 2, :], ACT.Exp).then_inc(*tick("sp_dt"))
                        act.wait_ge(*after("sp_lrdt", 1))
                        act.activation(v["mag"][:, :], v["t"][:, :], ACT.Exp).then_inc(*tick("sp_mag"))
                        act.wait_ge(*after("sp_angle", 1))
                        act.activation(v["sn"][:, :], v["th"][:, :], ACT.Sin).then_inc(*tick("sp_sin"))
                        act.activation(v["s2"][:, :], v["th"][:, :], ACT.Sin, scale=0.5).then_inc(*tick("sp_sin"))
                        for z in range(2):
                            for q4 in range(SQ // 4):
                                n = 4 * z + q4
                                act.wait_ge(*after("pe_bt", n + 1))
                                act.activation(bt[:, z, 4 * q4:4 * q4 + 4, :].rearrange("p q c -> p (q c)"), ps[n % 4][:, 0, :],
                                               ACT.Copy).then_inc(*tick("sp_bt"))

                    @block.tensor
                    def _(pe):
                        pe.wait_ge(*after("sp_va", 1))
                        for z in range(2):
                            for q4 in range(SQ // 4):
                                n = 4 * z + q4
                                if n >= 4:
                                    pe.wait_ge(*after("sp_bt", n - 3))
                                for q in range(4):
                                    mm = pe.transpose(ps[n % 4][:, 0, q * P:(q + 1) * P],
                                                      va[:, z, 4 * q4 + q, :, :].rearrange("p j h -> p (j h)"), ident)
                                mm.then_inc(*tick("pe_bt"))
                        pe.wait_ge(*after("sp_cz", 2))
                        for g4 in range(SSM_G // 4):
                            if g4 >= 4:
                                pe.wait_ge(*after("sp_gd", g4 - 3))
                            for g in range(4 * g4, 4 * g4 + 4):
                                dst = ps[g4 % 4][0:SSM_H, 1, (g % 4) * P:(g % 4 + 1) * P]
                                pe.matmul(dst, bb[:, 0, g // 2, :], cz[:, 0, g, 0:P], start=True, stop=False)
                                mm = pe.matmul(dst, bb[:, 1, g // 2, :], cz[:, 1, g, 0:P], start=False, stop=True)
                            mm.then_inc(*tick("pe_gd"))

                    @block.gpsimd
                    def _(pl):
                        ch = Chain(pl, sig("pool_chain"))
                        ch(pl.memset(toep[:, :, :], 0.0))
                        pl.memset(cz[:, :, :, :], 0.0).then_inc(*tick("sp_zero"))
                        pl.wait_ge(*after("sp_zero", 1))
                        pl.wait_ge(*after("sp_pw", 1))
                        cr, ci = bc[:, 2, :, :], bc[:, 3, :, :]
                        for k in range(SC + 1):
                            pr, pi = wideh(pw[:, 0, k, :]), wideh(pw[:, 1, k, :])
                            for z, (a, b, op) in enumerate(((cr, ci, ALU.subtract), (ci, cr, ALU.add))):
                                ch(pl.tensor_tensor(p1[:, :, :], a, pr, ALU.mult))
                                ch(pl.tensor_tensor(p2[:, :, :], b, pi, ALU.mult))
                                if z == 1:
                                    ch(pl.tensor_tensor(p1[:, :, :], p1[:, :, :], p2[:, :, :], ALU.add))
                                    ch(pl.tensor_scalar(p1[:, :, :], p1[:, :, :], -1.0, None, ALU.mult))
                                for g in range(2):
                                    rows = slice(64 * g, 64 * g + 64)
                                    dst = cz[rows, z, g:SSM_G:2, k * SSM_H:(k + 1) * SSM_H]
                                    if z == 0:
                                        ch(pl.tensor_tensor(dst, p1[rows, :, :], p2[rows, :, :], ALU.subtract))
                                    else:
                                        ch(pl.tensor_copy(dst, p1[rows, :, :]))
                        pl.engine_nop().then_inc(*tick("sp_cz", 1))
                        pl.engine_nop().then_inc(*tick("sp_cz", 1))
                        ch_n["pool"] = ch.n

                    @block.vector
                    def _(dve):
                        ch = Chain(dve, sig("dve_chain"))
                        V = {n: t[:, :] for n, t in v.items()}
                        lr, li = lam[:, 0, :], lam[:, 1, :]

                        def mul(o, a, b):
                            ch(dve.tensor_tensor(o, a, b, ALU.mult))

                        def add(o, a, b):
                            ch(dve.tensor_tensor(o, a, b, ALU.add))

                        def sub(o, a, b):
                            ch(dve.tensor_tensor(o, a, b, ALU.subtract))

                        def cmul(orr, oi, ar, ai, br, bi, t1, t2):
                            mul(t1, ai, bi)
                            mul(orr, ar, br)
                            sub(orr, orr, t1)
                            mul(t2, ai, br)
                            mul(oi, ar, bi)
                            add(oi, oi, t2)

                        dve.wait_ge(*after("sp_in", 48))
                        dve.wait_ge(*after("sp_dt", 1))
                        dve.tensor_tensor(V["t"], lr, V["dt"], ALU.mult).then_inc(*tick("sp_lrdt"))
                        mul(V["th"], li, V["dt"])
                        ch(dve.tensor_scalar(V["n"], V["th"], INV2PI, ROUND, ALU.mult, ALU.add))
                        ch(dve.tensor_scalar(V["n"], V["n"], -ROUND, None, ALU.add))
                        for part in (C1, C2, C3):
                            ch(dve.scalar_tensor_tensor(out=V["th"], in0=V["n"], scalar=-part, in1=V["th"],
                                                        op0=ALU.mult, op1=ALU.add))
                        dve.tensor_scalar(V["th"], V["th"], PI, -PI, ALU.min, ALU.max).then_inc(*tick("sp_angle"))
                        mul(V["den"], lr, lr)
                        mul(V["t2"], li, li)
                        add(V["den"], V["den"], V["t2"])
                        ch(dve.reciprocal(V["den"], V["den"]))
                        dve.wait_ge(*after("sp_sin", 2))
                        dve.wait_ge(*after("sp_mag", 1))
                        mul(V["cs"], V["s2"], V["s2"])
                        ch(dve.tensor_scalar(V["cs"], V["cs"], -2.0, 1.0, ALU.mult, ALU.add))
                        ch(dve.memset(pw[:, 0, 0, :], 1.0))
                        ch(dve.memset(pw[:, 1, 0, :], 0.0))
                        mul(pw[:, 0, 1, :], V["mag"], V["cs"])
                        mul(pw[:, 1, 1, :], V["mag"], V["sn"])
                        for k in range(2, SC + 1):
                            h = k // 2
                            cmul(pw[:, 0, k, :], pw[:, 1, k, :], pw[:, 0, h, :], pw[:, 1, h, :],
                                 pw[:, 0, k - h, :], pw[:, 1, k - h, :], V["t"], V["t2"])
                        ch(dve.engine_nop())
                        dve.engine_nop().then_inc(*tick("sp_pw"))
                        ch(dve.tensor_scalar(V["n"], pw[:, 0, 1, :], -1.0, None, ALU.add))
                        mul(V["zr"], V["n"], lr)
                        mul(V["t"], pw[:, 1, 1, :], li)
                        add(V["zr"], V["zr"], V["t"])
                        mul(V["zr"], V["zr"], V["den"])
                        mul(V["zi"], pw[:, 1, 1, :], lr)
                        mul(V["t"], V["n"], li)
                        sub(V["zi"], V["zi"], V["t"])
                        mul(V["zi"], V["zi"], V["den"])
                        cmul(bb[:, 0, :, :], bb[:, 1, :, :], wideh(V["zr"]), wideh(V["zi"]), bc[:, 0, :, :], bc[:, 1, :, :],
                             w1[:, :, :], w2[:, :, :])
                        for j in range(SC):
                            k = SC - 1 - j
                            cmul(va[:, 0, :, j, :], va[:, 1, :, j, :], wideh(pw[:, 0, k, :]), wideh(pw[:, 1, k, :]),
                                 bb[:, 0, :, :], bb[:, 1, :, :], w1[:, :, :], w2[:, :, :])
                        dve.engine_nop().then_inc(*tick("sp_va"))
                        mul(V["t"], V["mag"], V["mag"])
                        mul(V["t2"], V["t"], V["t"])
                        ch(dve.tensor_tensor(decay8[:, :], V["t2"], V["t2"], ALU.mult))
                        ch(dve.memset(rot[:, 0, :, 0:1], 1.0))
                        ch(dve.memset(rot[:, 1, :, 0:1], 0.0))
                        cur, nxt = (V["cs"], V["sn"]), (V["pr"], V["pi"])
                        for step in range(3 + 7):
                            if step >= 3:
                                m = 1 << (step - 3)
                                wd = lambda t: t.unsqueeze(2).to_broadcast([P, SQ, m])
                                r = r1[:, :, 0:m]
                                a_r, a_i = rot[:, 0, :, 0:m], rot[:, 1, :, 0:m]
                                o_r, o_i = rot[:, 0, :, m:2 * m], rot[:, 1, :, m:2 * m]
                                mul(r, a_i, wd(cur[1]))
                                mul(o_r, a_r, wd(cur[0]))
                                sub(o_r, o_r, r)
                                mul(r, a_i, wd(cur[0]))
                                mul(o_i, a_r, wd(cur[1]))
                                add(o_i, o_i, r)
                            cmul(nxt[0], nxt[1], cur[0], cur[1], cur[0], cur[1], V["t"], V["t2"])
                            cur, nxt = nxt, cur
                        for g4 in range(SSM_G // 4):
                            dve.wait_ge(*after("pe_gd", g4 + 1))
                            dve.tensor_copy(gd[:, 4 * g4:4 * g4 + 4, :].rearrange("p g n -> p (g n)"), ps[g4 % 4][0:SSM_H, 1, :])\
                               .then_inc(*tick("sp_gd"))
                        dve.tensor_tensor(dg[:, :, :], const[0:SSM_H, 0, 0:SSM_H].unsqueeze(1).to_broadcast([SSM_H, SSM_G, SSM_H]),
                                          dd[:, :].unsqueeze(2).to_broadcast([SSM_H, SSM_G, SSM_H]), ALU.mult)\
                           .then_inc(*tick("sp_gd"))
                        dve.wait_ge(*after("sp_gd", 9))
                        dve.tensor_tensor(gd[:, :, 0:SSM_H], gd[:, :, 0:SSM_H], dg[:, :, :], ALU.add).then_inc(*tick("sp_gd"))
                        ch_n["dve"] = ch.n
                passed({"sp_in": 48, "sp_dt": 1, "sp_lrdt": 1, "sp_mag": 1, "sp_angle": 1, "sp_sin": 2, "pe_bt": 8, "sp_bt": 8,
                        "sp_va": 1, "sp_cz": 2, "sp_gd": 10, "pe_gd": 8, "sp_zero": 1, "sp_pw": 1, "sp_toep": 16 * SC,
                        "dve_chain": ch_n["dve"], "pool_chain": ch_n["pool"]})

        chain_n = []
        stages = [("hawk", hawk), ("ffn0", lambda: ffn(0)), ("ple0", lambda: ple(0)), ("rwkv", rwkv),
                  ("ffn1", lambda: ffn(1)), ("ple1", lambda: ple(1)), ("final", final_norm), ("out", hybrid)]
        running = start is None
        for name, run in stages:
            if running:
                run()
            if name == stop:
                break
            running = running or name == start

        stored = sig("stored")
        with nc.Block() as block:
            @block.sync
            def _(sp):
                sp.dma_start(out, H[:, :, :]).then_inc(stored.sem, 16)
                sp.wait_ge(stored.sem, stored.at(16))

def strips(w):
    k, m = w.shape
    return np.ascontiguousarray(w.reshape(k // P, P, m // P, P).transpose(2, 1, 0, 3)).reshape(m // P, P, k)

def padded(w, rows, cols):
    out = np.zeros((rows, cols), w.dtype)
    out[:w.shape[0], :w.shape[1]] = w
    return out

def square_constants():
    c = np.zeros((len(CONSTS), P, P), np.float32)
    i, j = np.meshgrid(np.arange(P), np.arange(P), indexing="ij")
    same = i // CHUNK == j // CHUNK
    c[CIX["ident"]] = i == j
    c[CIX["mean"]] = 1.0 / D
    c[CIX["heads"]] = i // HEAD == j // HEAD
    c[CIX["mask_a"]] = same & (i < j)
    c[CIX["mask_r"]] = same & (i <= j)
    for s in (1, 2, 4, 8, 16, 32):
        c[CIX[f"level{s}"]] = (i // (2 * s) == j // (2 * s)) & (i % (2 * s) < s) & (j % (2 * s) >= s)
    return np.ascontiguousarray(c.transpose(1, 0, 2))

def laid_out(v):
    a = {}
    a["xT"] = np.ascontiguousarray(v["x"][0].T.reshape(DT, P, T).transpose(1, 0, 2))
    a["pT"] = np.ascontiguousarray(v["p"][:, 0].transpose(0, 2, 1).reshape(2, PLE_T, P, T).transpose(0, 2, 1, 3))
    cols = [v["norm_mix"][0], v["norm_mix"][1], v["norm_ffn"][0], v["norm_ffn"][1], v["norm_ple"][0],
            v["norm_ple"][1], v["norm_final"], v["lru_b_in"], v["lru_conv_w"], v["lru_conv_b"],
            v["lru_b_gate_a"], v["lru_b_gate_x"], v["lru_lambda"], v["lru_b_out"],
            v["rw_mu"], v["rw_w0"], v["rw_a0"], v["rw_k_k"], v["rw_k_a"], v["rw_r_k"], v["rw_ln_w"], v["rw_ln_b"],
            v["pre_norm_gain_2"], v["conv_w_2"], v["conv_b_2"], v["conv_ln_gain_2"], v["conv_ln_bias_2"],
            v["b_ssm_glu_2"], v["post_norm_gain_2"], v["ssm_d_2"]]
    a["params"] = np.ascontiguousarray(np.concatenate([c.reshape(-1, P) for c in cols]).T)
    a["consts"] = square_constants()
    a["scan_ident"] = np.tile(np.eye(HEAD, dtype=np.float32), (2, 1))
    a["scan_flags"] = np.tile((np.arange(4 * DT) % 4 != 0).astype(np.float32), (P, 1))
    a["rkv"] = np.concatenate([strips(v["rw_w_rkv"][0][n]) for n in range(3)])
    a["rw_o"] = strips(v["rw_w_o"][0])
    for n, cols in (("w", P), ("a", P), ("g", 2 * P)):
        a[f"rw_{n}1"] = strips(padded(v[f"rw_{n}1"][0], D, cols))
        a[f"rw_{n}2"] = strips(padded(v[f"rw_{n}2"][0], cols, D))
    a["hybrid_in"] = strips(v["w_in_2"][0])
    a["w_conv_out2"] = strips(v["w_conv_out_2"][0])
    a["w_glu2"] = strips(v["w_ssm_glu_2"][0])
    a["w_ssm_out2"] = strips(v["w_ssm_out_2"][0])
    a["w_out2"] = strips(v["w_out_2"][0])
    dt = np.repeat(v["ssm_log_dt_2"][0][:, None], SSM_P, 1)
    a["ssm_lam"] = np.stack([t.reshape(SSM_G // 2, P).T for t in (v["ssm_lambda_re_2"][0], v["ssm_lambda_im_2"][0], dt)], 1)
    a["ssm_bc"] = np.stack([t.reshape(SSM_G // 2, P, SSM_H).transpose(1, 0, 2) for t in
                            (v["ssm_b_re_2"][0], v["ssm_b_im_2"][0], v["ssm_c_re_2"][0].transpose(0, 2, 1),
                             v["ssm_c_im_2"][0].transpose(0, 2, 1))], 1)
    a["ssm_d"] = v["ssm_d_2"][0].T
    a["hawk_in"] = strips(v["lru_w_in"][0])
    a["gate_a"] = v["lru_w_gate_a"][0]
    a["gate_x"] = v["lru_w_gate_x"][0]
    a["hawk_out"] = strips(v["lru_w_out"][0])
    for l in range(2):
        a[f"ffn_in{l}"] = strips(v["ffn_w_in"][l])
        a[f"ffn_out{l}"] = strips(v["ffn_w_out"][l])
        a[f"ple_proj{l}"] = strips(v["ple_w_proj"][l])
        a[f"ple_gate{l}"] = strips(v["ple_w_gate"][l])
    return a

def kernel(**inputs):
    import concourse.bacc as bacc
    from concourse.bass_utils import run_bass_kernel_spmd

    nc = bacc.Bacc("TRN2", target_bir_lowering=False, num_devices=1)
    arrays, aps = {}, {}
    for name, a in laid_out(inputs).items():
        arrays[f"{name}_dram"] = np.ascontiguousarray(a)
        aps[name] = nc.dram_tensor(f"{name}_dram", a.shape, mybir.dt.from_np(a.dtype), kind="ExternalInput").ap()
    out = nc.dram_tensor("out_dram", (P, DT, T), mybir.dt.float32, kind="ExternalOutput").ap()
    build(nc, aps, out)
    got = run_bass_kernel_spmd(nc, [arrays], core_ids=[0]).results[0]["out_dram"]
    return np.ascontiguousarray(got.transpose(1, 0, 2).reshape(D, T).T).reshape(1, T, D)
```

```python
import numpy as np
import concourse.bass as bass
from concourse import mybir
from contextlib import ExitStack

P = 128
T = 1024
HALF = 512
D = 1024
DT = D // P
RNN = 1280
RT = RNN // P
FF = 2816
FT = FF // P
FF_GROUPS = (8, 8, 6)
PLE_T = 2
SEMAPHORES = 120
KMAX = 8
RMS_EPS = 1e-6
GN_EPS = 64e-5
LN_EPS = 1e-5
CHUNK = 64
HEAD = 64
TAPS = 31
SSM_G, SSM_P, SSM_H = 32, 64, 16
SC = 8
SN = T // SC

PARAMS = [
    ("norm_mix0", 8), ("norm_mix1", 8), ("norm_ffn0", 8), ("norm_ffn1", 8), ("norm_ple0", 8),
    ("norm_ple1", 8), ("norm_final", 8), ("lru_b_in", 20), ("conv_w", 40), ("conv_b", 10),
    ("b_gate_a", 10), ("b_gate_x", 10), ("lru_lambda", 10), ("lru_b_out", 8),
    ("rw_mu", 48), ("rw_w0", 8), ("rw_a0", 8), ("rw_k_k", 8), ("rw_k_a", 8), ("rw_r_k", 8),
    ("rw_ln_w", 8), ("rw_ln_b", 8),
    ("pre_norm2", 8), ("conv_w2", TAPS * 8), ("conv_b2", 8), ("ln_g2", 8), ("ln_b2", 8),
    ("b_glu2", 4), ("post_norm2", 8), ("ssm_d2", 4),
]
COL, _at = {}, 0
for _name, _n in PARAMS:
    COL[_name] = _at
    _at += _n
NPARAM = _at

CONSTS = ["ident", "mean", "heads", "mask_a", "mask_r"] + [f"level{s}" for s in (1, 2, 4, 8, 16, 32)]
CIX = {n: i for i, n in enumerate(CONSTS)}

class Signal:

    def __init__(self, name, sem, base):
        self.name, self.sem, self.base = name, sem, base

    def at(self, n):
        return self.base + n

    def passed(self, n):
        self.base += n

class Feed:
    ready = None

    def scalar_before(self, act):
        pass

    def scalar(self, act):
        pass

    def vector(self, dve):
        pass

    def pool(self, pl):
        pass

    def tensor(self, pe):
        pass

    def passed(self):
        pass


class Chain:

    def __init__(self, eng, done, start=0):
        self.eng, self.done, self.start, self.n = eng, done, start, 0

    def __call__(self, inst):
        self.n += 1
        inst.then_inc(self.done.sem, 1)
        self.eng.wait_ge(self.done.sem, self.done.at(self.start + self.n))

def build(nc, A, out, stop=None, start=None):
    fp32, r32 = mybir.dt.float32, mybir.dt.float32r
    ALU, ACT = mybir.AluOpType, mybir.ActivationFunctionType
    ds = bass.ds
    ctx = ExitStack()
    with ctx:
        def sb(name, shape, dt=fp32, c=ctx):
            return c.enter_context(nc.sbuf_tensor(name, shape, dt))

        semaphores = [(ctx.enter_context(nc.semaphore(f"signal{n}")), 1) for n in range(SEMAPHORES)]
        signals, made_in = {}, [[]]

        def sig(name):
            if name not in signals:
                signals[name] = Signal(name, *semaphores.pop(0))
                made_in[-1].append(name)
            return signals[name]

        def stage(f):
            def run(*args, **kwargs):
                made_in.append([])
                f(*args, **kwargs)
                for name in made_in.pop():
                    s = signals.pop(name)
                    semaphores.append((s.sem, s.base))
            return run

        with nc.Block() as block:
            @block.sync
            def _(sp):
                for s, _ in semaphores[0::4]:
                    sp.sem_inc(s, 1)

            @block.scalar
            def _(act):
                for s, _ in semaphores[1::4]:
                    act.sem_inc(s, 1)

            @block.gpsimd
            def _(pl):
                for s, _ in semaphores[2::4]:
                    pl.sem_inc(s, 1)

            @block.vector
            def _(dve):
                for s, _ in semaphores[3::4]:
                    dve.sem_inc(s, 1)

        H = sb("H", [P, DT, T])
        par = sb("par", [P, NPARAM])
        const = sb("const", [P, 3, P])
        eps = sb("eps", [P, 4])
        wraw = [sb(f"wraw{s}", [P, KMAX * P]) for s in "AB"]
        whi = [sb(f"whi{s}", [P, KMAX, P], r32) for s in "AB"]
        wlo = [sb(f"wlo{s}", [P, KMAX, P], r32) for s in "AB"]
        ps = [ctx.enter_context(nc.psum_tensor(f"ps{s}", [P, 2, HALF], fp32)) for s in "ABCD"]
        flat = [p[:, :, :].rearrange("p a b -> p (a b)") for p in ps]
        ident, mean = const[:, 0, :], const[:, 1, :]

        raw_in = [sig("raw_in_A"), sig("raw_in_B")]
        hi_done = [sig("hi_done_A"), sig("hi_done_B")]
        lo_done = [sig("lo_done_A"), sig("lo_done_B")]
        mm_done = [sig("mm_done_A"), sig("mm_done_B")]
        ps_free = [sig("ps_free_A"), sig("ps_free_B")]

        def after(name, n):
            s = sig(name)
            return s.sem, s.at(n)

        def tick(name, by=1):
            return sig(name).sem, by

        def passed(counts):
            for name, n in counts.items():
                sig(name).passed(n)

        def dram(name, shape):
            return nc.dram_tensor(name, shape, fp32, kind="Internal").ap()

        def pcol(name, i):
            return par[:, ds(COL[name] + i, 1)]

        def project(count, strips, scalar=None, vector=None, pool=None, own=(), vector_alone=None,
                    scalar_first=None, feed=None, fed=()):
            ns = len(strips)
            feed = feed or Feed()

            def split_hi(act, s, i):
                kt = strips[s][2]
                act.wait_ge(raw_in[s].sem, raw_in[s].at(16 * (i + 1)))
                act.wait_ge(mm_done[s].sem, mm_done[s].at(i))
                act.activation(whi[s][:, 0:kt, :], wraw[s][:, 0:kt * P].rearrange("p (k n) -> p k n", n=P),
                               ACT.Copy).then_inc(hi_done[s].sem, 1)

            def split_lo(pl, s, i):
                kt = strips[s][2]
                pl.wait_ge(hi_done[s].sem, hi_done[s].at(i + 1))
                pl.tensor_tensor(wlo[s][:, 0:kt, :], wraw[s][:, 0:kt * P].rearrange("p (k n) -> p k n", n=P),
                                 whi[s][:, 0:kt, :].bitcast(fp32), ALU.subtract).then_inc(lo_done[s].sem, 1)

            def loop(eng, step):
                if count > 2:
                    with eng.Fori(0, count - 1) as i:
                        step(i, False)
                else:
                    for i in range(count - 1):
                        step(i, False)
                step(count - 1, True)

            with nc.Block() as block:
                @block.sync
                def _(sp):
                    def step(i, last):
                        for s in range(ns):
                            w, at, kt = strips[s][:3]
                            sp.wait_ge(lo_done[s].sem, lo_done[s].at(i))
                            sp.dma_start(wraw[s][:, 0:kt * P], w[ds(at(i), 1), :, :].rearrange("a p n -> p (a n)"))\
                              .then_inc(raw_in[s].sem, 16)
                    loop(sp, step)

                @block.scalar
                def _(act):
                    if scalar_first is not None:
                        scalar_first(act)
                    feed.scalar_before(act)
                    for s in range(ns):
                        split_hi(act, s, 0)
                    feed.scalar(act)

                    def step(i, last):
                        for s in range(ns):
                            if scalar is not None:
                                act.wait_ge(mm_done[s].sem, mm_done[s].at(i + 1))
                                scalar(act, s, i, last)
                            if not last:
                                split_hi(act, s, i + 1)
                    loop(act, step)

                @block.gpsimd
                def _(pl):
                    for s in range(ns):
                        split_lo(pl, s, 0)
                    feed.pool(pl)

                    def step(i, last):
                        for s in range(ns):
                            if not last:
                                split_lo(pl, s, i + 1)
                            if pool is not None:
                                pool(pl, s, i, last)
                    loop(pl, step)

                @block.tensor
                def _(pe):
                    feed.tensor(pe)

                    def tile(s, k):
                        kt, xh, xl = strips[s][2:5]
                        for wp, xp in ((whi, xh), (whi, xl), (wlo, xh)):
                            for h in range(2):
                                mm = pe.matmul(ps[s][:, h, :], wp[s][:, k, :], xp[:, k, h * HALF:(h + 1) * HALF],
                                               start=(k == 0 and wp is whi and xp is xh),
                                               stop=(k == kt - 1 and wp is wlo))
                        if k == kt - 1:
                            mm.then_inc(mm_done[s].sem, 1)

                    def first_pair():
                        for k in range(max(strips[s][2] for s in range(ns))):
                            for s in range(ns):
                                if k == 0:
                                    pe.wait_ge(lo_done[s].sem, lo_done[s].at(1))
                                if s in fed:
                                    pe.wait_ge(feed.ready.sem, feed.ready.at(k + 1))
                                if k < strips[s][2]:
                                    tile(s, k)

                    def step(i, last):
                        for s in range(ns):
                            pe.wait_ge(lo_done[s].sem, lo_done[s].at(i + 1))
                            pe.wait_ge(ps_free[s].sem, ps_free[s].at(i))
                            for k in range(strips[s][2]):
                                tile(s, k)
                    first_pair()
                    if count > 3:
                        with pe.Fori(1, count - 1) as i:
                            step(i, False)
                    else:
                        for i in range(1, count - 1):
                            step(i, False)
                    if count > 1:
                        step(count - 1, True)

                @block.vector
                def _(dve):
                    feed.vector(dve)
                    if vector_alone is not None:
                        vector_alone(dve)
                    if vector is not None:
                        def step(i, last):
                            for s in range(ns):
                                dve.wait_ge(mm_done[s].sem, mm_done[s].at(i + 1))
                                vector(dve, s, i, last)
                        loop(dve, step)
            feed.passed()
            for s in range(ns):
                raw_in[s].passed(16 * count)
                for group in (hi_done, lo_done, mm_done, ps_free):
                    group[s].passed(count)
            for name, n in own:
                sig(name).passed(n)

        loaded = sig("loaded")
        made = sig("made")
        with nc.Block() as block:
            @block.sync
            def _(sp):
                sp.dma_start(H[:, :, :], A["xT"]).then_inc(loaded.sem, 16)
                sp.dma_start(par[:, :], A["params"]).then_inc(loaded.sem, 16)
                sp.dma_start(const[:, :, :], A["consts"][:, 0:3, :]).then_inc(loaded.sem, 16)

            @block.vector
            def _(dve):
                for n, v in enumerate((RMS_EPS, GN_EPS, LN_EPS, 0.0)):
                    dve.memset(eps[:, n:n + 1], v).then_inc(made.sem, 1)
                dve.wait_ge(made.sem, made.at(4))
                dve.wait_ge(loaded.sem, loaded.at(48))
        loaded.passed(48)
        made.passed(4)

        class Norm(Feed):

            def __init__(self, src, gain, room, xh=None, xl=None, keep=None, rms=None):
                self.src, self.gain, self.xh, self.xl, self.keep = src, gain, xh, xl, keep
                self.sq, self.xn = room[:, 0:4, :], room[:, 2:4, :]
                self.rms = room[:, 4, :] if rms is None else rms
                self.ready = sig("norm_lo") if keep is None else sig("norm_x")

            def scalar_before(self, act):
                for k in range(DT):
                    if k >= 4:
                        act.wait_ge(*after("norm_sum", k // 2 - 1))
                    act.activation(self.sq[:, k % 4, :], self.src[:, k, :], ACT.Square).then_inc(*tick("norm_sq"))

            def scalar(self, act):
                act.wait_ge(*after("norm_sum", DT // 2))
                act.activation(self.rms, flat[2], ACT.Ln, bias=eps[:, 0:1]).then_inc(*tick("norm_log"))
                act.wait_ge(*after("norm_log", 1))
                act.activation(self.rms, self.rms, ACT.Exp, scale=-0.5).then_inc(*tick("norm_root"))
                if self.keep is None:
                    for k in range(DT):
                        act.wait_ge(*after("norm_x", k + 1))
                        act.activation(self.xh[:, k, :], self.xn[:, k % 2, :], ACT.Copy).then_inc(*tick("norm_hi"))

            def tensor(self, pe):
                for p in range(DT // 2):
                    pe.wait_ge(*after("norm_add", p + 1))
                    for h in range(2):
                        mm = pe.matmul(ps[2][:, h, :], mean, self.sq[:, 2 * (p % 2), h * HALF:(h + 1) * HALF],
                                       start=(p == 0), stop=(p == DT // 2 - 1))
                    mm.then_inc(*tick("norm_sum"))

            def vector(self, dve):
                for p in range(DT // 2):
                    dve.wait_ge(*after("norm_sq", 2 * p + 2))
                    a = 2 * (p % 2)
                    dve.tensor_tensor(self.sq[:, a, :], self.sq[:, a, :], self.sq[:, a + 1, :], ALU.add)\
                       .then_inc(*tick("norm_add"))
                dve.wait_ge(*after("norm_root", 1))
                dve.wait_ge(*after("norm_add", DT // 2))
                for k in range(DT):
                    if self.keep is None and k >= 2:
                        dve.wait_ge(*after("norm_lo", k - 1))
                    dst = self.xn[:, k % 2, :] if self.keep is None else self.keep[:, k, :]
                    dve.scalar_tensor_tensor(out=dst, in0=self.src[:, k, :], scalar=pcol(self.gain, k), in1=self.rms,
                                             op0=ALU.mult, op1=ALU.mult).then_inc(*tick("norm_x"))
                if self.keep is not None:
                    dve.wait_ge(*after("norm_x", DT))

            def pool(self, pl):
                if self.keep is None:
                    for k in range(DT):
                        pl.wait_ge(*after("norm_hi", k + 1))
                        pl.tensor_tensor(self.xl[:, k, :], self.xn[:, k % 2, :], self.xh[:, k, :].bitcast(fp32),
                                         ALU.subtract).then_inc(*tick("norm_lo"))

            def passed(self):
                passed({"norm_sq": DT, "norm_sum": DT // 2, "norm_add": DT // 2, "norm_x": DT, "norm_root": 1, "norm_log": 1})
                if self.keep is None:
                    passed({"norm_hi": DT, "norm_lo": DT})

        class Split(Feed):

            def __init__(self, x, xh, xl, n, src=None):
                self.x, self.xh, self.xl, self.n, self.src = x, xh, xl, n, src
                self.ready = sig("split_lo")

            def scalar_before(self, act):
                if self.src is not None:
                    act.dma_start(self.x[:, :, :], self.src).then_inc(*tick("split_in", 16))

            def scalar(self, act):
                if self.src is not None:
                    act.wait_ge(*after("split_in", 16))
                for k in range(self.n):
                    act.activation(self.xh[:, k, :], self.x[:, k, :], ACT.Copy).then_inc(*tick("split_hi"))

            def pool(self, pl):
                for k in range(self.n):
                    pl.wait_ge(*after("split_hi", k + 1))
                    pl.tensor_tensor(self.xl[:, k, :], self.x[:, k, :], self.xh[:, k, :].bitcast(fp32), ALU.subtract)\
                      .then_inc(*tick("split_lo"))

            def passed(self):
                passed({"split_hi": self.n, "split_lo": self.n, "split_in": 16 if self.src is not None else 0})

        def alone(feed):
            with nc.Block() as block:
                @block.scalar
                def _(act):
                    feed.scalar_before(act)
                    feed.scalar(act)

                block.tensor(feed.tensor)
                block.vector(feed.vector)
            feed.passed()

        def add_to_residual(kt, w, col, xh, xl, bias=None, feed=None):
            def vector(dve, s, i, last):
                if bias is None:
                    dve.tensor_tensor(H[:, ds(2 * i + s, 1), :], ps_tile(s), H[:, ds(2 * i + s, 1), :],
                                      ALU.add).then_inc(ps_free[s].sem, 1)
                else:
                    dve.scalar_tensor_tensor(out=H[:, ds(2 * i + s, 1), :], in0=ps_tile(s),
                                             scalar=pcol(bias, 2 * i + s), in1=H[:, ds(2 * i + s, 1), :],
                                             op0=ALU.add, op1=ALU.add).then_inc(ps_free[s].sem, 1)
            wv = w[:, :, col * P:(col + kt) * P]
            project(DT // 2, [(wv, lambda i, s=s: 2 * i + s, kt, xh, xl) for s in range(2)], vector=vector,
                    feed=feed, fed=(0, 1) if feed else ())

        def ps_tile(s):
            return flat[s].rearrange("p (a t) -> p a t", a=1)

        def one(t):
            return t.rearrange("p (a t) -> p a t", a=1)

        @stage
        def ffn(l):
            with ExitStack() as c:
                xh = sb(f"ffn_xh{l}", [P, DT, T], r32, c)
                xl = sb(f"ffn_xl{l}", [P, DT, T], r32, c)
                hh = sb(f"ffn_hh{l}", [P, FF_GROUPS[0], T], r32, c)
                hl = sb(f"ffn_hl{l}", [P, FF_GROUPS[0], T], r32, c)
                gate = sb(f"ffn_gate{l}", [P, T], fp32, c)
                room = sb(f"ffn_room{l}", [P, 4, T], fp32, c)
                first = 0
                for g in FF_GROUPS:
                    hid_hi, hid_lo = sig("hid_hi"), sig("hid_lo")

                    def scalar(act, s, i, last):
                        if s == 0:
                            act.wait_ge(ps_free[1].sem, ps_free[1].at(i))
                            act.wait_ge(hid_lo.sem, hid_lo.at(i))
                            act.activation(gate[:, :], flat[0], ACT.Silu).then_inc(ps_free[0].sem, 1)
                        else:
                            act.wait_ge(ps_free[1].sem, ps_free[1].at(i + 1))
                            act.activation(hh[:, ds(i, 1), :], one(gate[:, :]), ACT.Copy).then_inc(hid_hi.sem, 1)

                    def vector(dve, s, i, last):
                        if s == 1:
                            dve.wait_ge(ps_free[0].sem, ps_free[0].at(i + 1))
                            dve.tensor_tensor(gate[:, :], flat[1], gate[:, :], ALU.mult)\
                               .then_inc(ps_free[1].sem, 1)

                    def pool(pl, s, i, last):
                        if s == 1:
                            pl.wait_ge(hid_hi.sem, hid_hi.at(i + 1))
                            pl.tensor_tensor(hl[:, ds(i, 1), :], one(gate[:, :]), hh[:, ds(i, 1), :].bitcast(fp32),
                                             ALU.subtract).then_inc(hid_lo.sem, 1)

                    w = A[f"ffn_in{l}"]
                    feed = Norm(H, f"norm_ffn{l}", room, xh, xl, rms=gate[:, :]) if first == 0 else None
                    project(g, [(w, lambda i, o=first: o + i, DT, xh, xl), (w, lambda i, o=first: FT + o + i, DT, xh, xl)],
                            scalar, vector, pool, own=(("hid_hi", g), ("hid_lo", g)), feed=feed, fed=(0, 1) if feed else ())
                    add_to_residual(g, A[f"ffn_out{l}"], first, hh, hl)
                    first += g

        @stage
        def ple(l):
            with ExitStack() as c:
                xh = sb(f"ple_xh{l}", [P, DT, T], r32, c)
                xl = sb(f"ple_xl{l}", [P, DT, T], r32, c)
                room = sb(f"ple_room{l}", [P, 5, T], fp32, c)
                p = sb(f"ple_p{l}", [P, PLE_T, T], fp32, c)
                ph = sb(f"ple_ph{l}", [P, PLE_T, T], r32, c)
                pl_ = sb(f"ple_pl{l}", [P, PLE_T, T], r32, c)
                gate = sb(f"ple_gate{l}", [P, T], fp32, c)
                split_operand(A["pT"][l], p, ph, pl_)
                used = sig("ple_used")

                def scalar(act, s, i, last):
                    if s == 0:
                        act.wait_ge(used.sem, used.at(i))
                        act.activation(gate[:, :], flat[0], ACT.Sigmoid).then_inc(ps_free[0].sem, 1)

                def vector(dve, s, i, last):
                    if s == 1:
                        dve.wait_ge(ps_free[0].sem, ps_free[0].at(i + 1))
                        dve.tensor_tensor(gate[:, :], flat[1], gate[:, :], ALU.mult).then_inc(ps_free[1].sem, 1)
                        dve.wait_ge(ps_free[1].sem, ps_free[1].at(i + 1))
                        dve.tensor_tensor(H[:, ds(i, 1), :], one(gate[:, :]), H[:, ds(i, 1), :],
                                          ALU.add).then_inc(used.sem, 1)
                project(DT, [(A[f"ple_gate{l}"], lambda i: i, DT, xh, xl), (A[f"ple_proj{l}"], lambda i: i, PLE_T, ph, pl_)],
                        scalar, vector, own=(("ple_used", DT),), feed=Norm(H, f"norm_ple{l}", room, xh, xl), fed=(0,))

        @stage
        def split_operand(src, p, ph, pl_):
            p_in, p_hi, p_lo = sig("p_in"), sig("p_hi"), sig("p_lo")
            with nc.Block() as block:
                if src is not None:
                    @block.sync
                    def _(sp):
                        sp.dma_start(p[:, :, :], src).then_inc(p_in.sem, 16)

                @block.scalar
                def _(act):
                    if src is not None:
                        act.wait_ge(p_in.sem, p_in.at(16))
                    act.activation(ph[:, :, :], p[:, :, :], ACT.Copy).then_inc(p_hi.sem, 1)

                @block.gpsimd
                def _(pl):
                    pl.wait_ge(p_hi.sem, p_hi.at(1))
                    pl.tensor_tensor(pl_[:, :, :], p[:, :, :], ph[:, :, :].bitcast(fp32), ALU.subtract)\
                      .then_inc(p_lo.sem, 1)
            if src is not None:
                p_in.passed(16)
            p_hi.passed(1)
            p_lo.passed(1)

        @stage
        def hawk():
            with ExitStack() as c:
                gate = sb("hawk_gate", [P, RT, T], fp32, c)
                c_rec = ExitStack()
                rec = sb("hawk_rec", [P, RT, 3 + T], fp32, c_rec)
                with ExitStack() as c1:
                    xh = sb("hawk_xh", [P, DT, T], r32, c1)
                    xl = sb("hawk_xl", [P, DT, T], r32, c1)

                    def gelu(act, s, i, last):
                        act.activation(gate[:, ds(2 * i + s, 1), :], ps_tile(s), ACT.Gelu_apprx_tanh,
                                       bias=pcol("lru_b_in", 2 * i + s)).then_inc(ps_free[s].sem, 1)
                    project(RT // 2, [(A["hawk_in"], lambda i, s=s: 2 * i + s, DT, xh, xl) for s in range(2)], gelu,
                            feed=Norm(H, "norm_mix0", gate[:, 0:5, :], xh, xl), fed=(0, 1))

                    def keep(act, s, i, last):
                        act.activation(rec[:, ds(2 * i + s, 1), 3:3 + T], ps_tile(s), ACT.Identity,
                                       bias=pcol("lru_b_in", RT + 2 * i + s)).then_inc(ps_free[s].sem, 1)
                    project(RT // 2, [(A["hawk_in"], lambda i, s=s: RT + 2 * i + s, DT, xh, xl) for s in range(2)], keep)
                lru(rec, gate)
                c_rec.close()
                xh = sb("lru_xh", [P, RT, T], r32, c)
                xl = sb("lru_xl", [P, RT, T], r32, c)
                for first in (0, RT // 2):
                    part = [t[:, first:first + RT // 2, :] for t in (gate, xh, xl)]
                    add_to_residual(RT // 2, A["hawk_out"], first, part[1], part[2], bias="lru_b_out" if first == 0 else None,
                                    feed=Split(*part, RT // 2))

        @stage
        def lru(rec, gate):
            with ExitStack() as c:
                gw = sb("lru_gw", [P, 2, P], fp32, c)
                sp8 = sb("lru_sp", [P, 8, RT], fp32, c)
                xf = sb("lru_xf", [P, 2, T], fp32, c)
                ta = sb("lru_ta", [P, T], fp32, c)
                ti = sb("lru_ti", [P, T], fp32, c)
                av = sb("lru_a", [P, T], fp32, c)
                tz = sb("lru_tz", [P, T], fp32, c)
                e = sb("lru_e", [P, T], fp32, c)
                prep, gw_in, xf_done, gates = sig("lru_prep"), sig("lru_gw_in"), sig("lru_xf_done"), sig("lru_gates")
                t_done, e_done, s_done, b_done = sig("lru_t"), sig("lru_e"), sig("lru_s"), sig("lru_b")
                dchain, achain = sig("dve_chain"), sig("act_chain")
                lam = par[:, COL["lru_lambda"]:COL["lru_lambda"] + RT]
                with nc.Block() as block:
                    @block.vector
                    def _(dve):
                        ch = Chain(dve, dchain)
                        ch(dve.memset(rec[:, :, 0:3], 0.0))
                        ch(dve.tensor_scalar(sp8[:, 0, :], lam, -1.0, 0.0, ALU.mult, ALU.max))
                        ch(dve.scalar_tensor_tensor(out=sp8[:, 1, :], in0=sp8[:, 0, :], scalar=2.0, in1=lam,
                                                    op0=ALU.mult, op1=ALU.add))
                        dve.tensor_scalar(sp8[:, 6, :], par[:, COL["b_gate_a"]:COL["b_gate_a"] + RT], 0.5, None,
                                          ALU.mult).then_inc(prep.sem, 1)
                        dve.tensor_scalar(sp8[:, 7, :], par[:, COL["b_gate_x"]:COL["b_gate_x"] + RT], 0.5, None,
                                          ALU.mult).then_inc(prep.sem, 1)
                        dve.wait_ge(prep.sem, prep.at(3))
                        ch(dve.tensor_scalar(sp8[:, 3, :], sp8[:, 2, :], 1.0, None, ALU.add))
                        ch(dve.tensor_scalar(sp8[:, 4, :], sp8[:, 3, :], -1.0, None, ALU.add))
                        dve.tensor_scalar(sp8[:, 5, :], sp8[:, 4, :], 0.0, None, ALU.is_equal).then_inc(prep.sem, 1)
                        dve.wait_ge(prep.sem, prep.at(5))
                        ch(dve.tensor_tensor(sp8[:, 4, :], sp8[:, 4, :], sp8[:, 5, :], ALU.add))
                        ch(dve.tensor_tensor(sp8[:, 1, :], sp8[:, 1, :], sp8[:, 5, :], ALU.add))
                        ch(dve.reciprocal(sp8[:, 4, :], sp8[:, 4, :]))
                        ch(dve.tensor_tensor(sp8[:, 1, :], sp8[:, 1, :], sp8[:, 4, :], ALU.mult))
                        ch(dve.tensor_tensor(sp8[:, 1, :], sp8[:, 1, :], sp8[:, 2, :], ALU.mult))
                        ch(dve.tensor_tensor(sp8[:, 1, :], sp8[:, 1, :], sp8[:, 0, :], ALU.add))
                        ch(dve.tensor_scalar(sp8[:, 4, :], sp8[:, 1, :], 4.0, None, ALU.mult))
                        ch(dve.tensor_scalar(sp8[:, 5, :], sp8[:, 1, :], -4.0, None, ALU.mult))
                        chain_n.append(ch.n)

                    @block.scalar
                    def _(act):
                        act.wait_ge(prep.sem, prep.at(2))
                        act.wait_ge(dchain.sem, dchain.at(3))
                        act.activation(sp8[:, 2, :], sp8[:, 1, :], ACT.Exp, scale=-1.0).then_inc(prep.sem, 1)
                        act.wait_ge(prep.sem, prep.at(4))
                        act.wait_ge(dchain.sem, dchain.at(5))
                        act.activation(sp8[:, 1, :], sp8[:, 3, :], ACT.Ln).then_inc(prep.sem, 1)
                prep.passed(5)
                dchain.passed(chain_n.pop())

                def col(j, n):
                    return sp8[:, j, ds(n, 1)]
                with nc.Block() as block:
                    @block.sync
                    def _(sp):
                        with sp.Fori(0, RT) as n:
                            sp.wait_ge(gates.sem, gates.at(n))
                            sp.dma_start(gw[:, 0, :], A["gate_a"][ds(n, 1), :, :].rearrange("a p n -> p (a n)"))\
                              .then_inc(gw_in.sem, 16)
                            sp.dma_start(gw[:, 1, :], A["gate_x"][ds(n, 1), :, :].rearrange("a p n -> p (a n)"))\
                              .then_inc(gw_in.sem, 16)

                    @block.tensor
                    def _(pe):
                        def body(n, z):
                            pe.wait_ge(gw_in.sem, gw_in.at(32 * n + 32))
                            pe.wait_ge(xf_done.sem, xf_done.at(n + 1))
                            pe.wait_ge(t_done.sem, t_done.at(n))
                            for j in range(2):
                                for h in range(2):
                                    mm = pe.matmul(ps[j][:, h, :], gw[:, j, :], xf[:, z, h * HALF:(h + 1) * HALF],
                                                   start=True, stop=True)
                            mm.then_inc(gates.sem, 1)
                        with pe.Fori(0, RT // 2) as i:
                            body(2 * i, 0)
                            body(2 * i + 1, 1)

                    @block.scalar
                    def _(act):
                        per = 4
                        with act.Fori(0, RT) as n:
                            ch = Chain(act, achain, per * n)
                            act.wait_ge(gates.sem, gates.at(n + 1))
                            act.wait_ge(b_done.sem, b_done.at(n))
                            ch(act.activation(ta[:, :], flat[0], ACT.Tanh, scale=0.5, bias=col(6, n)))
                            act.activation(ti[:, :], flat[1], ACT.Tanh, scale=0.5, bias=col(7, n)).then_inc(t_done.sem, 1)
                            ch(act.activation(av[:, :], ta[:, :], ACT.Exp, scale=col(5, n), bias=col(5, n)))
                            ch(act.activation(tz[:, :], ta[:, :], ACT.Tanh, scale=col(4, n), bias=col(4, n)))
                            ch(act.activation(e[:, :], av[:, :], ACT.Square))
                            act.wait_ge(e_done.sem, e_done.at(n + 1))
                            act.activation(e[:, :], e[:, :], ACT.Sqrt).then_inc(s_done.sem, 1)
                            assert ch.n == per

                    @block.vector
                    def _(dve):
                        def conv(n, z, start):
                            ch = Chain(dve, dchain, start)
                            ch(dve.tensor_scalar(xf[:, z:z + 1, :], rec[:, ds(n, 1), 0:T], pcol("conv_w", n),
                                                 pcol("conv_b", n), ALU.mult, ALU.add))
                            for j in range(1, 4):
                                i = dve.scalar_tensor_tensor(out=xf[:, z:z + 1, :], in0=rec[:, ds(n, 1), j:j + T],
                                                             scalar=pcol("conv_w", j * RT + n), in1=xf[:, z:z + 1, :],
                                                             op0=ALU.mult, op1=ALU.add)
                                if j < 3:
                                    ch(i)
                            i.then_inc(xf_done.sem, 1)
                            assert ch.n == 3

                        def recur(n, z, start):
                            ch = Chain(dve, dchain, start)
                            dve.wait_ge(achain.sem, achain.at(4 * n + 4))
                            dve.scalar_tensor_tensor(out=e[:, :], in0=e[:, :], scalar=1.0, in1=tz[:, :],
                                                     op0=ALU.add, op1=ALU.mult).then_inc(e_done.sem, 1)
                            dve.wait_ge(t_done.sem, t_done.at(n + 1))
                            dve.wait_ge(xf_done.sem, xf_done.at(n + 1))
                            ch(dve.scalar_tensor_tensor(out=ti[:, :], in0=ti[:, :], scalar=1.0, in1=xf[:, z, :],
                                                        op0=ALU.add, op1=ALU.mult))
                            dve.wait_ge(s_done.sem, s_done.at(n + 1))
                            ch(dve.scalar_tensor_tensor(out=ti[:, :], in0=ti[:, :], scalar=0.5, in1=e[:, :],
                                                        op0=ALU.mult, op1=ALU.mult))
                            i = dve.tensor_tensor_scan(out=ta[:, :], data0=av[:, :], data1=ti[:, :], initial=0.0,
                                                       op0=ALU.mult, op1=ALU.add)
                            i.then_inc(sig("lru_scan").sem, 1)
                            dve.wait_ge(sig("lru_scan").sem, sig("lru_scan").at(n + 1))
                            dve.tensor_tensor(gate[:, ds(n, 1), :], one(ta[:, :]), gate[:, ds(n, 1), :], ALU.mult)\
                               .then_inc(b_done.sem, 1)
                            assert ch.n == 2

                        conv(0, 0, 0)
                        with dve.Fori(0, RT // 2 - 1) as i:
                            for z in range(2):
                                n = 2 * i + z
                                dve.wait_ge(gates.sem, gates.at(n))
                                conv(n + 1, 1 - z, 5 * n + 3)
                                recur(n, z, 5 * n + 6)
                        dve.wait_ge(gates.sem, gates.at(RT - 2))
                        conv(RT - 1, 1, 5 * (RT - 2) + 3)
                        recur(RT - 2, 0, 5 * (RT - 2) + 6)
                        recur(RT - 1, 1, 5 * (RT - 1) + 3)
                dchain.passed(5 * RT)
                achain.passed(4 * RT)
                gw_in.passed(32 * RT)
                for s in (xf_done, gates, t_done, e_done, s_done, b_done, sig("lru_scan")):
                    s.passed(RT)

        def store_strips(dst, stage, func, bias=None):
            def scalar(act, s, i, last):
                m = 2 * i + s
                act.wait_ge(*after(f"strip_out_{'AB'[s]}", 16 * i))
                if bias is None:
                    act.activation(stage[:, s, :], flat[s], func).then_inc(ps_free[s].sem, 1)
                else:
                    act.activation(stage[:, s, :], flat[s], func, bias=pcol(bias, m)).then_inc(ps_free[s].sem, 1)
                act.wait_ge(ps_free[s].sem, ps_free[s].at(i + 1))
                act.dma_start(dst(m), stage[:, s, :]).then_inc(*tick(f"strip_out_{'AB'[s]}", 16))
                if last:
                    act.wait_ge(*after(f"strip_out_{'AB'[s]}", 16 * (i + 1)))
            return scalar

        @stage
        def rwkv():
            rows = lambda t: (lambda m: t[ds(m, 1), :, :].rearrange("a p t -> p (a t)"))
            R_, K_, V_ = (dram(f"rwd_{n}", [DT, P, T]) for n in "rkv")
            S_, A_, G_ = (dram(f"rwd_{n}", [DT, P, T]) for n in ("decay", "a", "g"))
            VG = dram("rw_vg", [4 * DT, P, 2 * P])
            QD = dram("rw_arbk", [4 * DT, P, 2, 4, P])
            PC = dram("rw_pc", [4 * DT, P, 4])
            BN = dram("rw_bonus", [DT, P, T])
            Y_ = dram("rw_y", [4 * DT, P, 2 * P])
            with ExitStack() as c:
                xn = sb("rw_xn", [P, DT, T], fp32, c)
                xh = sb("rw_xh", [P, DT, T], r32, c)
                xl = sb("rw_xl", [P, DT, T], r32, c)
                hh = sb("rw_hh", [P, 2, T], r32, c)
                hl = sb("rw_hl", [P, 2, T], r32, c)
                stage_ = sb("rw_stage", [P, 2, T], fp32, c)
                with ExitStack() as c2:
                    alone(Norm(H, "norm_mix1", sb("rw_room", [P, 5, T], fp32, c2), keep=xn))

                class Mixed(Feed):

                    def __init__(self, j):
                        self.j = j
                        self.ready = sig("mix_lo")

                    def vector(self, dve):
                        for k in range(DT):
                            if k >= 2:
                                dve.wait_ge(*after("mix_lo", k - 1))
                            dve.tensor_tensor(stage_[:, k % 2, 1:T], xn[:, k, 0:T - 1], xn[:, k, 1:T], ALU.subtract)
                            dve.tensor_scalar(stage_[:, k % 2, 0:1], xn[:, k, 0:1], -1.0, None, ALU.mult)\
                               .then_inc(*tick("mix_diff"))
                            dve.wait_ge(*after("mix_diff", k + 1))
                            dve.scalar_tensor_tensor(out=stage_[:, k % 2, :], in0=stage_[:, k % 2, :],
                                                     scalar=pcol("rw_mu", self.j * DT + k), in1=xn[:, k, :],
                                                     op0=ALU.mult, op1=ALU.add).then_inc(*tick("mix_x"))

                    def scalar(self, act):
                        for k in range(DT):
                            act.wait_ge(*after("mix_x", k + 1))
                            act.activation(xh[:, k, :], stage_[:, k % 2, :], ACT.Copy).then_inc(*tick("mix_hi"))

                    def pool(self, pl):
                        for k in range(DT):
                            pl.wait_ge(*after("mix_hi", k + 1))
                            pl.tensor_tensor(xl[:, k, :], stage_[:, k % 2, :], xh[:, k, :].bitcast(fp32), ALU.subtract)\
                              .then_inc(*tick("mix_lo"))

                    def passed(self):
                        passed({"mix_diff": DT, "mix_x": DT, "mix_hi": DT, "mix_lo": DT})

                def wide(w, dst, m0=0, func=ACT.Copy, bias=None, kt=DT, x=(xh, xl), mix=None):
                    project(DT // 2, [(w, lambda i, s=s: m0 + 2 * i + s, kt, *x) for s in range(2)],
                            store_strips(dst, stage_, func, bias),
                            own=(("strip_out_A", 16 * DT // 2), ("strip_out_B", 16 * DT // 2)),
                            feed=None if mix is None else Mixed(mix), fed=() if mix is None else (0, 1))

                def narrow(w, nt, func, mix):
                    def scalar(act, s, i, last):
                        act.activation(stage_[:, s, :], flat[s], func).then_inc(ps_free[s].sem, 1)
                        act.wait_ge(ps_free[s].sem, ps_free[s].at(1))
                        act.activation(hh[:, s, :], stage_[:, s, :], ACT.Copy).then_inc(*tick("lora_hi"))

                    def pool(pl, s, i, last):
                        pl.wait_ge(*after("lora_hi", s + 1))
                        pl.tensor_tensor(hl[:, s, :], stage_[:, s, :], hh[:, s, :].bitcast(fp32), ALU.subtract)\
                          .then_inc(*tick("lora_lo"))
                    project(1, [(w, lambda i, s=s: i + s, DT, xh, xl) for s in range(nt)], scalar, pool=pool,
                            own=(("lora_hi", nt), ("lora_lo", nt)), feed=Mixed(mix), fed=tuple(range(nt)))

                wide(A["rkv"], rows(R_), mix=0)
                wide(A["rkv"], rows(K_), DT, mix=2)
                wide(A["rkv"], rows(V_), 2 * DT, mix=3)
                narrow(A["rw_w1"], 1, ACT.Tanh, 1)
                wide(A["rw_w2"], rows(S_), 0, ACT.Sigmoid, "rw_w0", 1, (hh, hl))
                narrow(A["rw_a1"], 1, ACT.Copy, 4)
                wide(A["rw_a2"], rows(A_), 0, ACT.Sigmoid, "rw_a0", 1, (hh, hl))
                narrow(A["rw_g1"], 2, ACT.Sigmoid, 5)
                wide(A["rw_g2"], rows(G_), 0, ACT.Copy, None, 2, (hh, hl))

            rwkv_operands(R_, K_, V_, S_, A_, QD, PC, BN, VG)
            rwkv_scan(QD, PC, VG, Y_)
            with ExitStack() as c:
                o = sb("rw_o", [P, DT, T], fp32, c)
                rwkv_output(Y_, BN, G_, o)
                xh = sb("rwo_xh", [P, DT, T], r32, c)
                xl = sb("rwo_xl", [P, DT, T], r32, c)
                add_to_residual(DT, A["rw_o"], 0, xh, xl, feed=Split(o, xh, xl, DT))

        DECAY = float(np.exp(-0.5))

        @stage
        def rwkv_operands(R_, K_, V_, S_, A_, QD, PC, BN, VG):
            with ExitStack() as c:
                heads = const[:, 2, :]
                reset = sb("op_reset", [P, T], fp32, c)
                slots = {n: sb(f"op_{n}", [P, 2, T], fp32, c) for n in ("r", "k", "v", "w", "a", "bn")}
                inner = {n: sb(f"op_{n}", [P, T], fp32, c) for n in
                         ("s", "sm", "p", "pi", "pp", "kk", "t", "inv", "b", "k2", "rk")}
                q = sb("op_q", [P, 2, 4, 2, 4, P], fp32, c)
                pc = sb("op_pc", [P, 2, 16], fp32, c)
                src = {"r": R_, "k": K_, "v": V_, "w": S_, "a": A_}

                def tile_of(j):
                    return {**{n: t[:, j, :] for n, t in slots.items()}, **{n: t[:, :] for n, t in inner.items()}}

                def part_of(j):
                    return lambda z: q[:, j, :, :, z, :].rearrange("p g q t -> p (g q) t")

                def by8(t):
                    return t.rearrange("p (g t) -> p g t", g=8)
                with nc.Block() as block:
                    @block.vector
                    def _(dve):
                        dve.memset(reset[:, :], 1.0).then_inc(*tick("op_reset"))
                        dve.wait_ge(*after("op_reset", 1))
                        dve.memset(reset[:, 0:T:CHUNK], 0.0).then_inc(*tick("op_reset"))
                        dve.wait_ge(*after("op_reset", 2))
                passed({"op_reset": 2})
                def pairs(eng, body):
                    with eng.Fori(0, DT // 2) as i:
                        body(2 * i, 0, i)
                        body(2 * i + 1, 1, i)

                with nc.Block() as block:
                    @block.sync
                    def _(sp):
                        def load(m, j, r):
                            sp.wait_ge(*after(f"op_out_{j}", 16 * 7 * r))
                            for n in src:
                                sp.dma_start(slots[n][:, j, :], src[n][ds(m, 1), :, :].rearrange("a p t -> p (a t)"))\
                                  .then_inc(*tick(f"op_in_{j}", 16))

                        def store(m, j):
                            x = tile_of(j)
                            sp.wait_ge(*after("op_q", 4 * m + 4))
                            for g in range(4):
                                sp.dma_start(QD[ds(4 * m + g, 1), :, :, :, :].rearrange("a p q j t -> p (a q j t)"),
                                             q[:, j, g, :, :, :].rearrange("p q j t -> p (q j t)")).then_inc(*tick(f"op_out_{j}", 16))
                            sp.wait_ge(*after("op_pc", m + 1))
                            sp.dma_start(PC[ds(4 * m, 4), :, :].rearrange("g p c -> p g c"),
                                         pc[:, j, :].rearrange("p (g c) -> p g c", g=4)).then_inc(*tick(f"op_out_{j}", 16))
                            sp.dma_start(VG[ds(4 * m, 4), :, :].rearrange("g p t -> p g t"),
                                         x["v"].rearrange("p (g t) -> p g t", g=4)).then_inc(*tick(f"op_out_{j}", 16))
                            sp.wait_ge(*after("op_bonus", m + 1))
                            sp.dma_start(BN[ds(m, 1), :, :].rearrange("a p t -> p (a t)"), x["bn"])\
                              .then_inc(*tick(f"op_out_{j}", 16))
                        load(0, 0, 0)
                        with sp.Fori(0, DT // 2 - 1) as i:
                            load(2 * i + 1, 1, i)
                            store(2 * i, 0)
                            load(2 * i + 2, 0, i + 1)
                            store(2 * i + 1, 1)
                        load(DT - 1, 1, DT // 2 - 1)
                        store(DT - 2, 0)
                        store(DT - 1, 1)
                        for j in range(2):
                            sp.wait_ge(*after(f"op_out_{j}", 16 * 7 * DT // 2))

                    @block.gpsimd
                    def _(pl):
                        def body(m, j, r):
                            x, part = tile_of(j), part_of(j)
                            pl.wait_ge(*after("op_s", m + 1))
                            pl.tensor_tensor(x["sm"][:, :], x["s"][:, :], x["w"][:, :], ALU.subtract)\
                              .then_inc(*tick("op_sm"))
                            pl.wait_ge(*after("op_p", m + 1))
                            pl.tensor_tensor(part(1), by8(x["r"]), by8(x["p"]), ALU.mult).then_inc(*tick("op_q"))
                            pl.tensor_copy(pc[:, j, :], x["p"][:, CHUNK - 1:T:CHUNK]).then_inc(*tick("op_pc"))
                            pl.wait_ge(*after("op_k2", m + 1))
                            pl.wait_ge(*after("op_pi", m + 1))
                            pl.tensor_tensor(part(3), by8(x["k2"]), by8(x["pi"]), ALU.mult).then_inc(*tick("op_q"))
                        pairs(pl, body)

                    @block.scalar
                    def _(act):
                        def body(m, j, r):
                            x = tile_of(j)
                            act.wait_ge(*after("op_kk", m + 1))
                            act.activation(x["t"][:, :], x["kk"][:, :], ACT.Square).then_inc(*tick("op_sq"))
                            act.wait_ge(*after("op_s", m + 1))
                            act.activation(x["p"][:, :], x["s"][:, :], ACT.Exp, scale=-DECAY).then_inc(*tick("op_p"))
                            act.activation(x["pi"][:, :], x["s"][:, :], ACT.Exp, scale=DECAY).then_inc(*tick("op_pi"))
                            act.wait_ge(*after("op_sm", m + 1))
                            act.activation(x["pp"][:, :], x["sm"][:, :], ACT.Exp, scale=-DECAY).then_inc(*tick("op_pp"))
                            act.wait_ge(*after("op_floor", m + 1))
                            act.activation(x["inv"][:, :], x["inv"][:, :], ACT.Ln).then_inc(*tick("op_log"))
                            act.wait_ge(*after("op_log", m + 1))
                            act.activation(x["inv"][:, :], x["inv"][:, :], ACT.Exp, scale=-0.5).then_inc(*tick("op_root"))
                        pairs(act, body)

                    @block.tensor
                    def _(pe):
                        def body(m, j, r):
                            x = tile_of(j)
                            pe.wait_ge(*after("op_sq", m + 1))
                            for h in range(2):
                                mm = pe.matmul(ps[0][:, h, :], heads, x["t"][:, h * HALF:(h + 1) * HALF],
                                               start=True, stop=True)
                            mm.then_inc(*tick("op_norm"))
                            pe.wait_ge(*after("op_rk", m + 1))
                            pe.wait_ge(*after("op_bonus", m))
                            for h in range(2):
                                mm = pe.matmul(ps[1][:, h, :], heads, x["rk"][:, h * HALF:(h + 1) * HALF],
                                               start=True, stop=True)
                            mm.then_inc(*tick("op_rksum"))
                        pairs(pe, body)

                    @block.vector
                    def _(dve):
                        def body(m, j, r):
                            x, part = tile_of(j), part_of(j)
                            dve.wait_ge(*after(f"op_in_{j}", 80 * r + 80))
                            dve.wait_ge(*after(f"op_out_{j}", 16 * 7 * r))
                            dve.tensor_scalar(x["kk"][:, :], x["k"][:, :], pcol("rw_k_k", m), None, ALU.mult)\
                               .then_inc(*tick("op_kk"))
                            dve.tensor_tensor_scan(out=x["s"][:, :], data0=reset[:, :], data1=x["w"][:, :],
                                                   initial=0.0, op0=ALU.mult, op1=ALU.add).then_inc(*tick("op_s"))
                            dve.tensor_scalar(x["b"][:, :], x["a"][:, :], -1.0, pcol("rw_k_a", m), ALU.add, ALU.mult)\
                               .then_inc(*tick("op_v"))
                            dve.wait_ge(*after("op_v", 3 * m + 1))
                            dve.scalar_tensor_tensor(out=x["k2"][:, :], in0=x["b"][:, :], scalar=1.0, in1=x["k"][:, :],
                                                     op0=ALU.add, op1=ALU.mult).then_inc(*tick("op_k2"))
                            dve.wait_ge(*after("op_k2", m + 1))
                            dve.scalar_tensor_tensor(out=x["rk"][:, :], in0=x["r"][:, :], scalar=pcol("rw_r_k", m),
                                                     in1=x["k2"][:, :], op0=ALU.mult, op1=ALU.mult).then_inc(*tick("op_rk"))
                            dve.wait_ge(*after("op_norm", m + 1))
                            dve.tensor_scalar(x["inv"][:, :], flat[0], 1e-24, None, ALU.max).then_inc(*tick("op_floor"))
                            dve.wait_ge(*after("op_rksum", m + 1))
                            dve.tensor_tensor(x["bn"][:, :], flat[1], x["v"][:, :], ALU.mult).then_inc(*tick("op_bonus"))
                            dve.wait_ge(*after("op_root", m + 1))
                            dve.tensor_tensor(x["kk"][:, :], x["kk"][:, :], x["inv"][:, :], ALU.mult).then_inc(*tick("op_v"))
                            dve.wait_ge(*after("op_v", 3 * m + 2))
                            dve.wait_ge(*after("op_pp", m + 1))
                            dve.scalar_tensor_tensor(out=part(0), in0=by8(x["kk"]), scalar=-1.0, in1=by8(x["pp"]),
                                                     op0=ALU.mult, op1=ALU.mult).then_inc(*tick("op_q"))
                            dve.tensor_tensor(x["b"][:, :], x["kk"][:, :], x["a"][:, :], ALU.mult).then_inc(*tick("op_v"))
                            dve.wait_ge(*after("op_v", 3 * m + 3))
                            dve.wait_ge(*after("op_pi", m + 1))
                            dve.tensor_tensor(part(2), by8(x["b"]), by8(x["pi"]), ALU.mult).then_inc(*tick("op_q"))
                            dve.wait_ge(*after("op_q", 4 * m + 4))
                            dve.wait_ge(*after("op_pc", m + 1))
                        pairs(dve, body)
                passed({"op_in_0": 40 * DT, "op_in_1": 40 * DT, "op_out_0": 56 * DT, "op_out_1": 56 * DT,
                        "op_q": 4 * DT, "op_v": 3 * DT, "op_floor": DT, "op_log": DT})
                passed({n: DT for n in ("op_s", "op_sm", "op_p", "op_pi", "op_pp", "op_pc", "op_kk", "op_k2", "op_sq",
                                        "op_norm", "op_root", "op_rk", "op_rksum", "op_bonus")})

        @stage
        def rwkv_scan(QD, PC, VG, Y_):
            NG = 4 * DT
            LEVELS = (2, 4, 8, 16, 32)
            with ExitStack() as c:
                masks = sb("sc_masks", [P, 4, P], fp32, c)
                levels = sb("sc_levels", [P, 6, P], fp32, c)
                ident2 = sb("sc_ident2", [P, HEAD], fp32, c)
                flags = sb("sc_flags", [P, NG], fp32, c)
                ops = sb("sc_ops", [P, 2, 2, 4, P], fp32, c)
                vv = sb("sc_v", [P, 2, 2, P], fp32, c)
                pcs = sb("sc_pc", [P, NG * 4], fp32, c)
                arp = sb("sc_arp", [P, 2, 2, 2, 2, P], fp32, c)
                tm = sb("sc_tm", [P, 2, 3, P], fp32, c)
                cmask = sb("sc_cmask", [P, 2], fp32, c)
                bpad, vpad, zpad = (sb(f"sc_{n}pad", [P, 2, 2, P], fp32, c) for n in "bvz")
                arhs = sb("sc_arhs", [P, 2, 2, 2, HEAD], fp32, c)
                G_ = sb("sc_G", [P, 2, 4, 4, P], fp32, c)
                NT = sb("sc_NT", [P, 6, 4, P], fp32, c)
                X = sb("sc_X", [P, 4, P], fp32, c)
                XT = sb("sc_XT", [P, 4, P], fp32, c)
                Wt = sb("sc_Wt", [P, 4, P], fp32, c)
                WZ = sb("sc_WZ", [P, 4, 2, HEAD], fp32, c)
                vside = sb("sc_vside", [P, 2, 2, P], fp32, c)
                Wq = sb("sc_Wq", [P, 2, P], fp32, c)
                MT = sb("sc_MT", [P, 2, 4, HEAD], fp32, c)
                Q = sb("sc_Q", [P, 2, 4, HEAD], fp32, c)
                F = sb("sc_F", [P, 2, 2 * P], fp32, c)
                Yi = sb("sc_Yi", [P, 2, 2 * P], fp32, c)
                y = sb("sc_y", [P, 2, 2 * P], fp32, c)
                S = sb("sc_S", [P, 5, HEAD], fp32, c)
                bank = [ps[b // 2][:, b % 2, :] for b in range(8)]
                four = [b.rearrange("p (u t) -> p u t", u=4) for b in bank]

                with nc.Block() as block:
                    @block.sync
                    def _(sp):
                        for n, name in enumerate(("mask_a", "mask_r", "mask_a", "mask_r")):
                            sp.dma_start(masks[:, n, :], A["consts"][:, CIX[name], :]).then_inc(*tick("sc_const", 16))
                        sp.dma_start(levels[:, :, :], A["consts"][:, CIX["level1"]:CIX["level1"] + 6, :])\
                          .then_inc(*tick("sc_const", 16))
                        sp.dma_start(ident2[:, :], A["scan_ident"]).then_inc(*tick("sc_const", 16))
                        sp.dma_start(flags[:, :], A["scan_flags"]).then_inc(*tick("sc_const", 16))
                        sp.dma_start(cmask[:, :], A["scan_chunks"]).then_inc(*tick("sc_const", 16))
                        sp.dma_start(pcs[:, :].rearrange("p (g c) -> p g c", c=4), PC.rearrange("g p c -> p g c"))\
                          .then_inc(*tick("sc_const", 16))
                        sp.wait_ge(*after("sc_const", 144))

                    @block.vector
                    def _(dve):
                        dve.memset(S[:, :, :], 0.0).then_inc(*tick("sc_const0"))
                        dve.memset(arp[:, :, :, :, :, :], 0.0).then_inc(*tick("sc_const0"))
                        dve.memset(vside[:, :, :, :], 0.0).then_inc(*tick("sc_const0"))
                        dve.wait_ge(*after("sc_const0", 3))
                passed({"sc_const": 144, "sc_const0": 3})

                def half(e):
                    return slice(e * HEAD, (e + 1) * HEAD)

                score_bank = ((6, 7), (3, 5))

                def loop(eng, body, tail=None):
                    body(0, None, 0, 0, None, True)
                    with eng.Fori(0, (NG - 2) // 2) as i:
                        body(2 * i + 1, 2 * i, 1, i, i, False)
                        body(2 * i + 2, 2 * i + 1, 0, i + 1, i, False)
                    body(NG - 1, NG - 2, 1, NG // 2 - 1, NG // 2 - 1, False, last=True)
                    if tail is not None:
                        tail()

                with nc.Block() as block:
                    @block.sync
                    def _(sp):
                        def load(n, j):
                            sp.dma_start(ops[:, j, :, :, :].rearrange("p q j t -> p (q j t)"),
                                         QD[ds(n, 1), :, :, :, :].rearrange("a p q j t -> p (a q j t)")).then_inc(*tick(f"sc_in_{j}", 16))
                            for e in range(2):
                                for q in range(2):
                                    sp.dma_start(arp[half(e), j, q, e, :, :].rearrange("p z t -> p (z t)"),
                                                 QD[ds(n, 1), half(e), q, 0:2, :].rearrange("a p z t -> p (a z t)"))\
                                      .then_inc(*tick(f"sc_in_{j}", 16))
                            sp.dma_start(vv[:, j, :, :].rearrange("p q t -> p (q t)"),
                                         VG[ds(n, 1), :, :].rearrange("a p t -> p (a t)")).then_inc(*tick(f"sc_in_{j}", 16))

                        def out_y(n, j):
                            sp.wait_ge(*after("sc_y", n + 1))
                            sp.dma_start(Y_[ds(n, 1), :, :].rearrange("a p t -> p (a t)"), y[:, j, :])\
                              .then_inc(*tick(f"sc_y_out_{j}", 16))

                        load(0, 0)
                        load(1, 1)
                        with sp.Fori(0, (NG - 2) // 2) as i:
                            for j in range(2):
                                n = 2 * i + j
                                sp.wait_ge(*after("sc_Q", n + 1))
                                load(n + 2, j)
                                out_y(n, j)
                        for j in range(2):
                            out_y(NG - 2 + j, j)
                        for j in range(2):
                            sp.wait_ge(*after(f"sc_y_out_{j}", 8 * NG))

                    @block.tensor
                    def _(pe):
                        def chain_ready(n, c):
                            pe.wait_ge(*after("sc_S", 5 * n + c + 1))
                            if c == 0:
                                pe.wait_ge(*after("sc_F", n + 1))
                                pe.wait_ge(*after("sc_Q", n + 1))
                                pe.wait_ge(*after("sc_Yi", n + 1))
                                pe.wait_ge(*after("sc_y", n))

                        def chain(n, j, c):
                            for e in range(2):
                                mm = pe.matmul(bank[5][half(e), c * HEAD:(c + 1) * HEAD],
                                               MT[half(e), j, c, :], S[half(e), c, :], start=True, stop=True,
                                               tile_position=(e * HEAD, e * HEAD))
                            mm.then_inc(*tick("pe_state"))
                            for e in range(2):
                                mm = pe.matmul(bank[4][half(1 - e), c * HEAD:(c + 1) * HEAD], S[half(e), c, :],
                                               F[half(e), j, c * CHUNK:(c + 1) * CHUNK], start=True, stop=True,
                                               tile_position=(e * HEAD, (1 - e) * HEAD))
                            mm.then_inc(*tick("pe_y"))

                        def score(n, j, r, z):
                            pe.wait_ge(*after(f"sc_in_{j}", 96 * r + 96))
                            for q in range(2):
                                pe.matmul(bank[score_bank[z][q]], ops[:, j, q, 2 + z, :],
                                          arp[:, j, q, :, :, :].rearrange("p e z t -> p (e z t)"),
                                          start=True, stop=True).then_inc(*tick(f"pe_score_{z}"))

                        def body(n, b, j, r, rb, first, last=False):
                            G = G_[:, j, :, :, :]
                            pe.wait_ge(*after(f"sc_in_{j}", 96 * r + 96))
                            pe.wait_ge(*after("sc_akv", n))
                            pe.wait_ge(*after("sc_XTL", n))
                            for q in range(2):
                                for t, src in enumerate((ops[:, j, q, 0, :], ops[:, j, q, 2, :], ops[:, j, q, 3, :],
                                                         vv[:, j, q, :])):
                                    mm = pe.transpose(bank[q][:, t * P:(t + 1) * P], src, ident)
                            mm.then_inc(*tick("pe_tm"))
                            pe.wait_ge(*after("sc_Q", n))
                            if not first:
                                pe.wait_ge(*after("sc_y", b))
                            score(n, j, r, 1)
                            pe.wait_ge(*after("sc_X1", n + 1))
                            pe.wait_ge(*after("sc_tm", 2 * n + 2))
                            for u in range(4):
                                mm = pe.transpose(four[0][:, u, :], XT[:, u, :], ident)
                            mm.then_inc(*tick("pe_X"))
                            for li, s in enumerate(LEVELS):
                                pe.wait_ge(*after("sc_X", 5 * n + li + 1))
                                pe.wait_ge(*after("sc_NT", 5 * n + li + 1))
                                if li >= 1 and not first:
                                    chain_ready(b, li - 1)
                                for u in range(4):
                                    mm = pe.matmul(four[6][:, u, :], NT[:, li + 1, u, :], X[:, u, :], start=True, stop=True)
                                mm.then_inc(*tick("pe_W"))
                                if li == 0:
                                    pe.wait_ge(*after("sc_tm", 2 * n + 2))
                                    pe.wait_ge(*after("sc_G_1", 2 * n + 2))
                                    for q in range(2):
                                        for e in range(2):
                                            mm = pe.matmul(four[1][:, 2 * q + e, :], G[:, 2 * q + e, 2, :], tm[:, q, 2, :],
                                                           start=True, stop=True)
                                    mm.then_inc(*tick("pe_akv"))
                                elif not first:
                                    chain(b, 1 - j, li - 1)
                                pe.wait_ge(*after("sc_W", 5 * n + li + 1))
                                pe.wait_ge(*after("sc_XT", 4 * n + li))
                                if li < 4:
                                    for u in range(4):
                                        mm = pe.matmul(four[7][:, u, :], XT[:, u, :], Wt[:, u, :], start=True, stop=True)
                                    mm.then_inc(*tick("pe_Y"))

                                for u in range(4):
                                    mm = pe.matmul(four[0][:, u, :], Wt[:, u, :], XT[:, u, :], start=True, stop=True)
                                mm.then_inc(*tick("pe_YT"))
                            pe.wait_ge(*after("sc_XTL", n + 1))
                            pe.wait_ge(*after("sc_akv", n + 1))
                            for q in range(2):
                                for e in range(2):
                                    mm = pe.matmul(four[2][:, 2 * q + e, :], XT[:, 2 * q + e, :],
                                                   arhs[:, q, e, :, :].rearrange("p z f -> p (z f)"), start=True, stop=True)
                            mm.then_inc(*tick("pe_WZ"))
                            if not last:
                                pe.wait_ge(*after("sc_X", 5 * n + 5))
                                score(n + 1, 1 - j, r + j, 0)
                            pe.wait_ge(*after("sc_WZ", n + 1))
                            pe.wait_ge(*after("sc_pad", n + 1))
                            pe.wait_ge(*after("sc_y", n))
                            for q in range(2):
                                for e in range(2):
                                    pe.matmul(four[4][:, 2 * q + e, :], WZ[:, 2 * q + e, :, :].rearrange("p z f -> p (z f)"),
                                              G[:, 2 * q + e, 1, :], start=True, stop=False)
                                    mm = pe.matmul(four[4][:, 2 * q + e, :], vside[:, q, e, :], G[:, 2 * q + e, 3, :],
                                                   start=False, stop=True)
                            mm.then_inc(*tick("pe_Yi"))
                            pe.wait_ge(*after("sc_zpad", n + 1))
                            for q in range(2):
                                wide = bank[3 - q]
                                pe.matmul(wide[:, 0:256], Wq[:, q, :],
                                          bpad[:, q, :, :].rearrange("p c f -> p (c f)"), start=True, stop=True)
                                pe.matmul(wide[:, 256:512], tm[:, q, 0, :], zpad[:, q, :, :].rearrange("p c f -> p (c f)"),
                                          start=True, stop=False)
                                pe.matmul(wide[:, 256:512], tm[:, q, 1, :], vpad[:, q, :, :].rearrange("p c f -> p (c f)"),
                                          start=False, stop=True).then_inc(*tick("pe_Q"))

                        def tail():
                            for c in range(4):
                                chain_ready(NG - 1, c)
                                chain(NG - 1, 1, c)
                        score(0, 0, 0, 0)
                        loop(pe, body, tail)

                    @block.scalar
                    def _(act):
                        def body(n, b, j, r, rb, first, last=False):
                            act.wait_ge(*after("pe_tm", n + 1))
                            act.wait_ge(*after("pe_Yi", n))
                            for q in range(2):
                                act.activation(arhs[:, q, :, :, :].rearrange("p e z f -> p (e z) f")[:, 0:4:3, :],
                                               bank[q][:, 0:P].rearrange("p (e f) -> p e f", e=2), ACT.Copy)\
                                   .then_inc(*tick("sc_arhs"))
                                act.activation(tm[:, q, :, :], bank[q][:, P:4 * P].rearrange("p (z f) -> p z f", z=3),
                                               ACT.Copy).then_inc(*tick("sc_tm"))
                            act.wait_ge(*after("pe_X", n + 1))
                            act.activation(X[:, :, :], four[0], ACT.Copy).then_inc(*tick("sc_X"))
                            for li in range(5):
                                act.wait_ge(*after("pe_W", 5 * n + li + 1))
                                act.wait_ge(*after("pe_YT", 5 * n + li))
                                act.activation(Wt[:, :, :], four[6], ACT.Copy).then_inc(*tick("sc_W"))
                                if li == 0:
                                    act.wait_ge(*after("pe_akv", n + 1))
                                    for e in range(2):
                                        op = act.activation(arhs[:, :, e, 1 - e, :], four[1][:, e:4:2, half(e)], ACT.Copy)
                                    op.then_inc(*tick("sc_akv"))
                            act.wait_ge(*after("pe_WZ", n + 1))
                            act.activation(Wq[:, :, :].rearrange("p q (e f) -> p q e f", e=2),
                                           bank[2].rearrange("p (q z f) -> p q z f", q=2, z=4)[:, :, 0:4:3, :], ACT.Copy)
                            act.activation(WZ[:, :, :, :].rearrange("p u z f -> p (u z f)"), bank[2], ACT.Copy)\
                               .then_inc(*tick("sc_WZ"))
                            act.wait_ge(*after("sc_F", n + 1))
                            if not first:
                                act.wait_ge(*after("sc_y", b))
                            for e in range(2):
                                op = act.activation(Yi[half(1 - e), j, :].rearrange("p (q t) -> p q t", q=2),
                                                    four[4][half(1 - e), e:4:2, :], ACT.Copy)
                            op.then_inc(*tick("sc_Yi"))
                        loop(act, body)

                    @block.gpsimd
                    def _(pl):
                        def body(n, b, j, r, rb, first, last=False):
                            G = G_[:, j, :, :, :]
                            pl.wait_ge(*after("sc_G_0", 2 * n + 2))
                            for li in range(5):
                                if not first:
                                    pl.wait_ge(*after("pe_W", 5 * b + li + 1))
                                pl.tensor_tensor(NT[:, li + 1, :, :], G[:, :, 0, :],
                                                 levels[:, li + 1, :].unsqueeze(1).to_broadcast([P, 4, P]), ALU.mult)\
                                  .then_inc(*tick("sc_NT"))
                                if li == 1:
                                    pl.wait_ge(*after("sc_tm", 2 * n + 2))
                                    for pad, z in ((bpad, 0), (vpad, 2)):
                                        for q in range(2):
                                            op = pl.tensor_tensor(pad[:, q, :, :], tm[:, q, z, :].unsqueeze(1).to_broadcast([P, 2, P]),
                                                                  cmask[:, :].unsqueeze(2).to_broadcast([P, 2, P]), ALU.mult)
                                    for e in range(2):
                                        op = pl.tensor_copy(vside[:, :, e, half(1 - e)], tm[:, :, 2, half(e)])
                                    op.then_inc(*tick("sc_pad"))
                        loop(pl, body)

                    @block.vector
                    def _(dve):
                        def chain(n, j, r, c):
                            if c == 0:
                                dve.wait_ge(*after("sc_S", 5 * n))
                                dve.tensor_scalar(S[:, 0, :], S[:, 4, :], flags[:, ds(n, 1)], None, ALU.mult)\
                                   .then_inc(*tick("sc_S"))
                            dve.wait_ge(*after("pe_state", 4 * n + c + 1))
                            if c == 0:
                                dve.wait_ge(*after("pe_y", 4 * n))
                                dve.wait_ge(*after("sc_Q", n + 1))
                            dve.scalar_tensor_tensor(out=S[:, c + 1, :], in0=bank[5][:, c * HEAD:(c + 1) * HEAD],
                                                     scalar=pcs[:, ds(4 * n + c, 1)], in1=Q[:, j, c, :],
                                                     op0=ALU.mult, op1=ALU.add).then_inc(*tick("sc_S"))
                            if c == 3:
                                dve.wait_ge(*after("pe_y", 4 * n + 4))
                                dve.wait_ge(*after("sc_Yi", n + 1))
                                dve.wait_ge(*after("sc_S", 5 * n + 5))
                                dve.wait_ge(*after(f"sc_y_out_{j}", 16 * r))
                                dve.tensor_tensor(y[:, j, :], bank[4][:, 0:256], Yi[:, j, :], ALU.add)\
                                   .then_inc(*tick("sc_y"))

                        def masked(n, j, z):
                            for q in range(2):
                                dve.wait_ge(*after(f"pe_score_{z}", 2 * n + q + 1))
                                dve.tensor_tensor(G_[:, j, 2 * q:2 * q + 2, 2 * z:2 * z + 2, :],
                                                  bank[score_bank[z][q]].rearrange("p (e z t) -> p e z t", e=2, z=2),
                                                  masks[:, :, :].rearrange("p (e z) t -> p e z t", e=2), ALU.mult)\
                                   .then_inc(*tick(f"sc_G_{z}"))

                        def inverse_start(n, j):
                            masked(n, j, 0)
                            dve.wait_ge(*after("sc_G_0", 2 * n + 2))
                            dve.tensor_tensor(XT[:, :, :], G_[:, j, :, 0, :], levels[:, 0, :].unsqueeze(1).to_broadcast([P, 4, P]),
                                              ALU.mult).then_inc(*tick("sc_v"))
                            dve.wait_ge(*after("sc_v", n + 1))
                            dve.tensor_tensor(XT[:, :, :], XT[:, :, :], ident.unsqueeze(1).to_broadcast([P, 4, P]), ALU.add)\
                               .then_inc(*tick("sc_X1"))

                        def body(n, b, j, r, rb, first, last=False):
                            masked(n, j, 1)
                            for li in range(5):
                                if 1 <= li and not first:
                                    chain(b, 1 - j, rb, li - 1)
                                if li < 4:
                                    dve.wait_ge(*after("pe_Y", 4 * n + li + 1))
                                    dve.wait_ge(*after("sc_X", 5 * n + li + 1))
                                    dve.tensor_tensor(X[:, :, :], four[7], X[:, :, :], ALU.add).then_inc(*tick("sc_X"))
                                dve.wait_ge(*after("pe_YT", 5 * n + li + 1))
                                if li == 0:
                                    dve.wait_ge(*after("sc_X1", n + 1))
                                else:
                                    dve.wait_ge(*after("sc_XT", 4 * n + li))
                                dve.tensor_tensor(XT[:, :, :], four[0], XT[:, :, :], ALU.add)\
                                   .then_inc(*tick("sc_XT" if li < 4 else "sc_XTL"))

                            dve.wait_ge(*after("sc_WZ", n + 1))
                            for q in range(2):
                                op = dve.tensor_tensor(zpad[:, q, :, :],
                                                       WZ[:, 2 * q:2 * q + 2, :, :].rearrange("p u z f -> p (u z f)")[:, HEAD:3 * HEAD].unsqueeze(1).to_broadcast([P, 2, P]),
                                                       cmask[:, :].unsqueeze(2).to_broadcast([P, 2, P]), ALU.mult)
                            op.then_inc(*tick("sc_zpad"))
                            if not last:
                                inverse_start(n + 1, 1 - j)
                            dve.wait_ge(*after("pe_Yi", n + 1))
                            for e in range(2):
                                op = dve.tensor_tensor(F[half(e), j, :].rearrange("p (q t) -> p q t", q=2),
                                                       four[4][half(e), e:4:2, :], ops[half(e), j, :, 1, :], ALU.add)
                            op.then_inc(*tick("sc_F"))
                            for q in range(2):
                                dve.wait_ge(*after("pe_Q", 2 * n + q + 1))
                                wide = bank[3 - q].rearrange("p (z c f) -> p z c f", z=2, c=2)
                                for e in range(2):
                                    dve.tensor_tensor(MT[half(e), j, 2 * q:2 * q + 2, :], wide[half(e), 0, :, half(e)],
                                                      ident2[half(e), :].unsqueeze(1).to_broadcast([HEAD, 2, HEAD]), ALU.add)
                                    op = dve.tensor_tensor(Q[half(e), j, 2 * q:2 * q + 2, :], wide[half(e), 1, :, half(e)],
                                                           pcs[half(e), ds(4 * n + 2 * q, 2)].unsqueeze(2).to_broadcast([HEAD, 2, HEAD]),
                                                           ALU.mult)
                            op.then_inc(*tick("sc_Q"))

                        def tail():
                            for c in range(4):
                                chain(NG - 1, 1, NG // 2 - 1, c)
                        inverse_start(0, 0)
                        loop(dve, body, tail)
                passed({"sc_in_0": 48 * NG, "sc_in_1": 48 * NG, "pe_score_0": 2 * NG, "pe_score_1": 2 * NG, "sc_G_0": 2 * NG,
                        "sc_G_1": 2 * NG, "pe_Q": 2 * NG, "sc_zpad": NG, "sc_pad": NG, "sc_y_out_0": 8 * NG, "sc_y_out_1": 8 * NG, "sc_v": NG, "pe_W": 5 * NG,
                        "pe_YT": 5 * NG, "sc_W": 5 * NG, "sc_NT": 5 * NG, "sc_X": 5 * NG, "sc_XT": 4 * NG, "pe_Y": 4 * NG,
                        "sc_S": 5 * NG, "pe_state": 4 * NG, "pe_y": 4 * NG, "sc_tm": 2 * NG, "sc_arhs": 2 * NG})
                passed({n: NG for n in ("pe_tm", "pe_X", "sc_X1", "pe_akv", "sc_akv", "sc_XTL", "pe_WZ", "sc_WZ", "pe_Yi", "sc_Yi", "sc_Q", "sc_F", "sc_y")})

        @stage
        def rwkv_output(Y_, BN, G_, o):
            with ExitStack() as c:
                heads = const[:, 2, :]
                bn, g = (sb(f"ro_{n}", [P, DT, T], fp32, c) for n in ("bn", "g"))
                sq, rs = (sb(f"ro_{n}", [P, 2, T], fp32, c) for n in ("sq", "rs"))

                def at(t, m):
                    return t[:, ds(m, 1), :]

                def loop(eng, begin, finish):
                    begin(0, 0, 0)
                    with eng.Fori(0, DT // 2 - 1) as i:
                        begin(2 * i + 1, 1, i)
                        finish(2 * i, 0, i)
                        begin(2 * i + 2, 0, i + 1)
                        finish(2 * i + 1, 1, i)
                    begin(DT - 1, 1, DT // 2 - 1)
                    finish(DT - 2, 0, DT // 2 - 1)
                    finish(DT - 1, 1, DT // 2 - 1)

                with nc.Block() as block:
                    @block.sync
                    def _(sp):
                        for e in range(2):
                            sp.dma_start(o[e * HEAD:(e + 1) * HEAD, :, :].rearrange("p k (g t) -> p (k g) t", g=4),
                                         Y_[:, (1 - e) * HEAD:(2 - e) * HEAD, :].rearrange("n p t -> p n t"))\
                              .then_inc(*tick("ro_y_in", 16))
                        sp.dma_start(bn[:, :, :], BN.rearrange("k p t -> p k t")).then_inc(*tick("ro_bn_in", 16))
                        sp.dma_start(g[:, :, :], G_.rearrange("k p t -> p k t")).then_inc(*tick("ro_g_in", 16))

                    @block.tensor
                    def _(pe):
                        def begin(m, j, r):
                            pe.wait_ge(*after("ro_y_in", 32))
                            pe.wait_ge(*after("ro_yc", m))
                            for h in range(2):
                                mm = pe.matmul(ps[0][:, h, :], heads, o[:, ds(m, 1), h * HALF:(h + 1) * HALF], start=True, stop=True)
                            mm.then_inc(*tick("ro_sum"))

                        def finish(m, j, r):
                            pe.wait_ge(*after("ro_sq", m + 1))
                            pe.wait_ge(*after("ro_log", m))
                            for h in range(2):
                                mm = pe.matmul(ps[1][:, h, :], heads, sq[:, j, h * HALF:(h + 1) * HALF], start=True, stop=True)
                            mm.then_inc(*tick("ro_var"))
                        loop(pe, begin, finish)

                    @block.scalar
                    def _(act):
                        def begin(m, j, r):
                            act.wait_ge(*after("ro_yc", m + 1))
                            act.activation(sq[:, j:j + 1, :], at(o, m), ACT.Square).then_inc(*tick("ro_sq"))

                        def finish(m, j, r):
                            act.wait_ge(*after("ro_var", m + 1))
                            act.wait_ge(*after(f"ro_o_{j}", r))
                            act.activation(rs[:, j, :], flat[1], ACT.Ln, scale=1.0 / HEAD, bias=eps[:, 1:2]).then_inc(*tick("ro_log"))
                            act.wait_ge(*after("ro_log", m + 1))
                            act.activation(rs[:, j, :], rs[:, j, :], ACT.Exp, scale=-0.5).then_inc(*tick("ro_root"))
                        loop(act, begin, finish)

                    @block.vector
                    def _(dve):
                        def begin(m, j, r):
                            dve.wait_ge(*after("ro_sum", m + 1))
                            dve.scalar_tensor_tensor(out=at(o, m), in0=ps_tile(0), scalar=-1.0 / HEAD, in1=at(o, m),
                                                     op0=ALU.mult, op1=ALU.add).then_inc(*tick("ro_yc"))

                        def finish(m, j, r):
                            dve.wait_ge(*after("ro_root", m + 1))
                            dve.tensor_tensor(at(o, m), at(o, m), rs[:, j:j + 1, :], ALU.mult).then_inc(*tick("ro_v"))
                            dve.wait_ge(*after("ro_v", 3 * m + 1))
                            dve.tensor_scalar(at(o, m), at(o, m), pcol("rw_ln_w", m), pcol("rw_ln_b", m), ALU.mult, ALU.add)\
                               .then_inc(*tick("ro_v"))
                            dve.wait_ge(*after("ro_v", 3 * m + 2))
                            dve.wait_ge(*after("ro_bn_in", 16))
                            dve.tensor_tensor(at(o, m), at(o, m), at(bn, m), ALU.add).then_inc(*tick("ro_v"))
                            dve.wait_ge(*after("ro_v", 3 * m + 3))
                            dve.wait_ge(*after("ro_g_in", 16))
                            dve.tensor_tensor(at(o, m), at(o, m), at(g, m), ALU.mult)\
                               .then_inc(*tick(f"ro_o_{j}"))
                        loop(dve, begin, finish)
                passed({"ro_y_in": 32, "ro_bn_in": 16, "ro_g_in": 16, "ro_v": 3 * DT, "ro_o_0": DT // 2, "ro_o_1": DT // 2})
                passed({n: DT for n in ("ro_sum", "ro_yc", "ro_sq", "ro_var", "ro_log", "ro_root")})

        def final_norm():
            with ExitStack() as c:
                alone(Norm(H, "norm_final", sb("fin_room", [P, 5, T], fp32, c), keep=H))

        SQ = SSM_G // 2
        SU = SSM_G * SSM_H // P

        @stage
        def hybrid():
            rows = lambda t: (lambda m: t[ds(m, 1), :, :].rearrange("a p t -> p (a t)"))
            ZC, GC, GS, CC = (dram(f"hyd_{n}", [DT, P, T]) for n in ("zc", "gc", "gs", "cc"))
            U_, ZS = (dram(f"hyd_{n}", [SU, P, T]) for n in ("u", "zs"))
            w = A["hybrid_in"]
            with ExitStack() as c:
                xh = sb("hy_xh", [P, DT, T], r32, c)
                xl = sb("hy_xl", [P, DT, T], r32, c)
                stage = sb("hy_stage", [P, 2, T], fp32, c)
                LEAD = TAPS - 1
                cu = sb("hy_cu", [P, DT, LEAD + T], fp32, c)
                cc = sb("hy_cc", [P, DT, T], fp32, c)

                def scalar(act, s, i, last):
                    if s == 0:
                        act.wait_ge(ps_free[1].sem, ps_free[1].at(i))
                        act.activation(stage[:, 0, :], flat[0], ACT.Sigmoid).then_inc(ps_free[0].sem, 1)

                def vector(dve, s, i, last):
                    if s == 1:
                        dve.wait_ge(ps_free[0].sem, ps_free[0].at(i + 1))
                        dve.tensor_tensor(cu[:, ds(i, 1), LEAD:LEAD + T], ps_tile(1), stage[:, 0:1, :], ALU.mult)\
                           .then_inc(ps_free[1].sem, 1)
                        if last:
                            dve.memset(cu[:, :, 0:LEAD], 0.0).then_inc(*tick("cu_lead"))
                            dve.wait_ge(*after("cu_lead", 1))
                project(DT, [(w, lambda i: DT + i, DT, xh, xl), (w, lambda i: i, DT, xh, xl)], scalar, vector,
                        own=(("cu_lead", 1),), feed=Norm(H, "pre_norm2", cc[:, 0:5, :], xh, xl), fed=(0, 1))

                def conv(first):
                    def program(dve):
                        for j in range(TAPS):
                            for z in range(2):
                                k = first + z
                                n = 2 * j + z
                                if j == 0:
                                    op = dve.tensor_scalar(cc[:, k, :], cu[:, k, 0:T], pcol("conv_w2", k),
                                                           pcol("conv_b2", k), ALU.mult, ALU.add)
                                else:
                                    dve.wait_ge(*after("taps", n - 1))
                                    op = dve.scalar_tensor_tensor(out=cc[:, k, :], in0=cu[:, k, j:j + T],
                                                                  scalar=pcol("conv_w2", j * DT + k), in1=cc[:, k, :],
                                                                  op0=ALU.mult, op1=ALU.add)
                                op.then_inc(*tick("taps"))
                    return program

                def out_strips(dsts, funcs):
                    def scalar(act, s, i, last):
                        name = f"strip_out_{'AB'[s]}"
                        act.wait_ge(*after(name, 16 * i))
                        act.activation(stage[:, s, :], flat[s], funcs[s]).then_inc(ps_free[s].sem, 1)
                        act.wait_ge(ps_free[s].sem, ps_free[s].at(i + 1))
                        act.dma_start(dsts[s](i), stage[:, s, :]).then_inc(*tick(name, 16))
                        if last:
                            act.wait_ge(*after(name, 16 * (i + 1)))
                    return scalar
                own = (("strip_out_A", 64), ("strip_out_B", 64), ("taps", 2 * TAPS))

                def wide(t, at, func, first):
                    project(4, [(w, lambda i, s=s: at + 2 * i + s, DT, xh, xl) for s in range(2)],
                            out_strips([lambda i, s=s: rows(t)(2 * i + s) for s in range(2)], (func, func)),
                            own=own, vector_alone=conv(first))
                wide(ZC, 16, ACT.Silu, 0)
                project(4, [(w, lambda i: 24 + i, DT, xh, xl), (w, lambda i: 28 + i, DT, xh, xl)],
                        out_strips((rows(U_), rows(ZS)), (ACT.Copy, ACT.Silu)), own=own, vector_alone=conv(2))
                wide(GC, 32, ACT.Sigmoid, 4)
                wide(GS, 40, ACT.Sigmoid, 6)
                with nc.Block() as block:
                    @block.sync
                    def _(sp):
                        sp.dma_start(CC.rearrange("k p t -> p k t"), cc[:, :, :]).then_inc(*tick("cc_out", 16))
                        sp.wait_ge(*after("cc_out", 16))
                passed({"cc_out": 16})

            with ExitStack() as c:
                y = sb("ssm_y", [P, SU, T], fp32, c)
                ssm(U_, y)
                merged = sb("merged", [P, DT, T], fp32, c)
                ssm_out(y, ZS, GS, merged)
                conv_out(CC, ZC, GC, merged, y)
                c2 = ExitStack()
                xh = sb("wo_xh", [P, DT, T], r32, c2)
                xl = sb("wo_xl", [P, DT, T], r32, c2)
                def keep(act, s, i, last):
                    act.activation(merged[:, ds(2 * i + s, 1), :], ps_tile(s), ACT.Copy).then_inc(ps_free[s].sem, 1)
                project(DT // 2, [(A["w_out2"], lambda i, s=s: 2 * i + s, DT, xh, xl) for s in range(2)], keep,
                        feed=Split(merged, xh, xl, DT), fed=(0, 1))
                c2.close()
                alone(Norm(merged, "post_norm2", sb("post_room", [P, 5, T], fp32, c), keep=merged))
                with nc.Block() as block:
                    @block.vector
                    def _(dve):
                        for k in range(DT):
                            dve.tensor_tensor(H[:, k, :], H[:, k, :], merged[:, k, :], ALU.add).then_inc(*tick("last_add"))
                        dve.wait_ge(*after("last_add", DT))
                passed({"last_add": DT})

        @stage
        def gated_product(w, kt, xh, xl, G_, merged, add, room, feed):
            g, t = room[:, 0:2, :], room[:, 2:4, :]

            def scalar(act, s, i, last):
                if not last:
                    act.wait_ge(ps_free[s].sem, ps_free[s].at(i + 1))
                    act.dma_start(g[:, s, :], G_[ds(2 * i + 2 + s, 1), :, :].rearrange("a p t -> p (a t)"))\
                       .then_inc(*tick(f"gp_in_{'AB'[s]}", 16))

            def vector(dve, s, i, last):
                dve.wait_ge(*after(f"gp_in_{'AB'[s]}", 16 * (i + 1)))
                m = ds(2 * i + s, 1)
                if add:
                    dve.tensor_tensor(t[:, s, :], flat[s], g[:, s, :], ALU.mult).then_inc(ps_free[s].sem, 1)
                    dve.wait_ge(ps_free[s].sem, ps_free[s].at(i + 1))
                    dve.tensor_tensor(merged[:, m, :], t[:, s:s + 1, :], merged[:, m, :], ALU.add)\
                       .then_inc(*tick("gp_added"))
                else:
                    dve.tensor_tensor(merged[:, m, :], ps_tile(s), g[:, s:s + 1, :], ALU.mult)\
                       .then_inc(ps_free[s].sem, 1)

            def first_gates(act):
                for s in range(2):
                    act.dma_start(g[:, s, :], G_[s, :, :]).then_inc(*tick(f"gp_in_{'AB'[s]}", 16))
            project(DT // 2, [(w, lambda i, s=s: 2 * i + s, kt, xh, xl) for s in range(2)], scalar, vector,
                    scalar_first=first_gates, feed=feed, fed=(0, 1),
                    own=(("gp_added", 8 if add else 0), ("gp_in_A", 64), ("gp_in_B", 64)))

        @stage
        def ssm_out(y, ZS, GS, merged):
            with ExitStack() as c:
                xh = sb("glu_xh", [P, SU, T], r32, c)
                xl = sb("glu_xl", [P, SU, T], r32, c)
                zs = sb("glu_zs", [P, SU, T], fp32, c)
                gate = sb("glu_gate", [P, SU, T], fp32, c)
                def scalar(act, s, i, last):
                    m = 2 * i + s
                    act.activation(gate[:, ds(m, 1), :], ps_tile(s), ACT.Sigmoid, bias=pcol("b_glu2", m))\
                       .then_inc(ps_free[s].sem, 1)
                project(SU // 2, [(A["w_glu2"], lambda i, s=s: 2 * i + s, SU, xh, xl) for s in range(2)], scalar,
                        feed=Split(y, xh, xl, SU), fed=(0, 1))
                with nc.Block() as block:
                    @block.sync
                    def _(sp):
                        sp.dma_start(zs[:, :, :], ZS.rearrange("k p t -> p k t")).then_inc(*tick("zs_in", 16))

                    @block.vector
                    def _(dve):
                        for k in range(SU):
                            dve.tensor_tensor(y[:, k, :], y[:, k, :], gate[:, k, :], ALU.mult).then_inc(*tick("glu_y"))
                        dve.wait_ge(*after("zs_in", 16))
                        for k in range(SU):
                            dve.wait_ge(*after("glu_y", k + 1))
                            dve.tensor_tensor(y[:, k, :], y[:, k, :], zs[:, k, :], ALU.mult).then_inc(*tick("glu_z"))
                        dve.wait_ge(*after("glu_z", SU))
                passed({"zs_in": 16, "glu_y": SU, "glu_z": SU})
                gated_product(A["w_ssm_out2"], SU, xh, xl, GS, merged, False, gate, Split(y, xh, xl, SU))

        @stage
        def conv_out(CC, ZC, GC, merged, room):
            with ExitStack() as c:
                cc = sb("ln_cc", [P, DT, T], fp32, c)
                with ExitStack() as c2:
                    sq = sb("ln_sq", [P, 2, T], fp32, c2)
                    rs = sb("ln_rs", [P, T], fp32, c2)
                    zc = sb("ln_zc", [P, DT, T], fp32, c2)
                    with nc.Block() as block:
                        @block.sync
                        def _(sp):
                            sp.dma_start(cc[:, :, :], CC.rearrange("k p t -> p k t")).then_inc(*tick("ln_in", 16))
                            sp.dma_start(zc[:, :, :], ZC.rearrange("k p t -> p k t")).then_inc(*tick("ln_z_in", 16))

                        @block.tensor
                        def _(pe):
                            pe.wait_ge(*after("ln_in", 16))
                            for k in range(DT):
                                for h in range(2):
                                    mm = pe.matmul(ps[2][:, h, :], mean, cc[:, k, h * HALF:(h + 1) * HALF],
                                                   start=(k == 0), stop=(k == DT - 1))
                            mm.then_inc(*tick("ln_mean"))
                            for k in range(DT):
                                pe.wait_ge(*after("ln_sq", k + 1))
                                for h in range(2):
                                    mm = pe.matmul(ps[3][:, h, :], mean, sq[:, k % 2, h * HALF:(h + 1) * HALF],
                                                   start=(k == 0), stop=(k == DT - 1))
                                mm.then_inc(*tick("ln_var"))

                        @block.vector
                        def _(dve):
                            dve.wait_ge(*after("ln_in", 16))
                            dve.wait_ge(*after("ln_mean", 1))
                            for k in range(DT):
                                dve.tensor_tensor(cc[:, k, :], cc[:, k, :], flat[2], ALU.subtract).then_inc(*tick("ln_c"))
                            dve.wait_ge(*after("ln_root", 1))
                            dve.reciprocal(rs[:, :], rs[:, :]).then_inc(*tick("ln_inv"))
                            dve.wait_ge(*after("ln_inv", 1))
                            for k in range(DT):
                                dve.wait_ge(*after("ln_c", k + 1))
                                dve.scalar_tensor_tensor(out=cc[:, k, :], in0=cc[:, k, :], scalar=pcol("ln_g2", k),
                                                         in1=rs[:, :], op0=ALU.mult, op1=ALU.mult).then_inc(*tick("ln_n"))
                            dve.wait_ge(*after("ln_z_in", 16))
                            for k in range(DT):
                                dve.wait_ge(*after("ln_act", k + 1))
                                dve.tensor_tensor(cc[:, k, :], cc[:, k, :], zc[:, k, :], ALU.mult).then_inc(*tick("ln_y"))
                            dve.wait_ge(*after("ln_y", DT))

                        @block.scalar
                        def _(act):
                            for k in range(DT):
                                act.wait_ge(*after("ln_c", k + 1))
                                if k >= 2:
                                    act.wait_ge(*after("ln_var", k - 1))
                                act.activation(sq[:, k % 2, :], cc[:, k, :], ACT.Square).then_inc(*tick("ln_sq"))
                            act.wait_ge(*after("ln_var", DT))
                            act.activation(rs[:, :], flat[3], ACT.Sqrt, bias=eps[:, 2:3]).then_inc(*tick("ln_root"))
                            for k in range(DT):
                                act.wait_ge(*after("ln_n", k + 1))
                                act.activation(cc[:, k, :], cc[:, k, :], ACT.Silu, bias=pcol("ln_b2", k)).then_inc(*tick("ln_act"))
                    passed({n: DT for n in ("ln_c", "ln_n", "ln_y", "ln_sq", "ln_var", "ln_act")})
                    passed({"ln_in": 16, "ln_z_in": 16, "ln_mean": 1, "ln_root": 1, "ln_inv": 1})
                xh = sb("co_xh", [P, DT, T], r32, c)
                xl = sb("co_xl", [P, DT, T], r32, c)
                gated_product(A["w_conv_out2"], DT, xh, xl, GC, merged, True, room, Split(cc, xh, xl, DT))

        @stage
        def ssm(U_, y):
            HS = SC * SSM_H
            with ExitStack() as c:
                toep = sb("ssm_toep", [P, SSM_G, HS], fp32, c)
                bt = sb("ssm_bt", [P, 2, SQ, P], fp32, c)
                cz = sb("ssm_cz", [P, 2, SSM_G, (SC + 1) * SSM_H], fp32, c)
                rot = sb("ssm_rot", [P, 2, SQ, SN], fp32, c)
                decay8 = sb("ssm_decay8", [P, SQ], fp32, c)
                ssm_prepare(toep, bt, cz, rot, decay8, y)
                ut = sb("ssm_ut", [P, SSM_G, SN], fp32, c)
                with ExitStack() as c2:
                    u = sb("ssm_u", [P, SU, T], fp32, c2)
                    uc = sb("ssm_uc", [P, SSM_G, SC, SSM_H], fp32, c2)
                    with nc.Block() as block:
                        @block.sync
                        def _(sp):
                            sp.dma_start(u[:, :, :], U_.rearrange("k p t -> p k t")).then_inc(*tick("su_in", 16))

                        @block.tensor
                        def _(pe):
                            pe.wait_ge(*after("su_in", 16))
                            n = 0
                            for tt in range(SU):
                                for jh in range(2):
                                    if n >= 4:
                                        pe.wait_ge(*after("su_c", n - 3))
                                    for j in range(4):
                                        mm = pe.transpose(ps[n % 4][:, 0, j * P:(j + 1) * P], u[:, tt, 4 * jh + j:T:SC], ident)
                                    mm.then_inc(*tick("pe_uc"))
                                    n += 1
                            for g4 in range(SSM_G // 4):
                                pe.wait_ge(*after("su_c", 8))
                                if g4 >= 4:
                                    pe.wait_ge(*after("su_t", g4 - 3))
                                for g in range(4):
                                    mm = pe.transpose(ps[g4 % 4][:, 1, g * P:(g + 1) * P],
                                                      uc[:, 4 * g4 + g, :, :].rearrange("p j h -> p (j h)"), ident)
                                mm.then_inc(*tick("pe_ut"))

                        @block.vector
                        def _(dve):
                            n = 0
                            for tt in range(SU):
                                for jh in range(2):
                                    dve.wait_ge(*after("pe_uc", n + 1))
                                    dve.tensor_copy(uc[:, 8 * tt:8 * tt + 8, 4 * jh:4 * jh + 4, :].rearrange("p g j h -> p j g h"),
                                                    ps[n % 4][:, 0, :].rearrange("p (j g h) -> p j g h", j=4, g=8))\
                                       .then_inc(*tick("su_c"))
                                    n += 1
                            for g4 in range(SSM_G // 4):
                                dve.wait_ge(*after("pe_ut", g4 + 1))
                                dve.tensor_copy(ut[:, 4 * g4:4 * g4 + 4, :].rearrange("p g c -> p (g c)"), ps[g4 % 4][:, 1, :])\
                                   .then_inc(*tick("su_t"))
                            dve.wait_ge(*after("su_t", 8))
                    passed({"su_in": 16, "pe_uc": 8, "su_c": 8, "pe_ut": 8, "su_t": 8})

                with ExitStack() as c2:
                    b = sb("ssm_b", [P, 2, SQ, SN], fp32, c2)
                    d0, t1 = (y[:, 2 * z:2 * z + 2, :].rearrange("p k t -> p (k t)").rearrange("p (q c) -> p q c", q=SQ)
                              for z in range(2))
                    ee = sb("ssm_e", [P, 2, SQ * SN + 1], fp32, c2)
                    after_c, before_c = ([ee[:, z, o:o + SQ * SN].rearrange("p (q c) -> p q c", q=SQ) for z in range(2)]
                                         for o in (1, 0))
                    cos, sin = rot[:, 0, :, :], rot[:, 1, :, :]
                    with nc.Block() as block:
                        @block.tensor
                        def _(pe):
                            n = 0
                            for z in range(2):
                                for q4 in range(SQ // 4):
                                    if n >= 4:
                                        pe.wait_ge(*after("sb_b", n - 3))
                                    for q in range(4 * q4, 4 * q4 + 4):
                                        for g in range(2):
                                            mm = pe.matmul(ps[n % 4][g * 64:(g + 1) * 64, 0, (q % 4) * SN:(q % 4 + 1) * SN],
                                                           bt[:, z, q, g * 64:(g + 1) * 64], ut[:, 2 * q + g, :],
                                                           start=True, stop=True, tile_position=(0, g * 64))
                                    mm.then_inc(*tick("pe_b"))
                                    n += 1

                        @block.scalar
                        def _(act):
                            n = 0
                            for z in range(2):
                                for q4 in range(SQ // 4):
                                    act.wait_ge(*after("pe_b", n + 1))
                                    act.activation(b[:, z, 4 * q4:4 * q4 + 4, :].rearrange("p q c -> p (q c)"), ps[n % 4][:, 0, :],
                                                   ACT.Copy).then_inc(*tick("sb_b"))
                                    n += 1

                        @block.vector
                        def _(dve):
                            ch = Chain(dve, sig("dve_chain"))
                            ch(dve.tensor_copy(d0[:, :, :], decay8[:, :].unsqueeze(2).to_broadcast([P, SQ, SN])))
                            ch(dve.memset(d0[:, :, 0:1], 0.0))

                            dve.wait_ge(*after("sb_b", 8))
                            br, bi = b[:, 0, :, :], b[:, 1, :, :]
                            er, ei = after_c
                            flat3 = lambda t: t.rearrange("p q c -> p (q c)")
                            ch(dve.tensor_tensor(t1[:, :, :], bi, sin, ALU.mult))
                            ch(dve.tensor_tensor(er, br, cos, ALU.mult))
                            ch(dve.tensor_tensor(er, er, t1[:, :, :], ALU.add))
                            ch(dve.tensor_tensor(t1[:, :, :], br, sin, ALU.mult))
                            ch(dve.tensor_tensor(ei, bi, cos, ALU.mult))
                            ch(dve.tensor_tensor(bi, ei, t1[:, :, :], ALU.subtract))
                            ch(dve.tensor_copy(br, er))
                            ch(dve.tensor_tensor_scan(out=flat3(t1[:, :, :]), data0=flat3(d0[:, :, :]), data1=flat3(br),
                                                      initial=0.0, op0=ALU.mult, op1=ALU.add))
                            ch(dve.tensor_copy(br, t1[:, :, :]))
                            ch(dve.tensor_tensor_scan(out=flat3(t1[:, :, :]), data0=flat3(d0[:, :, :]), data1=flat3(bi),
                                                      initial=0.0, op0=ALU.mult, op1=ALU.add))
                            ch(dve.tensor_tensor(er, br, cos, ALU.mult))
                            ch(dve.tensor_tensor(bi, t1[:, :, :], sin, ALU.mult))
                            ch(dve.tensor_tensor(er, er, bi, ALU.subtract))
                            ch(dve.tensor_tensor(ei, br, sin, ALU.mult))
                            ch(dve.tensor_tensor(bi, t1[:, :, :], cos, ALU.mult))
                            ch(dve.tensor_tensor(ei, ei, bi, ALU.add))
                            for z in range(2):
                                ch(dve.memset(before_c[z][:, :, 0:1], 0.0))
                            chain_n.append(ch.n)
                    passed({"pe_b": 8, "sb_b": 8, "dve_chain": chain_n.pop()})

                    yc = b[:, :, :, :].rearrange("p z q c -> p (z q c)")\
                        .rearrange("p (i g h) -> p i g h", i=SC, g=SSM_G)
                    with nc.Block() as block:
                        @block.tensor
                        def _(pe):
                            for g4 in range(SSM_G // 4):
                                if g4 >= 4:
                                    pe.wait_ge(*after("sy_c", g4 - 3))
                                for g in range(4 * g4, 4 * g4 + 4):
                                    dst = ps[g4 % 4][:, 0, (g % 4) * P:(g % 4 + 1) * P]
                                    pe.matmul(dst, ut[:, g, :], toep[:, g, :], start=True, stop=False)
                                    pe.matmul(dst, before_c[0][:, g // 2, :], cz[:, 0, g, SSM_H:], start=False, stop=False)
                                    mm = pe.matmul(dst, before_c[1][:, g // 2, :], cz[:, 1, g, SSM_H:], start=False, stop=True)
                                mm.then_inc(*tick("pe_yc"))
                            for i in range(SC):
                                pe.wait_ge(*after("sy_c", 8))
                                if i >= 4:
                                    pe.wait_ge(*after("sy_t", i - 3))
                                for tt in range(SU):
                                    mm = pe.transpose(ps[i % 4][:, 1, tt * P:(tt + 1) * P],
                                                      yc[:, i, 8 * tt:8 * tt + 8, :].rearrange("p g h -> p (g h)"), ident)
                                mm.then_inc(*tick("pe_yt"))

                        @block.vector
                        def _(dve):
                            for g4 in range(SSM_G // 4):
                                dve.wait_ge(*after("pe_yc", g4 + 1))
                                dve.tensor_copy(yc[:, :, 4 * g4:4 * g4 + 4, :].rearrange("p i g h -> p g i h"),
                                                ps[g4 % 4][:, 0, :].rearrange("p (g i h) -> p g i h", g=4, i=SC))\
                                   .then_inc(*tick("sy_c"))

                        @block.scalar
                        def _(act):
                            for i in range(SC):
                                act.wait_ge(*after("pe_yt", i + 1))
                                act.activation(y[:, :, i:T:SC], ps[i % 4][:, 1, :].rearrange("p (k c) -> p k c", k=SU),
                                               ACT.Gelu_apprx_tanh).then_inc(*tick("sy_t"))
                    passed({"pe_yc": 8, "sy_c": 8, "pe_yt": 8, "sy_t": 8})

        @stage
        def ssm_prepare(toep, bt, cz, rot, decay8, room):
            with ExitStack() as c:
                lam = sb("sp_lam", [P, 3, SQ], fp32, c)
                bc = sb("sp_bc", [P, 4, SQ, SSM_H], fp32, c)
                dd = sb("sp_d", [SSM_H, SSM_G], fp32, c)
                v = {n: sb(f"sp_{n}", [P, SQ], fp32, c) for n in
                     ("dt", "mag", "th", "n", "s", "s2", "cs", "sn", "zr", "zi", "den", "t", "t2", "pr", "pi")}
                pw = sb("sp_pw", [P, 2, SC + 1, SQ], fp32, c)
                bb = sb("sp_bb", [P, 2, SQ, SSM_H], fp32, c)
                w1 = sb("sp_w1", [P, SQ, SSM_H], fp32, c)
                w2 = sb("sp_w2", [P, SQ, SSM_H], fp32, c)
                p1 = sb("sp_p1", [P, SQ, SSM_H], fp32, c)
                p2 = sb("sp_p2", [P, SQ, SSM_H], fp32, c)
                va = sb("sp_va", [P, 2, SQ, SC, SSM_H], fp32, c)
                gd = room[0:SSM_H, :, :].rearrange("p k t -> p (k t)").rearrange("p (g n) -> p g n", g=SSM_G)
                dg = sb("sp_dg", [SSM_H, SSM_G, SSM_H], fp32, c)
                r1 = sb("sp_r1", [P, SQ, SN // 2], fp32, c)
                ch_n = {}
                INV2PI = float(np.float32(1 / (2 * np.pi)))
                C1 = 6.28125
                C2 = float(np.float32(2 * np.pi - C1) - np.float32(2 * np.pi - C1) % np.float32(2.0 ** -20))
                C3 = float(2 * np.pi - C1 - C2)
                ROUND = float(3 << 22)
                PI = 3.1415925

                def wideh(t):
                    return t.unsqueeze(2).to_broadcast([P, SQ, SSM_H])
                with nc.Block() as block:
                    @block.sync
                    def _(sp):
                        sp.dma_start(lam[:, :, :], A["ssm_lam"]).then_inc(*tick("sp_in", 16))
                        sp.dma_start(bc[:, :, :, :], A["ssm_bc"]).then_inc(*tick("sp_in", 16))
                        sp.dma_start(dd[:, :], A["ssm_d"]).then_inc(*tick("sp_in", 16))
                        sp.wait_ge(*after("sp_gd", 10))
                        sp.wait_ge(*after("sp_zero", 1))
                        for j in range(SC):
                            sp.dma_start(toep[j * SSM_H:(j + 1) * SSM_H, :, j * SSM_H:P],
                                         gd[:, :, 0:P - j * SSM_H]).then_inc(*tick("sp_toep", 16))
                        sp.wait_ge(*after("sp_toep", 16 * SC))

                    @block.scalar
                    def _(act):
                        act.wait_ge(*after("sp_in", 48))
                        act.activation(v["dt"][:, :], lam[:, 2, :], ACT.Exp).then_inc(*tick("sp_dt"))
                        act.wait_ge(*after("sp_lrdt", 1))
                        act.activation(v["mag"][:, :], v["t"][:, :], ACT.Exp).then_inc(*tick("sp_mag"))
                        act.wait_ge(*after("sp_angle", 1))
                        act.activation(v["sn"][:, :], v["th"][:, :], ACT.Sin).then_inc(*tick("sp_sin"))
                        act.activation(v["s2"][:, :], v["th"][:, :], ACT.Sin, scale=0.5).then_inc(*tick("sp_sin"))
                        for z in range(2):
                            for q4 in range(SQ // 4):
                                n = 4 * z + q4
                                act.wait_ge(*after("pe_bt", n + 1))
                                act.activation(bt[:, z, 4 * q4:4 * q4 + 4, :].rearrange("p q c -> p (q c)"), ps[n % 4][:, 0, :],
                                               ACT.Copy).then_inc(*tick("sp_bt"))

                    @block.tensor
                    def _(pe):
                        pe.wait_ge(*after("sp_va", 1))
                        for z in range(2):
                            for q4 in range(SQ // 4):
                                n = 4 * z + q4
                                if n >= 4:
                                    pe.wait_ge(*after("sp_bt", n - 3))
                                for q in range(4):
                                    mm = pe.transpose(ps[n % 4][:, 0, q * P:(q + 1) * P],
                                                      va[:, z, 4 * q4 + q, :, :].rearrange("p j h -> p (j h)"), ident)
                                mm.then_inc(*tick("pe_bt"))
                        pe.wait_ge(*after("sp_cz", 2))
                        for g4 in range(SSM_G // 4):
                            if g4 >= 4:
                                pe.wait_ge(*after("sp_gd", g4 - 3))
                            for g in range(4 * g4, 4 * g4 + 4):
                                dst = ps[g4 % 4][0:SSM_H, 1, (g % 4) * P:(g % 4 + 1) * P]
                                pe.matmul(dst, bb[:, 0, g // 2, :], cz[:, 0, g, 0:P], start=True, stop=False)
                                mm = pe.matmul(dst, bb[:, 1, g // 2, :], cz[:, 1, g, 0:P], start=False, stop=True)
                            mm.then_inc(*tick("pe_gd"))

                    @block.gpsimd
                    def _(pl):
                        ch = Chain(pl, sig("pool_chain"))
                        ch(pl.memset(toep[:, :, :], 0.0))
                        pl.memset(cz[:, :, :, :], 0.0).then_inc(*tick("sp_zero"))
                        pl.wait_ge(*after("sp_zero", 1))
                        pl.wait_ge(*after("sp_pw", 1))
                        cr, ci = bc[:, 2, :, :], bc[:, 3, :, :]
                        for k in range(SC + 1):
                            pr, pi = wideh(pw[:, 0, k, :]), wideh(pw[:, 1, k, :])
                            for z, (a, b, op) in enumerate(((cr, ci, ALU.subtract), (ci, cr, ALU.add))):
                                ch(pl.tensor_tensor(p1[:, :, :], a, pr, ALU.mult))
                                ch(pl.tensor_tensor(p2[:, :, :], b, pi, ALU.mult))
                                if z == 1:
                                    ch(pl.tensor_tensor(p1[:, :, :], p1[:, :, :], p2[:, :, :], ALU.add))
                                    ch(pl.tensor_scalar(p1[:, :, :], p1[:, :, :], -1.0, None, ALU.mult))
                                for g in range(2):
                                    rows = slice(64 * g, 64 * g + 64)
                                    dst = cz[rows, z, g:SSM_G:2, k * SSM_H:(k + 1) * SSM_H]
                                    if z == 0:
                                        ch(pl.tensor_tensor(dst, p1[rows, :, :], p2[rows, :, :], ALU.subtract))
                                    else:
                                        ch(pl.tensor_copy(dst, p1[rows, :, :]))
                        pl.engine_nop().then_inc(*tick("sp_cz", 1))
                        pl.engine_nop().then_inc(*tick("sp_cz", 1))
                        ch_n["pool"] = ch.n

                    @block.vector
                    def _(dve):
                        ch = Chain(dve, sig("dve_chain"))
                        V = {n: t[:, :] for n, t in v.items()}
                        lr, li = lam[:, 0, :], lam[:, 1, :]

                        def mul(o, a, b):
                            ch(dve.tensor_tensor(o, a, b, ALU.mult))

                        def add(o, a, b):
                            ch(dve.tensor_tensor(o, a, b, ALU.add))

                        def sub(o, a, b):
                            ch(dve.tensor_tensor(o, a, b, ALU.subtract))

                        def cmul(orr, oi, ar, ai, br, bi, t1, t2):
                            mul(t1, ai, bi)
                            mul(orr, ar, br)
                            sub(orr, orr, t1)
                            mul(t2, ai, br)
                            mul(oi, ar, bi)
                            add(oi, oi, t2)

                        dve.wait_ge(*after("sp_in", 48))
                        dve.wait_ge(*after("sp_dt", 1))
                        dve.tensor_tensor(V["t"], lr, V["dt"], ALU.mult).then_inc(*tick("sp_lrdt"))
                        mul(V["th"], li, V["dt"])
                        ch(dve.tensor_scalar(V["n"], V["th"], INV2PI, ROUND, ALU.mult, ALU.add))
                        ch(dve.tensor_scalar(V["n"], V["n"], -ROUND, None, ALU.add))
                        for part in (C1, C2, C3):
                            ch(dve.scalar_tensor_tensor(out=V["th"], in0=V["n"], scalar=-part, in1=V["th"],
                                                        op0=ALU.mult, op1=ALU.add))
                        dve.tensor_scalar(V["th"], V["th"], PI, -PI, ALU.min, ALU.max).then_inc(*tick("sp_angle"))
                        mul(V["den"], lr, lr)
                        mul(V["t2"], li, li)
                        add(V["den"], V["den"], V["t2"])
                        ch(dve.reciprocal(V["den"], V["den"]))
                        dve.wait_ge(*after("sp_sin", 2))
                        dve.wait_ge(*after("sp_mag", 1))
                        mul(V["cs"], V["s2"], V["s2"])
                        ch(dve.tensor_scalar(V["cs"], V["cs"], -2.0, 1.0, ALU.mult, ALU.add))
                        ch(dve.memset(pw[:, 0, 0, :], 1.0))
                        ch(dve.memset(pw[:, 1, 0, :], 0.0))
                        mul(pw[:, 0, 1, :], V["mag"], V["cs"])
                        mul(pw[:, 1, 1, :], V["mag"], V["sn"])
                        for k in range(2, SC + 1):
                            h = k // 2
                            cmul(pw[:, 0, k, :], pw[:, 1, k, :], pw[:, 0, h, :], pw[:, 1, h, :],
                                 pw[:, 0, k - h, :], pw[:, 1, k - h, :], V["t"], V["t2"])
                        ch(dve.engine_nop())
                        dve.engine_nop().then_inc(*tick("sp_pw"))
                        ch(dve.tensor_scalar(V["n"], pw[:, 0, 1, :], -1.0, None, ALU.add))
                        mul(V["zr"], V["n"], lr)
                        mul(V["t"], pw[:, 1, 1, :], li)
                        add(V["zr"], V["zr"], V["t"])
                        mul(V["zr"], V["zr"], V["den"])
                        mul(V["zi"], pw[:, 1, 1, :], lr)
                        mul(V["t"], V["n"], li)
                        sub(V["zi"], V["zi"], V["t"])
                        mul(V["zi"], V["zi"], V["den"])
                        cmul(bb[:, 0, :, :], bb[:, 1, :, :], wideh(V["zr"]), wideh(V["zi"]), bc[:, 0, :, :], bc[:, 1, :, :],
                             w1[:, :, :], w2[:, :, :])
                        for j in range(SC):
                            k = SC - 1 - j
                            cmul(va[:, 0, :, j, :], va[:, 1, :, j, :], wideh(pw[:, 0, k, :]), wideh(pw[:, 1, k, :]),
                                 bb[:, 0, :, :], bb[:, 1, :, :], w1[:, :, :], w2[:, :, :])
                        dve.engine_nop().then_inc(*tick("sp_va"))
                        mul(V["t"], V["mag"], V["mag"])
                        mul(V["t2"], V["t"], V["t"])
                        ch(dve.tensor_tensor(decay8[:, :], V["t2"], V["t2"], ALU.mult))
                        ch(dve.memset(rot[:, 0, :, 0:1], 1.0))
                        ch(dve.memset(rot[:, 1, :, 0:1], 0.0))
                        cur, nxt = (V["cs"], V["sn"]), (V["pr"], V["pi"])
                        for step in range(3 + 7):
                            if step >= 3:
                                m = 1 << (step - 3)
                                wd = lambda t: t.unsqueeze(2).to_broadcast([P, SQ, m])
                                r = r1[:, :, 0:m]
                                a_r, a_i = rot[:, 0, :, 0:m], rot[:, 1, :, 0:m]
                                o_r, o_i = rot[:, 0, :, m:2 * m], rot[:, 1, :, m:2 * m]
                                mul(r, a_i, wd(cur[1]))
                                mul(o_r, a_r, wd(cur[0]))
                                sub(o_r, o_r, r)
                                mul(r, a_i, wd(cur[0]))
                                mul(o_i, a_r, wd(cur[1]))
                                add(o_i, o_i, r)
                            cmul(nxt[0], nxt[1], cur[0], cur[1], cur[0], cur[1], V["t"], V["t2"])
                            cur, nxt = nxt, cur
                        for g4 in range(SSM_G // 4):
                            dve.wait_ge(*after("pe_gd", g4 + 1))
                            dve.tensor_copy(gd[:, 4 * g4:4 * g4 + 4, :].rearrange("p g n -> p (g n)"), ps[g4 % 4][0:SSM_H, 1, :])\
                               .then_inc(*tick("sp_gd"))
                        dve.tensor_tensor(dg[:, :, :], const[0:SSM_H, 0, 0:SSM_H].unsqueeze(1).to_broadcast([SSM_H, SSM_G, SSM_H]),
                                          dd[:, :].unsqueeze(2).to_broadcast([SSM_H, SSM_G, SSM_H]), ALU.mult)\
                           .then_inc(*tick("sp_gd"))
                        dve.wait_ge(*after("sp_gd", 9))
                        dve.tensor_tensor(gd[:, :, 0:SSM_H], gd[:, :, 0:SSM_H], dg[:, :, :], ALU.add).then_inc(*tick("sp_gd"))
                        ch_n["dve"] = ch.n
                passed({"sp_in": 48, "sp_dt": 1, "sp_lrdt": 1, "sp_mag": 1, "sp_angle": 1, "sp_sin": 2, "pe_bt": 8, "sp_bt": 8,
                        "sp_va": 1, "sp_cz": 2, "sp_gd": 10, "pe_gd": 8, "sp_zero": 1, "sp_pw": 1, "sp_toep": 16 * SC,
                        "dve_chain": ch_n["dve"], "pool_chain": ch_n["pool"]})

        chain_n = []
        stages = [("hawk", hawk), ("ffn0", lambda: ffn(0)), ("ple0", lambda: ple(0)), ("rwkv", rwkv),
                  ("ffn1", lambda: ffn(1)), ("ple1", lambda: ple(1)), ("final", final_norm), ("out", hybrid)]
        running = start is None
        for name, run in stages:
            if running:
                run()
            if name == stop:
                break
            running = running or name == start

        stored = sig("stored")
        with nc.Block() as block:
            @block.sync
            def _(sp):
                sp.dma_start(out, H[:, :, :]).then_inc(stored.sem, 16)
                sp.wait_ge(stored.sem, stored.at(16))

def strips(w):
    k, m = w.shape
    return np.ascontiguousarray(w.reshape(k // P, P, m // P, P).transpose(2, 1, 0, 3)).reshape(m // P, P, k)

def padded(w, rows, cols):
    out = np.zeros((rows, cols), w.dtype)
    out[:w.shape[0], :w.shape[1]] = w
    return out

def square_constants():
    c = np.zeros((len(CONSTS), P, P), np.float32)
    i, j = np.meshgrid(np.arange(P), np.arange(P), indexing="ij")
    same = i // CHUNK == j // CHUNK
    c[CIX["ident"]] = i == j
    c[CIX["mean"]] = 1.0 / D
    c[CIX["heads"]] = i // HEAD == j // HEAD
    c[CIX["mask_a"]] = same & (i < j)
    c[CIX["mask_r"]] = same & (i <= j)
    for s in (1, 2, 4, 8, 16, 32):
        c[CIX[f"level{s}"]] = (i // (2 * s) == j // (2 * s)) & (i % (2 * s) < s) & (j % (2 * s) >= s)
    return np.ascontiguousarray(c.transpose(1, 0, 2))

def laid_out(v):
    a = {}
    a["xT"] = np.ascontiguousarray(v["x"][0].T.reshape(DT, P, T).transpose(1, 0, 2))
    a["pT"] = np.ascontiguousarray(v["p"][:, 0].transpose(0, 2, 1).reshape(2, PLE_T, P, T).transpose(0, 2, 1, 3))
    cols = [v["norm_mix"][0], v["norm_mix"][1], v["norm_ffn"][0], v["norm_ffn"][1], v["norm_ple"][0],
            v["norm_ple"][1], v["norm_final"], v["lru_b_in"], v["lru_conv_w"], v["lru_conv_b"],
            v["lru_b_gate_a"], v["lru_b_gate_x"], v["lru_lambda"], v["lru_b_out"],
            v["rw_mu"], v["rw_w0"], v["rw_a0"], v["rw_k_k"], v["rw_k_a"], v["rw_r_k"], v["rw_ln_w"], v["rw_ln_b"],
            v["pre_norm_gain_2"], v["conv_w_2"], v["conv_b_2"], v["conv_ln_gain_2"], v["conv_ln_bias_2"],
            v["b_ssm_glu_2"], v["post_norm_gain_2"], v["ssm_d_2"]]
    a["params"] = np.ascontiguousarray(np.concatenate([c.reshape(-1, P) for c in cols]).T)
    a["consts"] = square_constants()
    a["scan_ident"] = np.tile(np.eye(HEAD, dtype=np.float32), (2, 1))
    a["scan_chunks"] = np.repeat(np.eye(2, dtype=np.float32), CHUNK, axis=0)
    a["scan_flags"] = np.tile((np.arange(4 * DT) % 4 != 0).astype(np.float32), (P, 1))
    a["rkv"] = np.concatenate([strips(v["rw_w_rkv"][0][n]) for n in range(3)])
    a["rw_o"] = strips(v["rw_w_o"][0])
    for n, cols in (("w", P), ("a", P), ("g", 2 * P)):
        a[f"rw_{n}1"] = strips(padded(v[f"rw_{n}1"][0], D, cols))
        a[f"rw_{n}2"] = strips(padded(v[f"rw_{n}2"][0], cols, D))
    a["hybrid_in"] = strips(v["w_in_2"][0])
    a["w_conv_out2"] = strips(v["w_conv_out_2"][0])
    a["w_glu2"] = strips(v["w_ssm_glu_2"][0])
    a["w_ssm_out2"] = strips(v["w_ssm_out_2"][0])
    a["w_out2"] = strips(v["w_out_2"][0])
    dt = np.repeat(v["ssm_log_dt_2"][0][:, None], SSM_P, 1)
    a["ssm_lam"] = np.stack([t.reshape(SSM_G // 2, P).T for t in (v["ssm_lambda_re_2"][0], v["ssm_lambda_im_2"][0], dt)], 1)
    a["ssm_bc"] = np.stack([t.reshape(SSM_G // 2, P, SSM_H).transpose(1, 0, 2) for t in
                            (v["ssm_b_re_2"][0], v["ssm_b_im_2"][0], v["ssm_c_re_2"][0].transpose(0, 2, 1),
                             v["ssm_c_im_2"][0].transpose(0, 2, 1))], 1)
    a["ssm_d"] = v["ssm_d_2"][0].T
    a["hawk_in"] = strips(v["lru_w_in"][0])
    a["gate_a"] = v["lru_w_gate_a"][0]
    a["gate_x"] = v["lru_w_gate_x"][0]
    a["hawk_out"] = strips(v["lru_w_out"][0])
    for l in range(2):
        a[f"ffn_in{l}"] = strips(v["ffn_w_in"][l])
        a[f"ffn_out{l}"] = strips(v["ffn_w_out"][l])
        a[f"ple_proj{l}"] = strips(v["ple_w_proj"][l])
        a[f"ple_gate{l}"] = strips(v["ple_w_gate"][l])
    return a

def kernel(**inputs):
    import concourse.bacc as bacc
    from concourse.bass_utils import run_bass_kernel_spmd

    nc = bacc.Bacc("TRN2", target_bir_lowering=False, num_devices=1)
    arrays, aps = {}, {}
    for name, a in laid_out(inputs).items():
        arrays[f"{name}_dram"] = np.ascontiguousarray(a)
        aps[name] = nc.dram_tensor(f"{name}_dram", a.shape, mybir.dt.from_np(a.dtype), kind="ExternalInput").ap()
    out = nc.dram_tensor("out_dram", (P, DT, T), mybir.dt.float32, kind="ExternalOutput").ap()
    build(nc, aps, out)
    got = run_bass_kernel_spmd(nc, [arrays], core_ids=[0]).results[0]["out_dram"]
    return np.ascontiguousarray(got.transpose(1, 0, 2).reshape(D, T).T).reshape(1, T, D)
```
